# Optimizing a Trainium2 kernel written in Bass

```python
import jax, jax.numpy as jnp
from jax import lax
import numpy as np
import math

D_MODEL = 1024
BATCH = 1
SEQ = 256
DEPTH = 1

CHUNK = 64
Q_BLOCK = 128
MIX_WIDTH = D_MODEL
POOL_WIDTH = MIX_WIDTH // 2
POOL_WINDOWS = (2, 4, 8, 16)
POOL_GROUPS = len(POOL_WINDOWS)
POOL_GROUP_DIM = POOL_WIDTH // POOL_GROUPS
ATTN_WIDTH = MIX_WIDTH - POOL_WIDTH
DIFF_HEAD_DIM = 64
V_HEAD_DIM = 2 * DIFF_HEAD_DIM
N_DIFF_HEADS = ATTN_WIDTH // V_HEAD_DIM
IN_WIDTH = POOL_WIDTH + 3 * ATTN_WIDTH
D_FF = 2816
CONV_WIDTH = 3
ROPE_THETA = 10000.0
EPS = 1e-6


def rmsnorm(x, g):
    xf = x.astype(jnp.float32)
    y = xf * lax.rsqrt(jnp.mean(xf * xf, axis=-1, keepdims=True) + EPS)
    return (y * g.astype(jnp.float32)).astype(x.dtype)

def rope_tables(positions, dtype):
    inv_freq = ROPE_THETA ** (-jnp.arange(0, DIFF_HEAD_DIM, 2, dtype=jnp.float32) / DIFF_HEAD_DIM)
    ang = positions.astype(jnp.float32)[..., None] * inv_freq
    return (jnp.cos(ang)[:, :, None, None, :].astype(dtype),
            jnp.sin(ang)[:, :, None, None, :].astype(dtype))

def apply_rope(t, cos, sin):
    t1, t2 = jnp.split(t, 2, axis=-1)
    return jnp.concatenate([t1 * cos - t2 * sin, t1 * sin + t2 * cos], axis=-1)

def multiscale_pool(p, pool_w, pool_scale):
    s = p.shape[1]
    pf = p.astype(jnp.float32)
    csum = jnp.pad(jnp.cumsum(pf, axis=1), ((0, 0), (1, 0), (0, 0)))
    t = jnp.arange(s)
    pooled = []
    for g, w in enumerate(POOL_WINDOWS):
        cs = csum[..., g * POOL_GROUP_DIM:(g + 1) * POOL_GROUP_DIM]
        upper = cs[:, 1:]
        lower = jnp.pad(cs[:, :s + 1 - w], ((0, 0), (w - 1, 0), (0, 0)))
        count = jnp.minimum(t + 1, w).astype(jnp.float32)[None, :, None]
        pooled.append((upper - lower) / count)
    d = (jnp.concatenate(pooled, axis=-1) - pf).astype(p.dtype)
    d = d.reshape(p.shape[0], s, POOL_GROUPS, POOL_GROUP_DIM)
    y = jnp.einsum('bsgc,gcd->bsgd', d, pool_w).reshape(p.shape[0], s, POOL_WIDTH)
    return y * pool_scale

def diff_attention(q, k, v, lam, lam_init, head_g):
    b, h, _, s, _ = q.shape
    scale = DIFF_HEAD_DIM ** -0.5
    outs = []
    for i in range(s // Q_BLOCK):
        q0 = i * Q_BLOCK
        end = q0 + Q_BLOCK
        qb = q[:, :, :, q0:end]
        kb = k[:, :, :, :end]
        vb = v[:, :, :end]
        scores = jnp.einsum('bhnqd,bhnkd->bhnqk', qb, kb).astype(jnp.float32) * scale
        q_chunk = (q0 + jnp.arange(Q_BLOCK)) // CHUNK
        k_chunk = jnp.arange(end) // CHUNK
        mask = k_chunk[None, :] <= q_chunk[:, None]
        probs = jax.nn.softmax(jnp.where(mask, scores, -jnp.inf), axis=-1)
        attn = probs[:, :, 0] - lam * probs[:, :, 1]
        outs.append(jnp.einsum('bhqk,bhkd->bhqd', attn.astype(v.dtype), vb))
    o = jnp.concatenate(outs, axis=2)
    o = rmsnorm(o, head_g[None, :, None, :]) * (1.0 - lam_init)
    return o.transpose(0, 2, 1, 3).reshape(b, s, ATTN_WIDTH)

def causal_dwconv(u, w, bias):
    s = u.shape[1]
    upad = jnp.pad(u, ((0, 0), (CONV_WIDTH - 1, 0), (0, 0)))
    out = bias
    for j in range(CONV_WIDTH):
        out = out + w[j] * upad[:, j:j + s]
    return out

def first_inputs(seed: int = 0) -> dict:
    key = jax.random.key(seed)
    ks = jax.random.split(key, 20)
    nrm = lambda k, shape, s: jax.random.normal(k, shape, jnp.float32) * s
    x = jax.random.normal(ks[0], (BATCH, SEQ, D_MODEL), jnp.float32)
    offset = jax.random.randint(ks[1], (BATCH,), 0, 10000, dtype=jnp.int32)
    positions = offset[:, None] + jnp.arange(SEQ, dtype=jnp.int32)[None, :]
    return {
        "x": x,
        "positions": positions,
        "norm_mix_g": 1.0 + nrm(ks[2], (DEPTH, D_MODEL), 0.05),
        "w_in": nrm(ks[3], (DEPTH, D_MODEL, IN_WIDTH), D_MODEL ** -0.5),
        "pool_w": nrm(ks[4], (DEPTH, POOL_GROUPS, POOL_GROUP_DIM, POOL_GROUP_DIM), POOL_GROUP_DIM ** -0.5),
        "pool_scale": 1.0 + nrm(ks[5], (DEPTH, POOL_WIDTH), 0.05),
        "lambda_q1": nrm(ks[6], (DEPTH, DIFF_HEAD_DIM), 0.1),
        "lambda_k1": nrm(ks[7], (DEPTH, DIFF_HEAD_DIM), 0.1),
        "lambda_q2": nrm(ks[8], (DEPTH, DIFF_HEAD_DIM), 0.1),
        "lambda_k2": nrm(ks[9], (DEPTH, DIFF_HEAD_DIM), 0.1),
        "attn_norm_g": 1.0 + nrm(ks[10], (DEPTH, N_DIFF_HEADS, V_HEAD_DIM), 0.05),
        "w_o": nrm(ks[11], (DEPTH, MIX_WIDTH, D_MODEL), MIX_WIDTH ** -0.5),
        "norm_ffn_g": 1.0 + nrm(ks[12], (DEPTH, D_MODEL), 0.05),
        "w_up": nrm(ks[13], (DEPTH, D_MODEL, 2 * D_FF), D_MODEL ** -0.5),
        "conv_w": nrm(ks[14], (DEPTH, CONV_WIDTH, 2 * D_FF), CONV_WIDTH ** -0.5),
        "conv_b": nrm(ks[15], (DEPTH, 2 * D_FF), 0.02),
        "w_down": nrm(ks[16], (DEPTH, D_FF, D_MODEL), D_FF ** -0.5),
        "norm_final_g": 1.0 + nrm(ks[17], (D_MODEL,), 0.05),
    }

def first_block(x, positions, norm_mix_g, w_in, pool_w, pool_scale, lambda_q1, lambda_k1,
              lambda_q2, lambda_k2, attn_norm_g, w_o, norm_ffn_g, w_up, conv_w, conv_b,
              w_down, norm_final_g):
    b, s, _ = x.shape
    cos, sin = rope_tables(positions, x.dtype)
    for l in range(DEPTH):
        h = rmsnorm(x, norm_mix_g[l])
        proj = h @ w_in[l]
        p, q, k, v = jnp.split(
            proj, [POOL_WIDTH, POOL_WIDTH + ATTN_WIDTH, POOL_WIDTH + 2 * ATTN_WIDTH], axis=-1)
        pool_out = multiscale_pool(p, pool_w[l], pool_scale[l])
        q = apply_rope(q.reshape(b, s, N_DIFF_HEADS, 2, DIFF_HEAD_DIM), cos, sin)
        k = apply_rope(k.reshape(b, s, N_DIFF_HEADS, 2, DIFF_HEAD_DIM), cos, sin)
        q = q.transpose(0, 2, 3, 1, 4)
        k = k.transpose(0, 2, 3, 1, 4)
        v = v.reshape(b, s, N_DIFF_HEADS, V_HEAD_DIM).transpose(0, 2, 1, 3)
        lam_init = 0.8 - 0.6 * float(np.exp(-0.3 * l))
        lam = (jnp.exp(jnp.sum(lambda_q1[l].astype(jnp.float32) * lambda_k1[l].astype(jnp.float32)))
               - jnp.exp(jnp.sum(lambda_q2[l].astype(jnp.float32) * lambda_k2[l].astype(jnp.float32)))
               + lam_init)
        attn_out = diff_attention(q, k, v, lam, lam_init, attn_norm_g[l])
        mix = jnp.concatenate([pool_out, attn_out], axis=-1) @ w_o[l]
        x = x + mix
        h = rmsnorm(x, norm_ffn_g[l])
        u = causal_dwconv(h @ w_up[l], conv_w[l], conv_b[l])
        gate, val = jnp.split(u, 2, axis=-1)
        x = x + (jax.nn.silu(gate) * val) @ w_down[l]
    return rmsnorm(x, norm_final_g)


D_MIX = 2 * D_MODEL
SSD_WIDTH = D_MIX // 2
SSD_HEAD_DIM = 64
SSD_HEADS = SSD_WIDTH // SSD_HEAD_DIM
SSD_GROUPS = 2
SSD_STATE = 128
SSD_CONV = 4
SSD_XBC = SSD_WIDTH + 2 * SSD_GROUPS * SSD_STATE
ML_WIDTH = D_MIX - SSD_WIDTH
ML_HEADS = 8
ML_HEAD_DIM = ML_WIDTH // ML_HEADS
ML_CONV = 4
IN_COLS = (SSD_WIDTH + SSD_XBC + SSD_HEADS) + (4 * ML_WIDTH + 2 * ML_HEADS)
MOE_GROUPS = 4
EXPERTS_PER_GROUP = 8
N_EXPERTS = MOE_GROUPS * EXPERTS_PER_GROUP
TOP_K = 2
D_EXPERT = D_MODEL // 2
STAB_INIT = -1e30


def rmsnorm_2(x, w):
    xf = x.astype(jnp.float32)
    y = xf * lax.rsqrt(jnp.mean(xf * xf, axis=-1, keepdims=True) + EPS)
    return (y * w.astype(jnp.float32)).astype(x.dtype)

def group_rmsnorm(y, w, groups):
    b, l, c = y.shape
    yg = y.reshape(b, l, groups, c // groups)
    yg = yg * lax.rsqrt(jnp.mean(yg * yg, axis=-1, keepdims=True) + EPS)
    return yg.reshape(b, l, c) * w.astype(jnp.float32)

def causal_dwconv_2(x, w, b):
    k, c = w.shape
    y = lax.conv_general_dilated(x, w[:, None, :].astype(x.dtype), window_strides=(1,),
                                 padding=[(k - 1, 0)], dimension_numbers=("NWC", "WIO", "NWC"),
                                 feature_group_count=c)
    return y + b.astype(x.dtype)

def ssd_mixer(z, xbc, dt_raw, conv_w, conv_b, dt_bias, a_log, d_skip, norm_w):
    f32 = jnp.float32
    bsz, seq, _ = z.shape
    nc = seq // CHUNK
    r = SSD_HEADS // SSD_GROUPS
    xbc = jax.nn.silu(causal_dwconv_2(xbc, conv_w, conv_b)).astype(f32)
    xs = xbc[..., :SSD_WIDTH].reshape(bsz, seq, SSD_HEADS, SSD_HEAD_DIM)
    bm = xbc[..., SSD_WIDTH:SSD_WIDTH + SSD_GROUPS * SSD_STATE].reshape(bsz, seq, SSD_GROUPS, SSD_STATE)
    cm = xbc[..., SSD_WIDTH + SSD_GROUPS * SSD_STATE:].reshape(bsz, seq, SSD_GROUPS, SSD_STATE)
    dt = jax.nn.softplus(dt_raw.astype(f32) + dt_bias.astype(f32))
    a = -jnp.exp(a_log.astype(f32))
    xdt = (xs * dt[..., None]).reshape(bsz, nc, CHUNK, SSD_GROUPS, r, SSD_HEAD_DIM)
    xdt = jnp.moveaxis(xdt, 1, 0)
    adt = jnp.transpose((dt * a).reshape(bsz, nc, CHUNK, SSD_GROUPS, r), (1, 0, 3, 4, 2))
    bc = jnp.moveaxis(bm.reshape(bsz, nc, CHUNK, SSD_GROUPS, SSD_STATE), 1, 0)
    cc = jnp.moveaxis(cm.reshape(bsz, nc, CHUNK, SSD_GROUPS, SSD_STATE), 1, 0)
    mask = jnp.tril(jnp.ones((CHUNK, CHUNK), dtype=bool))

    def step(state, inp):
        x_c, a_c, b_c, c_c = inp
        a_cs = jnp.cumsum(a_c, axis=-1)
        seg = jnp.where(mask, a_cs[..., :, None] - a_cs[..., None, :], -jnp.inf)
        lmat = jnp.exp(seg)
        cb = jnp.einsum('blgn,bsgn->bgls', c_c, b_c)
        y = jnp.einsum('bgls,bgrls,bsgrp->blgrp', cb, lmat, x_c)
        y = y + jnp.einsum('blgn,bgrpn,bgrl->blgrp', c_c, state, jnp.exp(a_cs))
        decay = jnp.exp(a_cs[..., -1:] - a_cs)
        state = state * jnp.exp(a_cs[..., -1])[..., None, None] + \
            jnp.einsum('blgn,bgrl,blgrp->bgrpn', b_c, decay, x_c)
        return state, y

    state0 = jnp.zeros((bsz, SSD_GROUPS, r, SSD_HEAD_DIM, SSD_STATE), f32)
    _, y = lax.scan(step, state0, (xdt, adt, bc, cc))
    y = jnp.moveaxis(y, 0, 1).reshape(bsz, seq, SSD_HEADS, SSD_HEAD_DIM)
    y = y + d_skip.astype(f32)[:, None] * xs
    y = y.reshape(bsz, seq, SSD_WIDTH) * jax.nn.silu(z.astype(f32))
    return group_rmsnorm(y, norm_w, SSD_GROUPS).astype(z.dtype)

def mlstm_mixer(qk, v, o_pre, i_pre, f_pre, conv_w, conv_b, i_bias, f_bias, norm_w):
    f32 = jnp.float32
    bsz, seq, _ = v.shape
    nc = seq // CHUNK
    qk = jax.nn.silu(causal_dwconv_2(qk, conv_w, conv_b)).astype(f32)
    shp = (bsz, nc, CHUNK, ML_HEADS, ML_HEAD_DIM)
    q = jnp.moveaxis(qk[..., :ML_WIDTH].reshape(shp), 1, 0)
    k = jnp.moveaxis(qk[..., ML_WIDTH:].reshape(shp), 1, 0) * (ML_HEAD_DIM ** -0.5)
    vv = jnp.moveaxis(v.astype(f32).reshape(shp), 1, 0)
    ig = i_pre.astype(f32) + i_bias.astype(f32)
    lf = jax.nn.log_sigmoid(f_pre.astype(f32) + f_bias.astype(f32))
    ig = jnp.transpose(ig.reshape(bsz, nc, CHUNK, ML_HEADS), (1, 0, 3, 2))
    lf = jnp.transpose(lf.reshape(bsz, nc, CHUNK, ML_HEADS), (1, 0, 3, 2))
    mask = jnp.tril(jnp.ones((CHUNK, CHUNK), dtype=bool))

    def step(carry, inp):
        cmem, nmem, m = carry
        q_c, k_c, v_c, i_c, f_c = inp
        bcum = jnp.cumsum(f_c, axis=-1)
        dmat = jnp.where(mask, bcum[..., :, None] - bcum[..., None, :] + i_c[..., None, :], -jnp.inf)
        m_inter = bcum + m[..., None]
        m_t = jnp.maximum(m_inter, jnp.max(dmat, axis=-1))
        w = jnp.exp(dmat - m_t[..., None])
        s = jnp.einsum('blhd,bshd->bhls', q_c, k_c) * w
        inter = jnp.exp(m_inter - m_t)
        num = jnp.einsum('bhls,bshv->blhv', s, v_c) + \
            jnp.einsum('blhk,bhkv->blhv', q_c, cmem) * jnp.swapaxes(inter, 1, 2)[..., None]
        den = jnp.sum(s, axis=-1) + inter * jnp.einsum('blhk,bhk->bhl', q_c, nmem)
        den = jnp.maximum(jnp.abs(den), jnp.exp(-m_t))
        h = num / jnp.swapaxes(den, 1, 2)[..., None]
        g = bcum[..., -1]
        a = g[..., None] - bcum + i_c
        m_new = jnp.maximum(g + m, jnp.max(a, axis=-1))
        wc = jnp.exp(a - m_new[..., None])
        carry_scale = jnp.exp(g + m - m_new)
        cmem = cmem * carry_scale[..., None, None] + jnp.einsum('bhs,bshk,bshv->bhkv', wc, k_c, v_c)
        nmem = nmem * carry_scale[..., None] + jnp.einsum('bhs,bshk->bhk', wc, k_c)
        return (cmem, nmem, m_new), h

    carry0 = (jnp.zeros((bsz, ML_HEADS, ML_HEAD_DIM, ML_HEAD_DIM), f32),
              jnp.zeros((bsz, ML_HEADS, ML_HEAD_DIM), f32),
              jnp.full((bsz, ML_HEADS), STAB_INIT, f32))
    _, h = lax.scan(step, carry0, (q, k, vv, ig, lf))
    h = jnp.moveaxis(h, 0, 1).reshape(bsz, seq, ML_HEADS, ML_HEAD_DIM)
    mu = jnp.mean(h, axis=-1, keepdims=True)
    var = jnp.mean((h - mu) ** 2, axis=-1, keepdims=True)
    h = ((h - mu) * lax.rsqrt(var + EPS)).reshape(bsz, seq, ML_WIDTH) * norm_w.astype(f32)
    h = jax.nn.sigmoid(o_pre.astype(f32)) * h
    return h.astype(v.dtype)

def hier_moe(h, wg, bg, we, be, w_gate, w_up, w_down):
    bsz, seq, d = h.shape
    t = bsz * seq
    xf = h.reshape(t, d)
    x32 = xf.astype(jnp.float32)
    p_group = jax.nn.softmax(x32 @ wg.astype(jnp.float32) + bg.astype(jnp.float32), axis=-1)
    pg, g_sel = lax.top_k(p_group, 1)
    e_logits = (x32 @ we.astype(jnp.float32) + be.astype(jnp.float32)).reshape(t, MOE_GROUPS, EXPERTS_PER_GROUP)
    e_in = jnp.take_along_axis(e_logits, g_sel[:, :, None], axis=1)[:, 0]
    top_v, top_i = lax.top_k(e_in, TOP_K)
    gates = jax.nn.softmax(top_v, axis=-1) * pg
    ids = (g_sel * EXPERTS_PER_GROUP + top_i).reshape(-1).astype(jnp.int32)
    order = jnp.argsort(ids)
    tok = order // TOP_K
    xs = xf[tok]
    sizes = jnp.bincount(ids, length=N_EXPERTS).astype(jnp.int32)
    hg = lax.ragged_dot(xs, w_gate.astype(xs.dtype), sizes)
    hu = lax.ragged_dot(xs, w_up.astype(xs.dtype), sizes)
    ys = lax.ragged_dot(jax.nn.silu(hg) * hu, w_down.astype(xs.dtype), sizes)
    ys = ys * gates.reshape(-1)[order][:, None].astype(ys.dtype)
    y = jax.ops.segment_sum(ys, tok, num_segments=t)
    return y.reshape(bsz, seq, d).astype(h.dtype)

def second_inputs(seed: int = 0) -> dict:
    key = jax.random.key(seed)
    ks = jax.random.split(key, 26)
    nrm = lambda k, s, sc: jax.random.normal(k, s, jnp.float32) * sc
    dt0 = jnp.exp(jax.random.uniform(ks[6], (DEPTH, SSD_HEADS), jnp.float32, math.log(1e-3), math.log(1e-1)))
    return {
        "x": jax.random.normal(ks[0], (BATCH, SEQ, D_MODEL), jnp.float32),
        "norm1_w": 1.0 + nrm(ks[1], (DEPTH, D_MODEL), 0.02),
        "w_in": nrm(ks[2], (DEPTH, D_MODEL, IN_COLS), D_MODEL ** -0.5),
        "ssd_conv_w": nrm(ks[3], (DEPTH, SSD_CONV, SSD_XBC), SSD_CONV ** -0.5),
        "ssd_conv_b": nrm(ks[4], (DEPTH, SSD_XBC), 0.02),
        "ssd_dt_bias": dt0 + jnp.log(-jnp.expm1(-dt0)),
        "ssd_a_log": jnp.log(jax.random.uniform(ks[5], (DEPTH, SSD_HEADS), jnp.float32, 1.0, 16.0)),
        "ssd_d": 1.0 + nrm(ks[7], (DEPTH, SSD_HEADS), 0.1),
        "ssd_norm_w": 1.0 + nrm(ks[8], (DEPTH, SSD_WIDTH), 0.02),
        "ml_conv_w": nrm(ks[9], (DEPTH, ML_CONV, 2 * ML_WIDTH), ML_CONV ** -0.5),
        "ml_conv_b": nrm(ks[10], (DEPTH, 2 * ML_WIDTH), 0.02),
        "ml_i_bias": nrm(ks[11], (DEPTH, ML_HEADS), 0.1),
        "ml_f_bias": 3.0 + 3.0 * jax.random.uniform(ks[12], (DEPTH, ML_HEADS), jnp.float32),
        "ml_norm_w": 1.0 + nrm(ks[13], (DEPTH, ML_WIDTH), 0.02),
        "w_out": nrm(ks[14], (DEPTH, D_MIX, D_MODEL), D_MIX ** -0.5),
        "norm2_w": 1.0 + nrm(ks[15], (DEPTH, D_MODEL), 0.02),
        "router_g_w": nrm(ks[16], (DEPTH, D_MODEL, MOE_GROUPS), D_MODEL ** -0.5),
        "router_g_b": nrm(ks[17], (DEPTH, MOE_GROUPS), 0.01),
        "router_e_w": nrm(ks[18], (DEPTH, D_MODEL, N_EXPERTS), D_MODEL ** -0.5),
        "router_e_b": nrm(ks[19], (DEPTH, N_EXPERTS), 0.01),
        "exp_w_gate": nrm(ks[20], (DEPTH, N_EXPERTS, D_MODEL, D_EXPERT), D_MODEL ** -0.5),
        "exp_w_up": nrm(ks[21], (DEPTH, N_EXPERTS, D_MODEL, D_EXPERT), D_MODEL ** -0.5),
        "exp_w_down": nrm(ks[22], (DEPTH, N_EXPERTS, D_EXPERT, D_MODEL), D_EXPERT ** -0.5),
        "norm_f_w": 1.0 + nrm(ks[23], (D_MODEL,), 0.02),
    }

def second_block(x, norm1_w, w_in, ssd_conv_w, ssd_conv_b, ssd_dt_bias, ssd_a_log, ssd_d, ssd_norm_w,
              ml_conv_w, ml_conv_b, ml_i_bias, ml_f_bias, ml_norm_w, w_out, norm2_w,
              router_g_w, router_g_b, router_e_w, router_e_b, exp_w_gate, exp_w_up, exp_w_down, norm_f_w):
    o1 = SSD_WIDTH
    o2 = o1 + SSD_XBC
    o3 = o2 + SSD_HEADS
    o4 = o3 + 2 * ML_WIDTH
    o5 = o4 + ML_WIDTH
    o6 = o5 + ML_WIDTH
    o7 = o6 + ML_HEADS
    for layer in range(DEPTH):
        h = rmsnorm_2(x, norm1_w[layer])
        p = jnp.einsum('bsd,de->bse', h, w_in[layer])
        y_ssd = ssd_mixer(p[..., :o1], p[..., o1:o2], p[..., o2:o3],
                          ssd_conv_w[layer], ssd_conv_b[layer], ssd_dt_bias[layer],
                          ssd_a_log[layer], ssd_d[layer], ssd_norm_w[layer])
        y_ml = mlstm_mixer(p[..., o3:o4], p[..., o4:o5], p[..., o5:o6], p[..., o6:o7], p[..., o7:],
                           ml_conv_w[layer], ml_conv_b[layer], ml_i_bias[layer], ml_f_bias[layer],
                           ml_norm_w[layer])
        mix = jnp.concatenate([y_ssd, y_ml], axis=-1)
        x = x + jnp.einsum('bse,ed->bsd', mix, w_out[layer])
        h2 = rmsnorm_2(x, norm2_w[layer])
        x = x + hier_moe(h2, router_g_w[layer], router_g_b[layer], router_e_w[layer], router_e_b[layer],
                         exp_w_gate[layer], exp_w_up[layer], exp_w_down[layer])
    return rmsnorm_2(x, norm_f_w)


def setup_inputs(seed=0):
    out = dict(first_inputs(seed))
    for name, value in second_inputs(seed + 1).items():
        if name != "x":
            out[name + "_2"] = value
    return out


def reference(
    x, positions, norm_mix_g, w_in, pool_w, pool_scale, lambda_q1, lambda_k1, lambda_q2,
    lambda_k2, attn_norm_g, w_o, norm_ffn_g, w_up, conv_w, conv_b, w_down, norm_final_g,
    norm1_w_2, w_in_2, ssd_conv_w_2, ssd_conv_b_2, ssd_dt_bias_2, ssd_a_log_2, ssd_d_2,
    ssd_norm_w_2, ml_conv_w_2, ml_conv_b_2, ml_i_bias_2, ml_f_bias_2, ml_norm_w_2, w_out_2,
    norm2_w_2, router_g_w_2, router_g_b_2, router_e_w_2, router_e_b_2, exp_w_gate_2, exp_w_up_2,
    exp_w_down_2, norm_f_w_2,
):
    x = first_block(
        x, positions, norm_mix_g, w_in, pool_w, pool_scale, lambda_q1, lambda_k1, lambda_q2,
        lambda_k2, attn_norm_g, w_o, norm_ffn_g, w_up, conv_w, conv_b, w_down, norm_final_g,
    )
    return second_block(
        x, norm1_w_2, w_in_2, ssd_conv_w_2, ssd_conv_b_2, ssd_dt_bias_2, ssd_a_log_2, ssd_d_2,
        ssd_norm_w_2, ml_conv_w_2, ml_conv_b_2, ml_i_bias_2, ml_f_bias_2, ml_norm_w_2, w_out_2,
        norm2_w_2, router_g_w_2, router_g_b_2, router_e_w_2, router_e_b_2, exp_w_gate_2,
        exp_w_up_2, exp_w_down_2, norm_f_w_2,
    )


_drawn_inputs = setup_inputs


def setup_inputs(seed=0):
    import zlib

    import numpy as np

    out = dict(_drawn_inputs(seed))
    spreads = {}
    factors = {'lambda_k2': 4.926,
     'conv_b': 2.695,
     'ml_conv_b_2': 3.43,
     'ml_i_bias_2': 64.0,
     'ml_norm_w_2': 12.517,
     'router_e_b_2': 24.151,
     'norm_f_w_2': 8.023,
     'lambda_q1': 3.803,
     'ssd_conv_b_2': 4.544,
     'ssd_norm_w_2': 4.34,
     'norm2_w_2': 3.085,
     'router_g_b_2': 5.183}
    for name, (base, spread) in spreads.items():
        noise = np.random.default_rng([zlib.crc32(name.encode()), seed]).standard_normal(out[name].shape)
        drawn = base * np.exp(spread * noise) if base else spread * noise
        out[name] = __import__('jax').numpy.asarray(drawn.astype(out[name].dtype))
    for name, factor in factors.items():
        out[name] = (out[name] * factor).astype(out[name].dtype)
    return out
```

```python
from contextlib import ExitStack

import numpy as np

import concourse.bass as bass
from concourse import mybir

P = 128
T = 2
S = 256
D = 1024
ALU = mybir.AluOpType
ACT = mybir.ActivationFunctionType
F32 = mybir.dt.float32
I32 = mybir.dt.int32
AX = mybir.AxisListType.X
EPS = 1e-6
NEG = -1e30
FF = 22
NE = 32
RING = 6
SLOT = 4096

PT_ROWS = [("norm_mix_g", 8), ("pool_scale", 4), ("attn_norm_g", 4), ("norm_ffn_g", 8), ("conv_w", 132),
           ("conv_b", 44), ("norm1_w_2", 8), ("ssd_conv_w_2", 48), ("ssd_conv_b_2", 12), ("ssd_norm_w_2", 8),
           ("ml_conv_w_2", 64), ("ml_conv_b_2", 16), ("ml_norm_w_2", 8), ("norm2_w_2", 8)]
PT = {}
_at = 0
for _n, _k in PT_ROWS:
    PT[_n] = _at
    _at += _k
NPT = _at
BR_ROWS = [("lambda_q1", 64), ("lambda_k1", 64), ("lambda_q2", 64), ("lambda_k2", 64), ("ssd_dt_bias_2", 16),
           ("ml_i_bias_2", 8), ("ml_f_bias_2", 8), ("ssd_a_log_2", 16), ("ssd_d_2", 16), ("router_g_b_2", 4),
           ("router_e_b_2", 32)]
BR = {}
_at = 0
for _n, _k in BR_ROWS:
    BR[_n] = _at
    _at += _k
NBR = _at
CN_COLS = [("ident", 128), ("ux", 384), ("slt", 128), ("neg", 384), ("chm", 384), ("invf", 32), ("iota", 36), ("mh", 8)]
CN = {}
_at = 0
for _n, _k in CN_COLS:
    CN[_n] = _at
    _at += _k
NCN = _at


def inv_freq():
    exact = 10000.0 ** (-np.arange(0, 64, 2, dtype=np.float64) / 64)
    return exact.astype(np.float32)


def constants():
    c = np.zeros((P, NCN), np.float32)
    i = np.arange(P)
    tri = (i[:, None] <= i[None, :]).astype(np.float32)
    c[:, CN["ident"]:CN["ident"] + 128] = np.eye(P)
    c[:, CN["ux"]:CN["ux"] + 384] = np.concatenate([tri, np.ones((P, P)), tri], 1)
    c[:, CN["slt"]:CN["slt"] + 128] = i[:, None] > i[None, :]
    neg = np.where(i[None, :] > i[:, None], NEG, 0.0)
    c[:, CN["neg"]:CN["neg"] + 384] = np.concatenate([neg, 0 * neg, neg], 1)
    chm = np.where(i[None, :] // 64 > i[:, None] // 64, NEG, 0.0)
    c[:, CN["chm"]:CN["chm"] + 384] = np.concatenate([chm, 0 * chm, chm], 1)
    c[:, CN["invf"]:CN["invf"] + 32] = inv_freq()[None]
    c[:, CN["iota"]:CN["iota"] + 4] = 100 + np.arange(4)
    c[:, CN["iota"] + 4:CN["iota"] + 36] = 100 + np.arange(32)
    c[:, CN["mh"]:CN["mh"] + 8] = -0.5
    pool = np.zeros((P, 4, 384), np.float32)
    t = np.arange(S)
    for g, w in enumerate((2, 4, 8, 16)):
        count = np.minimum(t + 1, w).astype(np.float32)
        a = ((t[:, None] <= t[None, :]) & (t[:, None] > t[None, :] - w)) / count[None, :] - np.eye(S)
        pool[:, g, 0:256] = a[0:128]
        pool[:, g, 256:384] = a[128:256, 128:256]
    return c, pool.reshape(P, 1536)


class Engine:

    def __init__(self, sem):
        self.sem, self.n, self.ops, self.seen = sem, 0, [], {}

    def wait(self, *marks):
        for m in marks:
            if m is None:
                continue
            s, v = m
            if self.seen.get(id(s), 0) < v:
                self.seen[id(s)] = v
                self.ops.append(lambda e, s=s, v=v: e.wait_ge(s, v))

    def __call__(self, fn, *marks, sig=True):
        self.wait(*marks)
        if not sig:
            self.ops.append(fn)
            return None
        self.n += 1
        self.ops.append(lambda e: fn(e).then_inc(self.sem, 1))
        return self.sem, self.n

    def dma(self, sem, fn, *marks):
        self.wait(*marks)
        sem[1] += 16
        s = sem[0]
        self.ops.append(lambda e: fn(e).then_inc(s, 16))
        return s, sem[1]

    def run(self, e):
        for op in self.ops:
            op(e)


def bc(ap, *shape):
    return ap.broadcast_to(list(shape))


def build(nc, a, out):
    ctx = ExitStack()
    with ctx:
        def sb(name, *shape, dt=F32):
            return ctx.enter_context(nc.sbuf_tensor(name, [P, *shape], dt))

        def sem(name):
            return ctx.enter_context(nc.semaphore(name))

        def dsem(name):
            return [sem(name), 0]

        ring = [sb(f"ring{i}", SLOT) for i in range(RING)]
        cn = sb("cn", NCN)
        pt = sb("pt", NPT)
        br = sb("br", NBR)
        wrt = sb("wrt", 8, 36)
        gb = sb("gb", D)
        X = sb("X", T, D)
        H = sb("H", T, D)
        HT = sb("HT", 8, S)
        ZZ = sb("ZZ", T, D)
        XBCT = sb("XBCT", 12, S)
        XS = sb("XS", T, D)
        QKT = sb("QKT", 16, S)
        VV = sb("VV", T, D)
        MIXT = sb("MIXT", 16, S)
        CV = sb("CV", 4, S)
        wsm = MIXT[:, 15, :].rearrange("p (k n) -> p k n", k=8)
        sm = sb("sm", 512)
        bank = [ctx.enter_context(nc.psum_tensor(f"bank{i}", [P, 512], F32)) for i in range(8)]

        def const(name, n, at=0):
            return cn[:, CN[name] + at:CN[name] + at + n]

        ident = const("ident", 128)

        pe, ve, sc, po, sy = (Engine(sem(n)) for n in ("s_pe", "s_ve", "s_sc", "s_po", "s_sy"))
        rsem = [dsem(f"s_ring{i}") for i in range(RING)]

        def kmaj(w, k0, nk, c0, n):
            return w[k0 * 128:(k0 + nk) * 128, c0:c0 + n].rearrange("(k p) n -> p k n", p=P)

        stream = []
        for c in (1, 2, 3, 0):
            stream.append(("in", c, kmaj(a["w_in"], 0, 8, c * 512, 512)))
        for k in range(2):
            stream.append(("wo", k, kmaj(a["w_o"], 4 * k, 4, 0, D)))
        groups = [(g, min(4, FF - 4 * g)) for g in range(6)]
        ffn = []
        for g, n in groups:
            ffn.append([("gate", g, kmaj(a["w_up"], 0, 8, g * 512, n * 128)),
                        ("val", g, kmaj(a["w_up"], 0, 8, 2816 + g * 512, n * 128)),
                        ("down", g, kmaj(a["w_down"], 4 * g, n, 0, D))])
        for g, _ in groups:
            stream += ffn[g][0:2]
            if g:
                stream.append(ffn[g - 1][2])
        stream.append(ffn[5][2])
        W2 = a["w_in_2"]
        for c in range(3):
            stream.append(("xbc", c, kmaj(W2, 0, 8, 1024 + 512 * c, 512)))
        for c in range(2):
            stream.append(("z", c, kmaj(W2, 0, 8, 512 * c, 512)))
        for c in range(4):
            stream.append(("qk", c, kmaj(W2, 0, 8, 2576 + 512 * c, 512)))
        for c in range(2):
            stream.append(("v", c, kmaj(W2, 0, 8, 4624 + 512 * c, 512)))
        for c in range(2):
            stream.append(("o", c, kmaj(W2, 0, 8, 5648 + 512 * c, 512)))
        for k in range(4):
            stream.append(("wout", k, kmaj(a["w_out_2"], 4 * k, 4, 0, D)))
        for e in range(NE):
            stream.append(("eg", e, kmaj(a["exp_w_gate_2"][e], 0, 8, 0, 512)))
            stream.append(("eu", e, kmaj(a["exp_w_up_2"][e], 0, 8, 0, 512)))
            stream.append(("ed", e, kmaj(a["exp_w_down_2"][e], 0, 4, 0, D)))

        nxt = [0]
        loaded = {}
        freed = {}

        def load_next():
            i = nxt[0]
            kind, n, src = stream[i]
            nxt[0] += 1
            k, w = src.shape[1], src.shape[2]
            dst = ring[i % RING][:, 0:k * w].rearrange("p (k n) -> p k n", k=k)
            m = sy.dma(rsem[i % RING], lambda e: e.dma_start(dst, src), freed.get(i - RING))
            loaded[(kind, n)] = (dst, m, i)

        def weight(kind, n):
            return loaded[(kind, n)][0:2]

        def release(kind, n, mark):
            i = loaded[(kind, n)][2]
            freed[i] = mark
            assert nxt[0] == i + RING or nxt[0] == len(stream)
            if nxt[0] < len(stream):
                load_next()

        read = [None] * 8
        turn = [0]

        def work(n=4, base=4):
            b = base + turn[0] % n
            turn[0] += 1
            return b

        x_t = a["x"].rearrange("(t p) d -> p t d", p=P)
        ld = {}
        for i, (name, dst, src) in enumerate([
                ("x", X[:, :, :], x_t), ("cn", cn[:, :], a["cn"]), ("pt", pt[:, :], a["pt"]),
                ("pos", sm[:, 0:2].bitcast(I32), a["positions"])]):
            ld[name] = sc.dma(dsem(f"s_ld{i}"), lambda e, dst=dst, src=src: e.dma_start(dst, src))
        for _ in range(RING):
            load_next()
        pool_a = QKT[:, 0:6, :].rearrange("p a b -> p (a b)")
        pool_w = QKT[:, 6:8, :].rearrange("p a (b c) -> p (a b) c", c=128)
        gsem = dsem("s_gb")
        for i, (name, dst, src) in enumerate([
                ("br", br[:, :], a["br"].partition_broadcast(P)),
                ("pa", pool_a, a["pool_a"]),
                ("pw", pool_w, a["pool_w"].rearrange("g c d -> c g d")),
                ("wsm", wsm, a["wsm"]), ("wrt", wrt[:, :, :], a["wrt"])]):
            ld[name] = sc.dma(dsem(f"s_le{i}"), lambda e, dst=dst, src=src: e.dma_start(dst, src))
        ld["gb"] = sc.dma(gsem, lambda e: e.dma_start(gb[:, :], a["norm_final_g"].partition_broadcast(P)))

        smat = [2]

        def small(n):
            v = sm[:, smat[0]:smat[0] + n]
            smat[0] += n
            assert smat[0] <= 512
            return v

        def ptcol(name, i=0, n=1):
            return pt[:, PT[name] + i:PT[name] + i + n]

        def brow(name, n):
            return br[:, BR[name]:BR[name] + n]

        ss, rs = small(2), small(2)
        junk = CV[:, :, :].rearrange("p a b -> p (a b)")

        def rstd(dst, src, n, *marks):
            m = ve(lambda e: e.tensor_scalar(dst, src, 1.0 / n, EPS, ALU.mult, ALU.add), *marks)
            half = const("mh", dst.shape[1])
            return po(lambda e: e.tensor_tensor(dst, dst, half, ALU.pow), m, ld["cn"])

        hold = {}

        def rms_rows(xm):
            last = hold.get("junk")
            for t in range(T):
                last = sc(lambda e, t=t: e.activation(junk, X[:, t, :], ACT.Square, accum_out=ss[:, t:t + 1]),
                          xm, last, hold.get("ss"), ld["x"])
            hold["junk"] = last
            m = rstd(rs, ss, D, last)
            hold["ss"] = m
            return m

        def to_columns(src, m, n0, gname, dst, marks_free, engs=None):
            done = []
            for t in range(T):
                for b in range(2):
                    w = work()
                    for k in range(4):
                        p = pe(lambda e, w=w, k=k, b=b, t=t: e.transpose(
                            bank[w][:, k * 128:(k + 1) * 128], src[:, t, (4 * b + k) * 128:(4 * b + k + 1) * 128],
                            ident), m[t], read[w], ld["cn"], sig=(k == 3))
                    o = dst[:, n0 + 4 * b:n0 + 4 * b + 4, t * 128:(t + 1) * 128]
                    i = bank[w][:, :].rearrange("p (k c) -> p k c", k=4)
                    g = bc(ptcol(gname, 4 * b, 4).unsqueeze(2), P, 4, 128)
                    read[w] = ve(lambda e, o=o, i=i, g=g: e.tensor_tensor(o, i, g, ALU.mult), p, ld["pt"],
                                 marks_free)
                    done.append(read[w])
            return done[-1]

        def rmsnorm_T(xm, gname, ht_free):
            r = rms_rows(xm)
            m = [ve(lambda e, t=t: e.tensor_scalar(H[:, t, :], X[:, t, :], rs[:, t:t + 1], None, ALU.mult), r,
                    hold.get("H"))
                 for t in range(T)]
            hold["ss"] = m[1]
            done = to_columns(H, m, 0, gname, HT, ht_free)
            hold["H"] = (pe.sem, pe.n)
            return done

        def tok_major(kind, c, t, htm, n=512, src=None):
            w = work()
            wt, wm = weight(kind, c) if src is None else src
            for k in range(8):
                p = pe(lambda e, k=k, t=t, w=w, wt=wt: e.matmul(
                    bank[w][:, 0:n], HT[:, k, t * 128:(t + 1) * 128], wt[:, k, 0:n], start=(k == 0), stop=(k == 7)),
                    htm, wm, read[w], sig=(k == 7))
            return w, p

        ht = rmsnorm_T(None, "norm_mix_g", None)

        posf = small(2)
        m = ve(lambda e: e.tensor_copy(posf, sm[:, 0:2].bitcast(I32)), ld["pos"])
        RT = H[:, 0, :]
        ang = XBCT[:, 0, 0:64].rearrange("p (t f) -> p t f", t=T)
        kk = XBCT[:, 0, 64:128].rearrange("p (t f) -> p t f", t=T)
        kc = XBCT[:, 0, 128:192].rearrange("p (t f) -> p t f", t=T)
        sin = XBCT[:, 1, 0:64].rearrange("p (t f) -> p t f", t=T)
        cos = XBCT[:, 1, 64:128].rearrange("p (t f) -> p t f", t=T)
        for t in range(T):
            am = ve(lambda e, t=t: e.tensor_scalar(ang[:, t, :], const("invf", 32), posf[:, t:t + 1], None,
                                                   ALU.mult), m, ld["cn"])
        MAGIC = 12582912.0
        C1, C2 = 6.28125, 0.0019350051879882812
        C3 = 6.283185307179586 - C1 - C2
        rot = []
        for dst, kb, off in ((sin, kk, 0.0), (cos, kc, 0.25)):
            m = ve(lambda e, kb=kb, off=off: e.tensor_scalar(kb, ang, 1.0 / 6.283185307179586, off, ALU.mult,
                                                             ALU.add), am)
            m = ve(lambda e, kb=kb: e.tensor_scalar(kb, kb, MAGIC, None, ALU.add), m)
            m = ve(lambda e, kb=kb: e.tensor_scalar(kb, kb, MAGIC, None, ALU.subtract), m)
            prev = ang
            for c in (C1, C2, C3):
                m = ve(lambda e, kb=kb, dst=dst, c=c, prev=prev: e.scalar_tensor_tensor(
                    out=dst, in0=kb, scalar=-c, in1=prev, op0=ALU.mult, op1=ALU.add), m)
                prev = dst
            if off:
                m = ve(lambda e, dst=dst: e.tensor_scalar(dst, dst, 1.5707963267948966, None, ALU.add), m)
            m = ve(lambda e, dst=dst: e.tensor_scalar(dst, dst, 3.1415925, -3.1415925, ALU.min, ALU.max), m)
            rot.append(sc(lambda e, dst=dst: e.activation(dst, dst, ACT.Sin), m))

        qkr = [[None] * T for _ in range(2)]
        QKR = ZZ
        t3 = None
        for c in range(2):
            for t in range(T):
                w, p = tok_major("in", c + 1, t, ht)
                src = bank[w][:, :].rearrange("p (g f) -> p g f", f=32)
                tmp = CV[:, :, :].rearrange("p (j a) b -> p j (a b)", j=2)
                A, B = (tmp[:, j, :].rearrange("p (g f) -> p g f", f=32) for j in range(2))
                cb, sbb = (bc(v[:, t, :].unsqueeze(1), P, 16, 32) for v in (cos, sin))
                m1 = ve(lambda e, A=A, src=src, cb=cb: e.tensor_tensor(A, src, cb, ALU.mult), p, rot[1], t3,
                        hold["junk"])
                m2 = ve(lambda e, B=B, src=src, sbb=sbb: e.tensor_tensor(B, src, sbb, ALU.mult), rot[0])
                read[w] = m2
                o = QKR[:, t, c * 512:(c + 1) * 512].rearrange("p (g h f) -> p g h f", h=2, f=32)
                Av, Bv = (v.rearrange("p (g h) f -> p g h f", h=2) for v in (A, B))
                ve(lambda e, o=o, Av=Av, Bv=Bv: e.tensor_tensor(o[:, :, 0, :], Av[:, :, 0, :], Bv[:, :, 1, :],
                                                                ALU.subtract), m1, m2)
                t3 = ve(lambda e, o=o, Av=Av, Bv=Bv: e.tensor_tensor(o[:, :, 1, :], Bv[:, :, 0, :],
                                                                     Av[:, :, 1, :], ALU.add))
                qkr[c][t] = t3
            release("in", c + 1, (pe.sem, pe.n))
        hold["junk"] = t3
        vm = []
        for t in range(T):
            w, p = tok_major("in", 3, t, ht)
            read[w] = sc(lambda e, w=w, t=t: e.activation(VV[:, t, 0:512], bank[w][:, :], ACT.Copy), p)
            vm.append(read[w])
        release("in", 3, (pe.sem, pe.n))
        pm = []
        for t in range(T):
            w, p = tok_major("in", 0, t, ht)
            read[w] = sc(lambda e, w=w, t=t: e.activation(VV[:, t, 512:1024], bank[w][:, :], ACT.Copy), p)
            pm.append(read[w])
        release("in", 0, (pe.sem, pe.n))
        RT8 = XS[:, :, :].rearrange("p t (i s) -> p (t i) s", s=S)
        rt = None
        for t in range(T):
            for c in range(2):
                w = work()
                for k in range(4):
                    p = pe(lambda e, w=w, k=k, c=c, t=t: e.transpose(
                        bank[w][:, k * 128:(k + 1) * 128], QKR[:, t, c * 512 + k * 128:c * 512 + (k + 1) * 128],
                        ident), qkr[c][t], read[w], sig=(k == 3))
                rt = read[w] = sc(lambda e, w=w, c=c, t=t: e.activation(
                    RT8[:, 4 * c:4 * c + 4, t * 128:(t + 1) * 128],
                    bank[w][:, :].rearrange("p (k s) -> p k s", k=4), ACT.Copy), p)

        dT = CV
        for g in range(4):
            w = work()
            pg = VV[:, :, 512 + g * 128:512 + (g + 1) * 128]
            pe(lambda e, w=w, g=g, pg=pg: e.matmul(bank[w][:, 0:256], pg[:, 0, :],
                                                   pool_a[:, g * 384:g * 384 + 256], start=True, stop=False),
               pm[0], pm[1], ld["pa"], read[w], sig=False)
            p = pe(lambda e, w=w, g=g, pg=pg: e.matmul(bank[w][:, 128:256], pg[:, 1, :],
                                                       pool_a[:, g * 384 + 256:g * 384 + 384],
                                                       start=False, stop=True))
            m = read[w] = sc(lambda e, w=w, g=g: e.activation(dT[:, g, :], bank[w][:, 0:256], ACT.Copy), p,
                             hold["junk"])
            w = work()
            p = pe(lambda e, w=w, g=g: e.matmul(bank[w][:, 0:256], pool_w[:, g, :], dT[:, g, :], start=True,
                                                stop=True), m, ld["pw"], read[w])
            mixp = read[w] = ve(lambda e, w=w, g=g: e.tensor_scalar(MIXT[:, g, :], bank[w][:, 0:256],
                                                                    ptcol("pool_scale", g), None, ALU.mult), p)
        hold["junk"] = p

        lm, lt = small(6), junk[:, 0:64]
        m = hold["junk"]
        for i in range(2):
            m = ve(lambda e, i=i: e.tensor_tensor(lt, br[:, 128 * i:128 * i + 64], br[:, 128 * i + 64:128 * i + 128],
                                                  ALU.mult), m, ld["br"])
            m = ve(lambda e, i=i: e.reduce_sum(lm[:, i:i + 1], lt, AX), m)
        m = sc(lambda e: e.activation(lm[:, 2:4], lm[:, 0:2], ACT.Exp), m)
        m = ve(lambda e: e.tensor_tensor(lm[:, 4:5], lm[:, 3:4], lm[:, 2:3], ALU.subtract), m)
        nlam = ve(lambda e: e.tensor_scalar(lm[:, 5:6], lm[:, 4:5], -0.2, None, ALU.add), m)

        NSC = 64 ** -0.5
        Sx = XBCT[:, 3:9, :].rearrange("p a b -> p (a b)")
        AT = XBCT[:, 9:12, :].rearrange("p a b -> p (a b)")
        mx, nm, sums, rr = small(4), small(4), small(4), small(4)
        sx_free = [None] * 2
        at_free = [None] * 2
        tp_free = None
        OB = [0, 1]
        mxm = None
        avm = None
        for h in range(4):
            em = []
            for n in range(2):
                w = work()
                q, k = RT8[64 * n:64 * n + 64, h, :], RT8[64 * n:64 * n + 64, 4 + h, :]
                pe(lambda e, w=w, q=q, k=k: e.matmul(bank[w][:, 0:128], q[:, 0:128], k[:, 0:128], start=True,
                                                     stop=True), rt, read[w], sig=False)
                p = pe(lambda e, w=w, q=q, k=k: e.matmul(bank[w][:, 128:384], q[:, 128:256], k[:, 0:256],
                                                         start=True, stop=True))
                sx = Sx[:, ((h % 2) * 2 + n) * 384:((h % 2) * 2 + n + 1) * 384]
                m = read[w] = ve(lambda e, w=w, sx=sx: e.tensor_tensor(sx, bank[w][:, 0:384], const("chm", 384),
                                                                       ALU.add), p, sx_free[h % 2])
                ve(lambda e, sx=sx, n=n: e.reduce_max(mx[:, 2 * n:2 * n + 1], sx[:, 0:128], AX), m, mxm)
                m = ve(lambda e, sx=sx, n=n: e.reduce_max(mx[:, 2 * n + 1:2 * n + 2], sx[:, 128:384], AX))
                m = ve(lambda e, n=n: e.tensor_scalar(nm[:, 2 * n:2 * n + 2], mx[:, 2 * n:2 * n + 2], -NSC, None,
                                                      ALU.mult), m, hold.get("exp"))
                for i, (c0, c1) in enumerate(((0, 128), (128, 384))):
                    em.append(sc(lambda e, sx=sx, n=n, i=i, c0=c0, c1=c1: e.activation(
                        sx[:, c0:c1], sx[:, c0:c1], ACT.Exp, bias=nm[:, 2 * n + i:2 * n + i + 1], scale=NSC,
                        accum_out=sums[:, 2 * n + i:2 * n + i + 1]), m, hold.get("sums")))
            hold["exp"] = em[-1]
            m = ve(lambda e: e.reciprocal(rr[:, 0:4], sums[:, 0:4]), em[-1])
            hold["sums"] = m
            m = ve(lambda e: e.tensor_scalar(rr[:, 2:4], rr[:, 2:4], lm[:, 5:6], None, ALU.mult), m, nlam)
            s0 = Sx[:, (h % 2) * 768:(h % 2) * 768 + 384]
            s1 = Sx[:, (h % 2) * 768 + 384:(h % 2) * 768 + 768]
            for i, (c0, c1) in enumerate(((0, 128), (128, 384))):
                ma = ve(lambda e, s0=s0, i=i, c0=c0, c1=c1: e.tensor_scalar(s0[:, c0:c1], s0[:, c0:c1],
                                                                            rr[:, i:i + 1], None, ALU.mult), m)
                ma = ve(lambda e, s0=s0, s1=s1, i=i, c0=c0, c1=c1: e.scalar_tensor_tensor(
                    out=s0[:, c0:c1], in0=s1[:, c0:c1], scalar=rr[:, 2 + i:3 + i], in1=s0[:, c0:c1],
                    op0=ALU.mult, op1=ALU.add), ma)
            w = work()
            for j in range(3):
                p = pe(lambda e, w=w, j=j, s0=s0: e.transpose(bank[w][:, j * 128:(j + 1) * 128],
                                                              s0[:, j * 128:(j + 1) * 128], ident), ma, read[w],
                       sig=(j == 2))
            sx_free[h % 2] = p
            at = AT[:, (h % 2) * 384:(h % 2) * 384 + 384]
            am = read[w] = sc(lambda e, w=w, at=at: e.activation(at, bank[w][:, 0:384], ACT.Copy), p,
                              at_free[h % 2])
            vh = VV[:, :, h * 128:(h + 1) * 128]
            oc = slice(h * 128, (h + 1) * 128)
            pe(lambda e, at=at, vh=vh, oc=oc: e.matmul(bank[0][:, oc], at[:, 0:128], vh[:, 0, :], start=True,
                                                       stop=True), am, vm[0], vm[1], read[0], read[1], sig=False)
            pe(lambda e, at=at, vh=vh, oc=oc: e.matmul(bank[1][:, oc], at[:, 128:256], vh[:, 0, :], start=True,
                                                       stop=False), sig=False)
            avm = pe(lambda e, at=at, vh=vh, oc=oc: e.matmul(bank[1][:, oc], at[:, 256:384], vh[:, 1, :],
                                                             start=False, stop=True))
            at_free[h % 2] = avm
        OT = H
        os_, orr = small(8), small(8)
        om = []
        for i in range(T):
            o = bank[i][:, :]
            sqv = XBCT[:, 3:5, :].rearrange("p a b -> p (a b)")
            m = sc(lambda e, o=o, sqv=sqv: e.activation(sqv, o, ACT.Square), avm, hold.get("sq"))
            m = ve(lambda e, i=i, sqv=sqv: e.reduce_sum(os_[:, 4 * i:4 * i + 4],
                                                        sqv.rearrange("p (h c) -> p h c", h=4), AX), m)
            hold["sq"] = m
            m = rstd(orr[:, 4 * i:4 * i + 4], os_[:, 4 * i:4 * i + 4], 128, m)
            m = ve(lambda e, i=i: e.tensor_scalar(orr[:, 4 * i:4 * i + 4], orr[:, 4 * i:4 * i + 4], 0.8, None,
                                                  ALU.mult), m)
            m = ve(lambda e, i=i, o=o: e.tensor_tensor(
                OT[:, i, 0:512].rearrange("p (h c) -> p h c", h=4), o.rearrange("p (h c) -> p h c", h=4),
                bc(orr[:, 4 * i:4 * i + 4].unsqueeze(2), P, 4, 128), ALU.mult), m, hold.get("H"))
            read[i] = m
            om.append(m)
        for t in range(T):
            w = work()
            for k in range(4):
                p = pe(lambda e, w=w, k=k, t=t: e.transpose(bank[w][:, k * 128:(k + 1) * 128],
                                                            OT[:, t, k * 128:(k + 1) * 128], ident), om[t],
                       read[w], sig=(k == 3))
            mixa = read[w] = ve(lambda e, w=w, t=t: e.tensor_tensor(
                MIXT[:, 4:8, t * 128:(t + 1) * 128], bank[w][:, :].rearrange("p (k c) -> p k c", k=4),
                bc(ptcol("attn_norm_g", 0, 4).unsqueeze(2), P, 4, 128), ALU.mult), p)
        hold["H"] = p

        def project_out(kinds, marks):
            nk = len(kinds) * 4
            for i, (kind, n) in enumerate(kinds):
                wt, wm = weight(kind, n)
                for k in range(4):
                    for t in range(T):
                        for hf in range(2):
                            p = pe(lambda e, i=i, k=k, t=t, hf=hf, wt=wt: e.matmul(
                                bank[2 * t + hf][:, :], MIXT[:, 4 * i + k, t * 128:(t + 1) * 128],
                                wt[:, k, hf * 512:(hf + 1) * 512], start=(4 * i + k == 0),
                                stop=(4 * i + k == nk - 1)),
                                wm, marks[i], *(read[0:4] if i == 0 else ()), sig=(k == 3 and t == 1 and hf == 1))
                release(kind, n, p)
            return p

        def add_to_x(p, *marks):
            for b in range(4):
                xv = X[:, b // 2, (b % 2) * 512:(b % 2 + 1) * 512]
                read[b] = ve(lambda e, b=b, xv=xv: e.tensor_tensor(xv, bank[b][:, :], xv, ALU.add), p, *marks)
            return read[3]

        p = project_out([("wo", 0), ("wo", 1)], [mixp, mixa])
        xm = add_to_x(p)

        ht = rmsnorm_T(xm, "norm_ffn_g", (pe.sem, pe.n))
        ACTT = [XBCT[:, 0:4, :], XBCT[:, 4:8, :]]
        UB = [CV[:, 0:2, :], CV[:, 2:4, :]]
        actm = {}
        act_free = [hold["sq"], hold["sq"]]
        ub_free = [hold["junk"], hold["junk"]]

        def up(g, n):
            for jj in range(n):
                j = 4 * g + jj
                w = work()
                for half, kind in enumerate(("gate", "val")):
                    wt, wm = weight(kind, g)
                    for k in range(8):
                        p = pe(lambda e, w=w, half=half, wt=wt, k=k, jj=jj: e.matmul(
                            bank[w][:, half * 256:half * 256 + 256], wt[:, k, jj * 128:(jj + 1) * 128],
                            HT[:, k, :], start=(k == 0), stop=(k == 7)), ht, wm, read[w],
                            sig=(k == 7 and half == 1))
                ub = UB[j % 2]
                ms = []
                for half in range(2):
                    c = 22 * half + j
                    ms.append(sc(lambda e, w=w, half=half, ub=ub, c=c: e.activation(
                        ub[:, half, :], bank[w][:, half * 256:half * 256 + 256], ACT.Identity,
                        bias=ptcol("conv_b", c), scale=ptcol("conv_w", 88 + c)), p, ub_free[j % 2]))
                for half in range(2):
                    c = 22 * half + j
                    for tap, sh in ((1, 1), (0, 2)):
                        ms[half] = ve(lambda e, w=w, half=half, ub=ub, c=c, tap=tap, sh=sh: e.scalar_tensor_tensor(
                            out=ub[:, half, sh:256], in0=bank[w][:, half * 256:half * 256 + 256 - sh],
                            scalar=ptcol("conv_w", 44 * tap + c), in1=ub[:, half, sh:256], op0=ALU.mult,
                            op1=ALU.add), ms[1] if tap else None, ms[half])
                read[w] = ms[1]
                m = sc(lambda e, ub=ub: e.activation(ub[:, 0, :], ub[:, 0, :], ACT.Silu), ms[0])
                m = ve(lambda e, ub=ub, g=g, jj=jj: e.tensor_tensor(ACTT[g % 2][:, jj, :], ub[:, 0, :],
                                                                    ub[:, 1, :], ALU.mult), m, ms[1],
                       act_free[g % 2])
                ub_free[j % 2] = m
                actm[j] = m
            for kind in ("gate", "val"):
                release(kind, g, p)

        def down(g, n):
            wt, wm = weight("down", g)
            for jj in range(n):
                j = 4 * g + jj
                for t in range(T):
                    for hf in range(2):
                        p = pe(lambda e, g=g, jj=jj, j=j, t=t, hf=hf, wt=wt: e.matmul(
                            bank[2 * t + hf][:, :], ACTT[g % 2][:, jj, t * 128:(t + 1) * 128],
                            wt[:, jj, hf * 512:(hf + 1) * 512], start=(j == 0), stop=(j == FF - 1)),
                            wm, actm[j], *(read[0:4] if j == 0 else ()), sig=(t == 1 and hf == 1))
            act_free[g % 2] = p
            release("down", g, p)
            return p

        for g, n in groups:
            up(g, n)
            if g:
                down(g - 1, 4)
        htf = (pe.sem, pe.n)
        p = down(5, 2)
        hold["junk"] = ub_free[1]
        xm = add_to_x(p)

        def final_norm(xm):
            r = rms_rows(xm)
            for t in range(T):
                m = ve(lambda e, t=t: e.scalar_tensor_tensor(out=X[:, t, :], in0=X[:, t, :],
                                                             scalar=rs[:, t:t + 1], in1=gb[:, :],
                                                             op0=ALU.mult, op1=ALU.mult), r, ld["gb"])
            hold["ss"] = m
            return m

        xm = final_norm(xm)
        ld["gb"] = sc.dma(gsem, lambda e: e.dma_start(gb[:, :], a["norm_f_w_2"].partition_broadcast(P)), xm)

        ht = rmsnorm_T(xm, "norm1_w_2", htf)
        ubf = [[hold["junk"]] * 4]

        def conv4(kind, c, cw, cb, ntile, dst, dfree):
            wt, wm = weight(kind, c)
            last = None
            for jj in range(4):
                j = 4 * c + jj
                w = work()
                for k in range(8):
                    p = pe(lambda e, w=w, wt=wt, k=k, jj=jj: e.matmul(
                        bank[w][:, 0:256], wt[:, k, jj * 128:(jj + 1) * 128], HT[:, k, :], start=(k == 0),
                        stop=(k == 7)), ht, wm, read[w], sig=(k == 7))
                u = CV[:, j % 4, :]
                m = sc(lambda e, w=w, u=u, j=j: e.activation(u, bank[w][:, 0:256], ACT.Identity,
                                                             bias=ptcol(cb, j), scale=ptcol(cw, 3 * ntile + j)),
                       p, ubf[0][j % 4])
                for tap, sh in ((2, 1), (1, 2), (0, 3)):
                    m = ve(lambda e, w=w, u=u, j=j, tap=tap, sh=sh: e.scalar_tensor_tensor(
                        out=u[:, sh:256], in0=bank[w][:, 0:256 - sh], scalar=ptcol(cw, ntile * tap + j),
                        in1=u[:, sh:256], op0=ALU.mult, op1=ALU.add), m)
                read[w] = m
                last = sc(lambda e, u=u, j=j: e.activation(dst[:, j, :], u, ACT.Silu), m, dfree)
                f = list(ubf[0])
                f[j % 4] = last
                ubf[0] = f
            release(kind, c, p)
            return last

        for c in range(3):
            xbc = conv4("xbc", c, "ssd_conv_w_2", "ssd_conv_b_2", 12, XBCT, act_free[0])
        G = small(64).rearrange("p (t c) -> p t c", t=T)
        LE = small(64).rearrange("p (t c) -> p t c", t=T)
        for t in range(T):
            w, p = tok_major(None, None, t, ht, n=32, src=(wsm, ld["wsm"]))
            gm = read[w] = ve(lambda e, w=w, t=t: e.tensor_tensor(G[:, t, :], bank[w][:, 0:32],
                                                                  brow("ssd_dt_bias_2", 32), ALU.add), p)
        m = ve(lambda e: e.scalar_tensor_tensor(out=LE, in0=G, scalar=-1.0, in1=G, op0=ALU.mult, op1=ALU.max), gm)
        zm = []
        for c in range(2):
            for t in range(T):
                w, p = tok_major("z", c, t, ht)
                read[w] = sc(lambda e, w=w, c=c, t=t: e.activation(ZZ[:, t, c * 512:(c + 1) * 512], bank[w][:, :],
                                                                   ACT.Silu), p, t3)
                zm.append(read[w])
            release("z", c, p)
        m = sc(lambda e: e.activation(LE, LE, ACT.Exp, scale=-1.0), m)
        m = sc(lambda e: e.activation(LE, LE, ACT.Ln, bias=1.0), m)
        DTv, LF, IG = small(32).rearrange("p (t c) -> p t c", t=T), small(16).rearrange("p (t c) -> p t c", t=T), G[:, :, 16:24]
        dtm = ve(lambda e: e.scalar_tensor_tensor(out=DTv, in0=G[:, :, 0:16], scalar=0.0, in1=LE[:, :, 0:16],
                                                  op0=ALU.max, op1=ALU.add), m)
        lfm = ve(lambda e: e.scalar_tensor_tensor(out=LF, in0=G[:, :, 24:32], scalar=0.0, in1=LE[:, :, 24:32],
                                                  op0=ALU.min, op1=ALU.subtract))
        AV, ADT = small(16), small(32).rearrange("p (t c) -> p t c", t=T)
        m = sc(lambda e: e.activation(AV, brow("ssd_a_log_2", 16), ACT.Exp))
        m = ve(lambda e: e.tensor_scalar(AV, AV, -1.0, None, ALU.mult), m)
        adm = ve(lambda e: e.tensor_tensor(ADT, DTv, bc(AV.unsqueeze(1), P, T, 16), ALU.mult), m, dtm)

        xsm = None
        for t in range(T):
            for b in range(2):
                w = work()
                for k in range(4):
                    p = pe(lambda e, w=w, k=k, b=b, t=t: e.transpose(
                        bank[w][:, k * 128:(k + 1) * 128], XBCT[:, 4 * b + k, t * 128:(t + 1) * 128], ident),
                        xbc, read[w], sig=(k == 3))
                xsm = read[w] = sc(lambda e, w=w, b=b, t=t: e.activation(XS[:, t, b * 512:(b + 1) * 512],
                                                                         bank[w][:, :], ACT.Copy), p)
        XDT = H
        for t in range(T):
            xd = ve(lambda e, t=t: e.tensor_tensor(
                XDT[:, t, :].rearrange("p (h c) -> p h c", h=16), XS[:, t, :].rearrange("p (h c) -> p h c", h=16),
                bc(DTv[:, t, :].unsqueeze(2), P, 16, 64), ALU.mult), xsm, dtm, hold["H"])
        for t in range(T):
            xsd = po(lambda e, t=t: e.tensor_tensor(
                XS[:, t, :].rearrange("p (h c) -> p h c", h=16), XS[:, t, :].rearrange("p (h c) -> p h c", h=16),
                bc(brow("ssd_d_2", 16).unsqueeze(2), P, 16, 64), ALU.mult), xd, xsm)
        CB = MIXT[:, 8:12, :].rearrange("p a b -> p (a b)")
        cbm = None
        for g in range(2):
            w = work()
            bt, ct = XBCT[:, 8 + g, :], XBCT[:, 10 + g, :]
            pe(lambda e, w=w, bt=bt, ct=ct: e.matmul(bank[w][:, 0:256], bt[:, 0:128], ct, start=True, stop=True),
               xbc, read[w], sig=False)
            p = pe(lambda e, w=w, bt=bt, ct=ct: e.matmul(bank[w][:, 256:384], bt[:, 128:256], ct[:, 128:256],
                                                         start=True, stop=True))
            cbm = read[w] = ve(lambda e, w=w, g=g: e.tensor_tensor(CB[:, g * 384:(g + 1) * 384],
                                                                   bank[w][:, 0:384], const("ux", 384),
                                                                   ALU.mult), p)
        xbct_free = p

        slt = const("slt", 128)
        LA = [QKT[:, 2 * i:2 * i + 2, :].rearrange("p a b -> p (a b)") for i in range(2)]
        EE = [QKT[:, 4 + 2 * i:6 + 2 * i, :].rearrange("p a b -> p (a b)") for i in range(2)]
        WW = [QKT[:, 8 + 2 * i:10 + 2 * i, :].rearrange("p a b -> p (a b)") for i in range(2)]
        la_free, ww_free, ee_free = [mixp] * 2, [None] * 2, [None] * 2
        ux = const("ux", 384)
        for h in range(16):
            i = h % 2
            la = LA[i]
            for t in range(T):
                lam_ = ve(lambda e, la=la, t=t, h=h: e.tensor_scalar(la[:, t * 128:(t + 1) * 128], slt,
                                                                     ADT[:, t, h:h + 1], None, ALU.mult), adm,
                          la_free[i])
            lam_ = ve(lambda e, la=la, h=h: e.tensor_scalar(la[:, 256:384], ux[:, 128:256], ADT[:, 1, h:h + 1],
                                                            None, ALU.mult))
            w = work()
            pe(lambda e, w=w, la=la: e.matmul(bank[w][:, 0:256], la[:, 0:128], ux[:, 0:256], start=True,
                                              stop=False), lam_, read[w], sig=False)
            pe(lambda e, w=w, la=la: e.matmul(bank[w][:, 128:256], la[:, 256:384], ux[:, 0:128], start=False,
                                              stop=True), sig=False)
            p = pe(lambda e, w=w, la=la: e.matmul(bank[w][:, 256:384], la[:, 128:256], ux[:, 0:128], start=True,
                                                  stop=True))
            la_free[i] = p
            em_ = read[w] = sc(lambda e, w=w, i=i: e.activation(EE[i][:, 0:384], bank[w][:, 0:384], ACT.Exp), p,
                               ee_free[i])
            g = h // 8
            wm_ = ve(lambda e, i=i, g=g: e.tensor_tensor(WW[i][:, 0:384], EE[i][:, 0:384],
                                                         CB[:, g * 384:(g + 1) * 384], ALU.mult), em_, cbm,
                     ww_free[i])
            ee_free[i] = wm_
            hb, hc = h // 8, (h % 8) * 64
            xd0, xd1 = XDT[:, 0, h * 64:(h + 1) * 64], XDT[:, 1, h * 64:(h + 1) * 64]
            pe(lambda e, i=i, hb=hb, hc=hc, xd0=xd0: e.matmul(bank[hb][:, hc:hc + 64], WW[i][:, 0:128], xd0,
                                                              start=True, stop=True), wm_, xd, *read[0:4],
               sig=False)
            pe(lambda e, i=i, hb=hb, hc=hc, xd0=xd0: e.matmul(bank[2 + hb][:, hc:hc + 64], WW[i][:, 128:256],
                                                              xd0, start=True, stop=False), sig=False)
            ww_free[i] = pe(lambda e, i=i, hb=hb, hc=hc, xd1=xd1: e.matmul(
                bank[2 + hb][:, hc:hc + 64], WW[i][:, 256:384], xd1, start=False, stop=True))
        yp = ww_free[1]
        gss, grs = small(4), small(4)
        YG = XS
        gmk = []
        for b in range(4):
            t, g = b // 2, b % 2
            yv, zv = YG[:, t, g * 512:(g + 1) * 512], ZZ[:, t, g * 512:(g + 1) * 512]
            m = read[b] = ve(lambda e, b=b, yv=yv: e.tensor_tensor(yv, bank[b][:, :], yv, ALU.add), yp, xsd)
            m = ve(lambda e, yv=yv, zv=zv: e.tensor_tensor(yv, yv, zv, ALU.mult), m, zm[3])
            hold["junk"] = sc(lambda e, b=b, yv=yv: e.activation(junk[:, 0:512], yv, ACT.Square,
                                                                 accum_out=gss[:, b:b + 1]), m, hold["junk"],
                              *ubf[0])
        m = rstd(grs, gss, 512, hold["junk"])
        for b in range(4):
            t, g = b // 2, b % 2
            yv = YG[:, t, g * 512:(g + 1) * 512]
            gmk.append(ve(lambda e, b=b, yv=yv: e.tensor_scalar(yv, yv, grs[:, b:b + 1], None, ALU.mult), m))
        mix0 = to_columns(YG, [gmk[1], gmk[3]], 0, "ssd_norm_w_2", MIXT, yp)
        xs_free = (pe.sem, pe.n)
        ubf[0] = [hold["junk"]] * 4

        for c in range(4):
            qk = conv4("qk", c, "ml_conv_w_2", "ml_conv_b_2", 16, QKT, yp)
        vmm = []
        for c in range(2):
            for t in range(T):
                w, p = tok_major("v", c, t, ht)
                read[w] = ve(lambda e, w=w, c=c, t=t: e.tensor_copy(VV[:, t, c * 512:(c + 1) * 512],
                                                                    bank[w][:, :]), p)
                vmm.append(read[w])
            release("v", c, p)
        OG = ZZ
        ogm = None
        for c in range(2):
            for t in range(T):
                w, p = tok_major("o", c, t, ht)
                ogm = read[w] = sc(lambda e, w=w, c=c, t=t: e.activation(OG[:, t, c * 512:(c + 1) * 512],
                                                                         bank[w][:, :], ACT.Sigmoid), p, gmk[3])
            release("o", c, p)

        flat = XBCT[:, :, :].rearrange("p a b -> p (a b)")
        RR = [flat[:, i * 384:(i + 1) * 384] for i in range(2)]
        DD = [flat[:, 768 + i * 384:768 + (i + 1) * 384] for i in range(2)]
        SQ = [flat[:, 1536 + i * 384:1536 + (i + 1) * 384] for i in range(2)]
        ST = [flat[:, 2304 + i * 384:2304 + (i + 1) * 384] for i in range(2)]
        mmx = small(16).rearrange("p (t h) -> p t h", t=T)
        nmx = small(16).rearrange("p (t h) -> p t h", t=T)
        den = small(16).rearrange("p (t h) -> p t h", t=T)
        rr_free, dd_free, sq_free, st_free = [xbct_free] * 2, [xbct_free] * 2, [xbct_free] * 2, [xbct_free] * 2
        KS = 128 ** -0.5
        for h in range(8):
            i = h % 2
            R, DDi, SQi, STi = RR[i], DD[i], SQ[i], ST[i]
            for t in range(T):
                m = ve(lambda e, R=R, t=t, h=h: e.tensor_scalar(R[:, t * 128:(t + 1) * 128], slt,
                                                                LF[:, t, h:h + 1], None, ALU.mult), lfm,
                       rr_free[i])
                rm = ve(lambda e, R=R, t=t, h=h: e.scalar_tensor_tensor(
                    out=R[:, t * 128:(t + 1) * 128], in0=ident, scalar=IG[:, t, h:h + 1],
                    in1=R[:, t * 128:(t + 1) * 128], op0=ALU.mult, op1=ALU.add), m)
            rm = ve(lambda e, R=R, h=h: e.tensor_scalar(R[:, 256:384], ux[:, 128:256], LF[:, 1, h:h + 1], None,
                                                        ALU.mult))
            w = work()
            pe(lambda e, w=w, R=R: e.matmul(bank[w][:, 0:128], ux[:, 0:128], R[:, 0:128], start=True, stop=True),
               rm, read[w], sig=False)
            pe(lambda e, w=w, R=R: e.matmul(bank[w][:, 128:256], ux[:, 128:256], R[:, 0:128], start=True,
                                            stop=False), sig=False)
            pe(lambda e, w=w, R=R: e.matmul(bank[w][:, 128:256], ux[:, 0:128], R[:, 256:384], start=False,
                                            stop=True), sig=False)
            p = pe(lambda e, w=w, R=R: e.matmul(bank[w][:, 256:384], ux[:, 0:128], R[:, 128:256], start=True,
                                                stop=True))
            rr_free[i] = p
            m = read[w] = ve(lambda e, w=w, DDi=DDi: e.tensor_tensor(DDi, bank[w][:, 0:384], const("neg", 384),
                                                                     ALU.add), p, dd_free[i])
            ve(lambda e, DDi=DDi, h=h: e.reduce_max(mmx[:, 0, h:h + 1], DDi[:, 0:128], AX), m)
            m = ve(lambda e, DDi=DDi, h=h: e.reduce_max(mmx[:, 1, h:h + 1], DDi[:, 128:384], AX))
            m = ve(lambda e, h=h: e.tensor_scalar(nmx[:, :, h:h + 1], mmx[:, :, h:h + 1], -1.0, None, ALU.mult), m)
            for t, (c0, c1) in enumerate(((0, 128), (128, 384))):
                em_ = sc(lambda e, DDi=DDi, t=t, h=h, c0=c0, c1=c1: e.activation(
                    DDi[:, c0:c1], DDi[:, c0:c1], ACT.Exp, bias=nmx[:, t, h:h + 1]), m)
            w = work()
            q, k = QKT[:, h, :], QKT[:, 8 + h, :]
            pe(lambda e, w=w, q=q, k=k: e.matmul(bank[w][:, 0:128], q[:, 0:128], k[:, 0:128], start=True,
                                                 stop=True), qk, read[w], sig=False)
            p = pe(lambda e, w=w, q=q, k=k: e.matmul(bank[w][:, 128:384], q[:, 128:256], k, start=True,
                                                     stop=True))
            for t, (c0, c1) in enumerate(((0, 128), (128, 384))):
                sm_ = ve(lambda e, w=w, SQi=SQi, DDi=DDi, t=t, h=h, c0=c0, c1=c1: e.tensor_tensor_reduce(
                    SQi[:, c0:c1], bank[w][:, c0:c1], DDi[:, c0:c1], KS, 0.0, ALU.mult, ALU.add,
                    den[:, t, h:h + 1]), p, em_, sq_free[i])
            read[w] = dd_free[i] = sm_
            w = work()
            for j in range(3):
                p = pe(lambda e, w=w, j=j, SQi=SQi: e.transpose(bank[w][:, j * 128:(j + 1) * 128],
                                                                SQi[:, j * 128:(j + 1) * 128], ident), sm_,
                       read[w], sig=(j == 2))
            sq_free[i] = p
            am = read[w] = sc(lambda e, w=w, STi=STi: e.activation(STi, bank[w][:, 0:384], ACT.Copy), p,
                              st_free[i])
            hb, hc = h // 4, (h % 4) * 128
            v0, v1 = VV[:, 0, h * 128:(h + 1) * 128], VV[:, 1, h * 128:(h + 1) * 128]
            pe(lambda e, STi=STi, hb=hb, hc=hc, v0=v0: e.matmul(bank[hb][:, hc:hc + 128], STi[:, 0:128], v0,
                                                                start=True, stop=True), am, *vmm, *read[0:4],
               sig=False)
            pe(lambda e, STi=STi, hb=hb, hc=hc, v0=v0: e.matmul(bank[2 + hb][:, hc:hc + 128], STi[:, 128:256],
                                                                v0, start=True, stop=False), sig=False)
            st_free[i] = pe(lambda e, STi=STi, hb=hb, hc=hc, v1=v1: e.matmul(
                bank[2 + hb][:, hc:hc + 128], STi[:, 256:384], v1, start=False, stop=True))
        yp = st_free[1]
        em_ = sc(lambda e: e.activation(nmx, nmx, ACT.Exp))
        m = ve(lambda e: e.scalar_tensor_tensor(out=den, in0=den, scalar=-1.0, in1=den, op0=ALU.mult, op1=ALU.max), sm_)
        m = ve(lambda e: e.tensor_tensor(den, den, nmx, ALU.max), m, em_)
        m = ve(lambda e: e.reciprocal(den, den), m)
        mu = small(16).rearrange("p (b h) -> p b h", b=4)
        va = small(16).rearrange("p (b h) -> p b h", b=4)
        YM = XS
        ymk = []
        jv = junk[:, 0:512].rearrange("p (h c) -> p h c", h=4)
        for b in range(4):
            t, g = b // 2, b % 2
            yv = YM[:, t, g * 512:(g + 1) * 512].rearrange("p (h c) -> p h c", h=4)
            ov = OG[:, t, g * 512:(g + 1) * 512].rearrange("p (h c) -> p h c", h=4)
            bv = bank[b][:, :].rearrange("p (h c) -> p h c", h=4)
            m2 = read[b] = ve(lambda e, yv=yv, bv=bv, t=t, g=g: e.tensor_tensor(
                yv, bv, bc(den[:, t, 4 * g:4 * g + 4].unsqueeze(2), P, 4, 128), ALU.mult), m, yp, xs_free)
            m2 = ve(lambda e, yv=yv, b=b: e.reduce_sum(mu[:, b, :], yv, AX), m2)
            m2 = ve(lambda e, b=b: e.tensor_scalar(mu[:, b, :], mu[:, b, :], 1.0 / 128, None, ALU.mult), m2)
            m2 = ve(lambda e, yv=yv, b=b: e.tensor_tensor(yv, yv, bc(mu[:, b, :].unsqueeze(2), P, 4, 128),
                                                          ALU.subtract), m2)
            m3 = sc(lambda e, yv=yv: e.activation(jv, yv, ACT.Square), m2, hold["junk"], *ubf[0])
            m3 = ve(lambda e, b=b: e.reduce_sum(va[:, b, :], jv, AX), m3)
            hold["junk"] = m3
            m3 = rstd(va[:, b, :], va[:, b, :], 128, m3)
            m3 = ve(lambda e, yv=yv, b=b: e.tensor_tensor(yv, yv, bc(va[:, b, :].unsqueeze(2), P, 4, 128),
                                                          ALU.mult), m3)
            ymk.append(ve(lambda e, yv=yv, ov=ov: e.tensor_tensor(yv, yv, ov, ALU.mult), m3, ogm))
        mix1 = to_columns(YM, [ymk[1], ymk[3]], 8, "ml_norm_w_2", MIXT, yp)
        p = project_out([("wout", k) for k in range(4)], [mix0, mix0, mix1, mix1])
        xm = add_to_x(p)

        hold["H"] = yp
        ht = rmsnorm_T(xm, "norm2_w_2", (pe.sem, pe.n))
        L = small(72).rearrange("p (t c) -> p t c", t=T)
        for t in range(T):
            w, p = tok_major(None, None, t, ht, n=36, src=(wrt, ld["wrt"]))
            lmk = read[w] = ve(lambda e, w=w, t=t: e.tensor_tensor(L[:, t, :], bank[w][:, 0:36],
                                                                   brow("router_g_b_2", 36), ALU.add), p)
        smat[0] = 8
        gmx, gsum, gid = small(2), small(2), small(2)
        ge = small(8).rearrange("p (t c) -> p t c", t=T)
        assert smat[0] < 120
        RB = CV[:, :, :].rearrange("p a b -> p (a b)")
        at_ = [0]

        def rb(n):
            v = RB[:, at_[0]:at_[0] + T * n].rearrange("p (t c) -> p t c", t=T)
            at_[0] += T * n
            return v

        def bt(v, n):
            return bc(v.unsqueeze(2), P, T, n)

        free0 = [hold["junk"]]

        def top1(vals, n, iota, mval, onehot, *marks):
            eq, idx = rb(n), rb(1)
            m = ve(lambda e: e.reduce_max(mval, vals, AX), *marks)
            m = ve(lambda e: e.tensor_tensor(eq, vals, bt(mval, n), ALU.is_ge), m, *free0)
            m = ve(lambda e: e.scalar_tensor_tensor(out=eq, in0=eq, scalar=-100.0, in1=bc(iota.unsqueeze(1), P, T, n),
                                                    op0=ALU.mult, op1=ALU.add), m)
            m = ve(lambda e: e.tensor_reduce(idx[:, :, 0], eq, AX, ALU.min), m)
            return ve(lambda e: e.tensor_tensor(onehot, eq, bt(idx[:, :, 0], n), ALU.is_equal), m)

        goh, oh1, oh2, el, ge2 = rb(4), rb(32), rb(32), rb(32), rb(4)
        m1_, m2_, dm, g1, g2, pg = (small(2) for _ in range(6))
        m = top1(L[:, :, 0:4], 4, const("iota", 4), gmx, goh, lmk)
        gm1 = ve(lambda e: e.tensor_tensor(ge2, L[:, :, 0:4], bt(gmx, 4), ALU.subtract), m)
        gm1 = sc(lambda e: e.activation(ge2, ge2, ACT.Exp), gm1)
        m = ve(lambda e: e.tensor_scalar(goh, goh, 1.0, 1e30, ALU.subtract, ALU.mult), m)
        for t in range(T):
            m = ve(lambda e, t=t: e.tensor_tensor(el[:, t, :].rearrange("p (g c) -> p g c", g=4),
                                                  L[:, t, 4:36].rearrange("p (g c) -> p g c", g=4),
                                                  bc(goh[:, t, :].unsqueeze(2), P, 4, 8), ALU.add), m)
        m = top1(el, 32, const("iota", 32, 4), m1_, oh1, m)
        m = ve(lambda e: e.scalar_tensor_tensor(out=el, in0=oh1, scalar=-2e30, in1=el, op0=ALU.mult,
                                                op1=ALU.add), m)
        m = top1(el, 32, const("iota", 32, 4), m2_, oh2, m)
        m = ve(lambda e: e.tensor_tensor(dm, m2_, m1_, ALU.subtract), m)
        m = sc(lambda e: e.activation(dm, dm, ACT.Exp), m)
        mg = ve(lambda e: e.reduce_sum(gsum, ge2, AX), gm1)
        m = ve(lambda e: e.tensor_scalar(g1, dm, 1.0, None, ALU.add), m)
        m = ve(lambda e: e.tensor_tensor(g1, g1, gsum, ALU.mult), m, mg)
        m = ve(lambda e: e.reciprocal(g1, g1), m)
        m = ve(lambda e: e.tensor_tensor(g2, g1, dm, ALU.mult), m)
        GT = rb(32)
        m = ve(lambda e: e.tensor_tensor(oh1, oh1, bt(g1, 32), ALU.mult), m)
        m = ve(lambda e: e.tensor_tensor(oh2, oh2, bt(g2, 32), ALU.mult), m)
        gtm = ve(lambda e: e.tensor_tensor(GT, oh1, oh2, ALU.add), m)
        assert at_[0] <= 1024

        GB = [VV[:, 0, i * 256:(i + 1) * 256] for i in range(2)]
        SG = [ZZ[:, 0, i * 256:(i + 1) * 256] for i in range(2)]
        HID = [XBCT[:, 0:4, :], XBCT[:, 4:8, :]]
        gb_free, sg_free = [ogm, ogm], [ymk[3]] * 2
        hid_free = [yp, yp]
        hidm = {}

        def e_up(x):
            i = x % 2
            w = work()
            for t in range(T):
                p = pe(lambda e, w=w, t=t, x=x: e.matmul(bank[w][:, t * 128:(t + 1) * 128],
                                                         bc(GT[:, t, x:x + 1], P, 128), ident, start=True,
                                                         stop=True), gtm, read[w], sig=(t == 1))
            gbm = read[w] = sc(lambda e, w=w, i=i: e.activation(GB[i], bank[w][:, 0:256], ACT.Copy), p,
                               gb_free[i], yp)
            wg, wgm = weight("eg", x)
            wu, wum = weight("eu", x)
            for f in range(4):
                w = work()
                for half, wt in enumerate((wg, wu)):
                    for k in range(8):
                        p = pe(lambda e, w=w, half=half, wt=wt, k=k, f=f: e.matmul(
                            bank[w][:, half * 256:half * 256 + 256], wt[:, k, f * 128:(f + 1) * 128], HT[:, k, :],
                            start=(k == 0), stop=(k == 7)), ht, wgm, wum, read[w], sig=(k == 7 and half == 1))
                sg = SG[f % 2]
                m = sc(lambda e, w=w, sg=sg: e.activation(sg, bank[w][:, 0:256], ACT.Silu), p, sg_free[f % 2])
                m = ve(lambda e, sg=sg, i=i: e.tensor_tensor(sg, sg, GB[i], ALU.mult), m, gbm)
                m = ve(lambda e, w=w, sg=sg, i=i, f=f: e.tensor_tensor(HID[i][:, f, :], sg,
                                                                       bank[w][:, 256:512], ALU.mult), m,
                       hid_free[i])
                read[w] = sg_free[f % 2] = hidm[(x, f)] = m
            gb_free[i] = m
            release("eg", x, p)
            release("eu", x, p)

        def e_down(x):
            wt, wm = weight("ed", x)
            for f in range(4):
                for t in range(T):
                    for hf in range(2):
                        p = pe(lambda e, x=x, f=f, t=t, hf=hf, wt=wt: e.matmul(
                            bank[2 * t + hf][:, :], HID[x % 2][:, f, t * 128:(t + 1) * 128],
                            wt[:, f, hf * 512:(hf + 1) * 512], start=(x == 0 and f == 0),
                            stop=(x == NE - 1 and f == 3)),
                            wm, hidm[(x, f)], *(read[0:4] if x == 0 else ()), sig=(t == 1 and hf == 1))
            hid_free[x % 2] = p
            release("ed", x, p)
            return p

        for x in range(NE):
            e_up(x)
            p = e_down(x)
        xm = add_to_x(p)
        m = final_norm(xm)
        osem = dsem("s_out")
        om = sy.dma(osem, lambda e: e.dma_start(out.rearrange("(t p) d -> p t d", p=P), X[:, :, :]), m)
        sy.wait(om)

        block = ctx.enter_context(nc.Block())

        @block.sync
        def _(e):
            sy.run(e)

        @block.scalar
        def _(e):
            sc.run(e)

        @block.vector
        def _(e):
            ve.run(e)

        @block.gpsimd
        def _(e):
            po.run(e)

        @block.tensor
        def _(e):
            pe.run(e)


def kernel(**inputs):
    from concourse import bacc
    from concourse.bass_utils import run_bass_kernel_spmd

    f = {n: np.asarray(v) for n, v in inputs.items()}
    cn, pool_a = constants()
    w2 = f["w_in_2"][0]

    def ktile(w):
        return np.ascontiguousarray(w.reshape(8, P, w.shape[1]).transpose(1, 0, 2))

    arrays = {
        "x": f["x"][0], "positions": np.ascontiguousarray(f["positions"][0].reshape(T, P).T), "cn": cn, "pool_a": pool_a,
        "pt": np.ascontiguousarray(np.concatenate([f[n].reshape(k, P) for n, k in PT_ROWS]).T),
        "br": np.concatenate([f[n].reshape(k) for n, k in BR_ROWS]),
        "wsm": ktile(np.concatenate([w2[:, 2560:2576], w2[:, 6672:6688]], 1)),
        "wrt": ktile(np.concatenate([f["router_g_w_2"][0], f["router_e_w_2"][0]], 1)),
        "norm_final_g": f["norm_final_g"], "norm_f_w_2": f["norm_f_w_2"],
    }
    for n in ("w_in", "pool_w", "w_o", "w_up", "w_down", "w_in_2", "w_out_2", "exp_w_gate_2", "exp_w_up_2",
              "exp_w_down_2"):
        arrays[n] = f[n][0]
    nc = bacc.Bacc("TRN2", target_bir_lowering=False, num_devices=1)
    a, fed = {}, {}
    for n, v in arrays.items():
        fed[f"in_{n}"] = v
        a[n] = nc.dram_tensor(f"in_{n}", v.shape, mybir.dt.from_np(v.dtype), kind="ExternalInput").ap()
    out = nc.dram_tensor("out", (S, D), F32, kind="ExternalOutput").ap()
    build(nc, a, out)
    r = run_bass_kernel_spmd(nc, [fed], core_ids=[0])
    return np.asarray(r.results[0]["out"]).reshape(1, S, D)
```

```python
from contextlib import ExitStack

import numpy as np

import concourse.bass as bass
from concourse import mybir

P = 128
T = 2
S = 256
D = 1024
ALU = mybir.AluOpType
ACT = mybir.ActivationFunctionType
F32 = mybir.dt.float32
F32R = mybir.dt.float32r
I32 = mybir.dt.int32
AX = mybir.AxisListType.X
EPS = 1e-6
NEG = -1e30
FF = 22
NE = 32
RAW = 5
HL = 3
PC = 2048
FILL = ((4, 0, 0), (4, 0, 1), (6, 1, 0), (7, 1, 1))
UNITS = 35

PT_ROWS = [("norm_mix_g", 8), ("pool_scale", 4), ("attn_norm_g", 4), ("norm_ffn_g", 8), ("conv_w", 132),
           ("conv_b", 44), ("norm1_w_2", 8), ("ssd_conv_w_2", 48), ("ssd_conv_b_2", 12), ("ssd_norm_w_2", 8),
           ("ml_conv_w_2", 64), ("ml_conv_b_2", 16), ("ml_norm_w_2", 8), ("norm2_w_2", 8)]
PT = {}
_at = 0
for _n, _k in PT_ROWS:
    PT[_n] = _at
    _at += _k
NPT = _at
BR_ROWS = [("lambda_q1", 64), ("lambda_k1", 64), ("lambda_q2", 64), ("lambda_k2", 64), ("ssd_dt_bias_2", 16),
           ("ml_i_bias_2", 8), ("ml_f_bias_2", 8), ("ssd_a_log_2", 16), ("ssd_d_2", 16), ("router_g_b_2", 4),
           ("router_e_b_2", 32)]
BR = {}
_at = 0
for _n, _k in BR_ROWS:
    BR[_n] = _at
    _at += _k
NBR = _at
CN_COLS = [("ident", 128), ("ux", 384), ("slt", 128), ("neg", 384), ("chm", 384), ("invf", 32), ("iota", 36), ("mh", 8), ("lo", 4), ("hi", 4),
           ("up1", 1), ("slot", 4), ("ecode", 128), ("tcode", 128)]
CN = {}
_at = 0
for _n, _k in CN_COLS:
    CN[_n] = _at
    _at += _k
NCN = _at


def inv_freq():
    exact = 10000.0 ** (-np.arange(0, 64, 2, dtype=np.float64) / 64)
    return exact.astype(np.float32)


def constants():
    c = np.zeros((P, NCN), np.float32)
    i = np.arange(P)
    tri = (i[:, None] <= i[None, :]).astype(np.float32)
    c[:, CN["ident"]:CN["ident"] + 128] = np.eye(P)
    c[:, CN["ux"]:CN["ux"] + 384] = np.concatenate([tri, np.ones((P, P)), tri], 1)
    c[:, CN["slt"]:CN["slt"] + 128] = i[:, None] > i[None, :]
    neg = np.where(i[None, :] > i[:, None], NEG, 0.0)
    c[:, CN["neg"]:CN["neg"] + 384] = np.concatenate([neg, 0 * neg, neg], 1)
    chm = np.where(i[None, :] // 64 > i[:, None] // 64, NEG, 0.0)
    c[:, CN["chm"]:CN["chm"] + 384] = np.concatenate([chm, 0 * chm, chm], 1)
    c[:, CN["invf"]:CN["invf"] + 32] = inv_freq()[None]
    c[:, CN["iota"]:CN["iota"] + 4] = 100 + np.arange(4)
    c[:, CN["iota"] + 4:CN["iota"] + 36] = 100 + np.arange(32)
    c[:, CN["mh"]:CN["mh"] + 8] = -0.5
    c[:, CN["lo"]:CN["lo"] + 4] = 128 * np.arange(4)
    c[:, CN["hi"]:CN["hi"] + 4] = 128 * np.arange(4) + 128
    c[:, CN["up1"]] = i + 1
    c[:, CN["slot"]:CN["slot"] + 4] = 128 * np.arange(4)[None] + i[:, None]
    c[:, CN["ecode"]:CN["ecode"] + 128] = i[None] // 4
    c[:, CN["tcode"]:CN["tcode"] + 128] = i[None] % 4
    pool = np.zeros((P, 4, 384), np.float32)
    t = np.arange(S)
    for g, w in enumerate((2, 4, 8, 16)):
        count = np.minimum(t + 1, w).astype(np.float32)
        a = ((t[:, None] <= t[None, :]) & (t[:, None] > t[None, :] - w)) / count[None, :] - np.eye(S)
        pool[:, g, 0:256] = a[0:128]
        pool[:, g, 256:384] = a[128:256, 128:256]
    return c, pool.reshape(P, 1536)


class Engine:

    def __init__(self, sem):
        self.sem, self.n, self.ops, self.seen = sem, 0, [], {}

    def wait(self, *marks):
        for m in marks:
            if m is None:
                continue
            s, v = m
            if self.seen.get(id(s), 0) < v:
                self.seen[id(s)] = v
                self.ops.append(lambda e, s=s, v=v: e.wait_ge(s, v))

    def __call__(self, fn, *marks, sig=True):
        self.wait(*marks)
        if not sig:
            self.ops.append(fn)
            return None
        self.n += 1
        s = self.sem
        self.ops.append(lambda e: fn(e).then_inc(s, 1))
        return s, self.n

    def dma(self, sem, fn, *marks):
        self.wait(*marks)
        sem[1] += 16
        s = sem[0]
        self.ops.append(lambda e: fn(e).then_inc(s, 16))
        return s, sem[1]

    def mark(self):
        return self.sem, self.n

    def do(self, fn):
        self.ops.append(fn)

    def run(self, e):
        for op in self.ops:
            op(e)


def bc(ap, *shape):
    return ap.broadcast_to(list(shape))


def build(nc, a, out):
    ctx = ExitStack()
    with ctx:
        def sb(name, *shape, dt=F32):
            return ctx.enter_context(nc.sbuf_tensor(name, [P, *shape], dt))

        def sem(name):
            return ctx.enter_context(nc.semaphore(name))

        def dsem(name):
            return [sem(name), 0]

        raw = [sb(f"raw{i}", PC) for i in range(RAW)]
        WH = [sb(f"WH{i}", PC, dt=F32R) for i in range(HL)]
        WL = [sb(f"WL{i}", PC, dt=F32R) for i in range(HL)]
        HTH, HTL = sb("HTH", 8, S, dt=F32R), sb("HTL", 8, S, dt=F32R)
        MXH, MXL = sb("MXH", 8, S, dt=F32R), sb("MXL", 8, S, dt=F32R)
        wsh, wsl = sb("wsh", 288, dt=F32R), sb("wsl", 288, dt=F32R)
        cn = sb("cn", NCN)
        pt = sb("pt", NPT)
        br = sb("br", NBR)
        X = sb("X", T, D)
        H = sb("H", T, D)
        TMP = sb("TMP", 2, 512)
        CV = sb("CV", 4, S)
        sm = sb("sm", 400)
        BIG = sb("BIG", 11264)
        bank = [ctx.enter_context(nc.psum_tensor(f"bank{i}", [P, 512], F32)) for i in range(8)]

        def big(at, *shape):
            n = int(np.prod(shape))
            v = BIG[:, at:at + n]
            if len(shape) == 2:
                v = v.rearrange("p (a b) -> p a b", a=shape[0])
            return v

        ZZ, XBCT, XS, VV = big(0, T, D), big(2048, 12, S), big(5120, T, D), big(7168, T, D)
        QKT = big(9216, 8, S)
        cvf = CV[:, :, :].rearrange("p a b -> p (a b)")

        def const(name, n, at=0):
            return cn[:, CN[name] + at:CN[name] + at + n]

        ident = const("ident", 128)
        pe, ve, sc, po, sy = (Engine(sem(n)) for n in ("s_pe", "s_ve", "s_sc", "s_po", "s_sy"))
        rsem = [dsem(f"s_raw{i}") for i in range(RAW)]

        st = {"stream": [], "loaded": {}, "rawfree": {}, "split": {}, "hlfree": {}, "nxt": 0, "cur": 0}

        def pump():
            while st["nxt"] < len(st["stream"]):
                i = st["nxt"]
                if i >= RAW and i - RAW not in st["rawfree"]:
                    return
                src = st["stream"][i]
                dst = raw[i % RAW][:, :]
                st["loaded"][i] = sy.dma(rsem[i % RAW], lambda e, dst=dst, src=src: e.dma_start(
                    dst.rearrange("p (k n) -> p k n", k=src().shape[1]), src()), st["rawfree"].get(i - RAW))
                st["nxt"] += 1

        def add(src):
            st["stream"].append(src if callable(src) else lambda: src)

        def split_to(i):
            while len(st["split"]) <= min(i, len(st["stream"]) - 1):
                j = len(st["split"])
                pump()
                r, h, l = raw[j % RAW][:, :], WH[j % HL], WL[j % HL]
                m = sc(lambda e, r=r, h=h: e.activation(h[:, :], r, ACT.Copy), st["loaded"][j],
                       st["hlfree"].get(j - HL))
                m = ve(lambda e, r=r, h=h, l=l: e.tensor_tensor(l[:, :], r, h[:, :].bitcast(F32), ALU.subtract), m,
                       st["loaded"][j], st["hlfree"].get(j - HL))
                st["split"][j] = m
                st["rawfree"][j] = m
                pump()

        def take():
            i = st["cur"]
            st["cur"] += 1
            split_to(i)
            return i, WH[i % HL], WL[i % HL], st["split"][i]

        def done(i, mark, ahead=2):
            st["hlfree"][i] = mark
            split_to(i + ahead)

        def kpiece(w, k0, nk, c0, n):
            return w[k0 * 128:(k0 + nk) * 128, c0:c0 + n].rearrange("(k p) n -> p k n", p=P)

        for c in (1, 2, 3, 0):
            for kh in range(2):
                add(kpiece(a["w_in"], 4 * kh, 4, c * 512, 512))
        for kh in range(2):
            for c in range(2):
                add(kpiece(a["w_o"], 4 * kh, 4, c * 512, 512))
        NG = FF // 2
        for g in range(NG):
            add(kpiece(a["w_up"], 0, 8, g * 256, 256))
            add(kpiece(a["w_up"], 0, 8, 2816 + g * 256, 256))
            if g:
                add(kpiece(a["w_down"], 2 * g - 2, 2, 0, D))
        add(kpiece(a["w_down"], 2 * NG - 2, 2, 0, D))
        W2 = a["w_in_2"]
        for c in range(6):
            add(kpiece(W2, 0, 8, 1024 + 256 * c, 256))
        for c in range(2):
            for kh in range(2):
                add(kpiece(W2, 4 * kh, 4, 512 * c, 512))
        for c0 in (4624, 5136, 5648, 6160):
            for kh in range(2):
                add(kpiece(W2, 4 * kh, 4, c0, 512))
        for h in range(-2, 8):
            if h < 6:
                add(kpiece(W2, 0, 8, (2576 if h % 2 == 0 else 3600) + 256 * (h // 2 + 1), 256))
            for at_h, job, step in FILL:
                if at_h == h:
                    add(kpiece(a["w_out_2"], 4 * step, 4, job * 512, 512))
        for c in range(2):
            for kh in range(2):
                add(kpiece(a["w_out_2"], 8 + 4 * kh, 4, c * 512, 512))

        read = [None] * 8
        turn = [0, 0]

        def work(pool=(4, 5, 6, 7), which=0):
            b = pool[turn[which] % len(pool)]
            turn[which] += 1
            return b

        ld = {}

        def load(name, dst, src, *marks, eng=None):
            ld[name] = (eng or sc).dma(dsem(f"s_ld_{name}"), lambda e: e.dma_start(dst, src), *marks)

        load("x", X[:, :, :], a["x"].rearrange("(t p) d -> p t d", p=P))
        load("cn", cn[:, :], a["cn"])
        load("pt", pt[:, :], a["pt"])
        load("pos", sm[:, 0:2].bitcast(I32), a["positions"])
        pump()
        pool_a = BIG[:, 9216:10752]
        pool_w = BIG[:, 10752:11264].rearrange("p (g c) -> p g c", g=4)
        load("br", br[:, :], a["br"].partition_broadcast(P))
        load("pa", pool_a, a["pool_a"])
        load("pw", pool_w, a["pool_w"].rearrange("g c d -> c g d"))

        smat = [2]

        def small(n):
            v = sm[:, smat[0]:smat[0] + n]
            smat[0] += n
            assert smat[0] <= 400
            return v

        def ptcol(name, i=0, n=1):
            return pt[:, PT[name] + i:PT[name] + i + n]

        def brow(name, n):
            return br[:, BR[name]:BR[name] + n]

        ss, rs = small(2), small(2)
        hold = {}

        def rstd(dst, src, n, *marks):
            m = ve(lambda e: e.tensor_scalar(dst, src, 1.0 / n, EPS, ALU.mult, ALU.add), *marks)
            half = const("mh", dst.shape[1])
            return po(lambda e: e.tensor_tensor(dst, dst, half, ALU.pow), m, ld["cn"])

        def rms_rows(xm):
            last = hold.get("junk")
            for t in range(T):
                last = sc(lambda e, t=t: e.activation(cvf, X[:, t, :], ACT.Square, accum_out=ss[:, t:t + 1]),
                          xm, last, hold.get("ss"), ld["x"])
            hold["junk"] = last
            m = rstd(rs, ss, D, last)
            hold["ss"] = m
            return m

        tmpf = [None, None]

        def split_cols(v_fn, dh, dl, *marks):
            j = turn[1] % 2
            turn[1] += 1
            tv = TMP[:, j, :]
            shape = dh.shape[1:]
            if len(shape) == 2:
                tv = tv.rearrange("p (a b) -> p a b", a=shape[0])
            m0 = ve(lambda e: v_fn(e, tv), *marks, tmpf[j])
            m = sc(lambda e: e.activation(dh, tv, ACT.Copy), m0)
            m = ve(lambda e: e.tensor_tensor(dl, tv, dh.bitcast(F32), ALU.subtract), m)
            tmpf[j] = m
            return m0, m

        def transpose4(w, src, *marks):
            for k in range(4):
                p = pe(lambda e, k=k: e.transpose(bank[w][:, k * 128:(k + 1) * 128],
                                                  src[:, k * 128:(k + 1) * 128], ident), *marks, read[w],
                       ld["cn"], sig=(k == 3))
            return p

        def to_columns(src, m, gname, dh, dl, *free, banks=(4, 5, 6, 7)):
            for t in range(T):
                for b in range(2):
                    w = work(banks)
                    p = transpose4(w, src[:, t, b * 512:(b + 1) * 512], m[t])
                    i = bank[w][:, :].rearrange("p (k c) -> p k c", k=4)
                    g = bc(ptcol(gname, 4 * b, 4).unsqueeze(2), P, 4, 128)
                    o = [d[:, 4 * b:4 * b + 4, t * 128:(t + 1) * 128] for d in (dh, dl)]
                    read[w], last = split_cols(lambda e, tv, i=i, g=g: e.tensor_tensor(tv, i, g, ALU.mult),
                                               o[0], o[1], p, ld["pt"], *free)
            return last

        def rmsnorm_T(xm, gname, ht_free):
            r = rms_rows(xm)
            m = [ve(lambda e, t=t: e.tensor_scalar(H[:, t, :], X[:, t, :], rs[:, t:t + 1], None, ALU.mult), r,
                    hold.get("H")) for t in range(T)]
            hold["ss"] = m[1]
            last = to_columns(H, m, gname, HTH, HTL, ht_free)
            hold["H"] = pe.mark()
            return last

        def three(out_, ah, al, bh, bl, *marks, start, stop, sig=False):
            pe(lambda e: e.matmul(out_, ah, bh, start=start, stop=False), *marks, sig=False)
            pe(lambda e: e.matmul(out_, ah, bl, start=False, stop=False), sig=False)
            return pe(lambda e: e.matmul(out_, al, bh, start=False, stop=stop), sig=sig)

        def tok_half(lh, ll, lm, banks, kh, *marks):
            i, wh, wl, wm = take()
            wh, wl = (v[:, :].rearrange("p (k n) -> p k n", k=4) for v in (wh, wl))
            ps = []
            for t in range(T):
                w = banks[t]
                for k in range(4):
                    ts = slice(t * 128, (t + 1) * 128)
                    p = three(bank[w][:, :], lh[:, 4 * kh + k, ts], ll[:, 4 * kh + k, ts], wh[:, k, :], wl[:, k, :],
                              lm, wm, *marks, *((read[w],) if kh == 0 else ()), start=(kh == 0 and k == 0),
                              stop=(kh == 1 and k == 3), sig=(k == 3))
                ps.append(p)
            done(i, p)
            return ps

        def tok_job(lh, ll, lm, evac, banks):
            def first():
                tok_half(lh, ll, lm, banks, 0)

            def second():
                ps = tok_half(lh, ll, lm, banks, 1)
                for t in range(T):
                    read[banks[t]] = evac(t, banks[t], ps[t])
            return [first, second]

        def small_proj(n, lm, raw_w, raw_m, evac):
            m = sc(lambda e: e.activation(wsh[:, 0:8 * n], raw_w, ACT.Copy), raw_m, hold.get("ws"))
            m = ve(lambda e: e.tensor_tensor(wsl[:, 0:8 * n], raw_w, wsh[:, 0:8 * n].bitcast(F32), ALU.subtract), m)
            h, l = (v[:, 0:8 * n].rearrange("p (k n) -> p k n", k=8) for v in (wsh, wsl))
            for t in range(T):
                w = work()
                for k in range(8):
                    ts = slice(t * 128, (t + 1) * 128)
                    p = three(bank[w][:, 0:n], HTH[:, k, ts], HTL[:, k, ts], h[:, k, :], l[:, k, :], lm, m, read[w],
                              start=(k == 0), stop=(k == 7), sig=(k == 7))
                read[w] = last = evac(t, w, p)
            hold["ws"] = p
            return last

        ht = rmsnorm_T(None, "norm_mix_g", None)
        split_to(1)

        posf = small(2)
        m = ve(lambda e: e.tensor_copy(posf, sm[:, 0:2].bitcast(I32)), ld["pos"])
        ang, kk, kc = (XBCT[:, 0, 64 * i:64 * i + 64].rearrange("p (t f) -> p t f", t=T) for i in range(3))
        sin, cos = (XBCT[:, 1, 64 * i:64 * i + 64].rearrange("p (t f) -> p t f", t=T) for i in range(2))
        for t in range(T):
            am = ve(lambda e, t=t: e.tensor_scalar(ang[:, t, :], const("invf", 32), posf[:, t:t + 1], None,
                                                   ALU.mult), m, ld["cn"])
        MAGIC = 12582912.0
        C1, C2 = 6.28125, 0.0019350051879882812
        C3 = 6.283185307179586 - C1 - C2
        rot = []
        for dst, kb, off in ((sin, kk, 0.0), (cos, kc, 0.25)):
            m = ve(lambda e, kb=kb, off=off: e.tensor_scalar(kb, ang, 1.0 / 6.283185307179586, off, ALU.mult,
                                                             ALU.add), am)
            m = ve(lambda e, kb=kb: e.tensor_scalar(kb, kb, MAGIC, None, ALU.add), m)
            m = ve(lambda e, kb=kb: e.tensor_scalar(kb, kb, MAGIC, None, ALU.subtract), m)
            prev = ang
            for c in (C1, C2, C3):
                m = ve(lambda e, kb=kb, dst=dst, c=c, prev=prev: e.scalar_tensor_tensor(
                    out=dst, in0=kb, scalar=-c, in1=prev, op0=ALU.mult, op1=ALU.add), m)
                prev = dst
            if off:
                m = ve(lambda e, dst=dst: e.tensor_scalar(dst, dst, 1.5707963267948966, None, ALU.add), m)
            m = ve(lambda e, dst=dst: e.tensor_scalar(dst, dst, 3.1415925, -3.1415925, ALU.min, ALU.max), m)
            rot.append(sc(lambda e, dst=dst: e.activation(dst, dst, ACT.Sin), m))

        QKR = ZZ
        qkr = [[None] * T for _ in range(2)]
        t3 = [None]

        def rope(c):
            def evac(t, w, p):
                src = bank[w][:, :].rearrange("p (g f) -> p g f", f=32)
                A, B = (cvf[:, j * 512:(j + 1) * 512].rearrange("p (g f) -> p g f", f=32) for j in range(2))
                cb, sbb = (bc(v[:, t, :].unsqueeze(1), P, 16, 32) for v in (cos, sin))
                m1 = ve(lambda e: e.tensor_tensor(A, src, cb, ALU.mult), p, rot[1], t3[0], hold["junk"])
                m2 = ve(lambda e: e.tensor_tensor(B, src, sbb, ALU.mult), rot[0])
                o = QKR[:, t, c * 512:(c + 1) * 512].rearrange("p (g h f) -> p g h f", h=2, f=32)
                Av, Bv = (v.rearrange("p (g h) f -> p g h f", h=2) for v in (A, B))
                ve(lambda e: e.tensor_tensor(o[:, :, 0, :], Av[:, :, 0, :], Bv[:, :, 1, :], ALU.subtract), m1, m2)
                t3[0] = ve(lambda e: e.tensor_tensor(o[:, :, 1, :], Bv[:, :, 0, :], Av[:, :, 1, :], ALU.add))
                qkr[c][t] = t3[0]
                return m2
            return evac

        vm, pm = [], []

        def copy_to(dst_fn, marks):
            def evac(t, w, p):
                m = sc(lambda e: e.activation(dst_fn(t), bank[w][:, :], ACT.Copy), p)
                marks.append(m)
                return m
            return evac

        jobs = []
        for c in range(2):
            for step in tok_job(HTH, HTL, ht, rope(c), (4 + 2 * c, 5 + 2 * c)):
                step()
        for step in tok_job(HTH, HTL, ht, copy_to(lambda t: VV[:, t, 0:512], vm), (4, 5)):
            step()
        hold["junk"] = t3[0]
        RT8 = XS.rearrange("p t (i s) -> p (t i) s", s=S)
        rt = None
        for t in range(T):
            for c in range(2):
                w = work((6, 7))
                p = transpose4(w, QKR[:, t, c * 512:(c + 1) * 512], qkr[c][t])
                rt = read[w] = sc(lambda e, w=w, c=c, t=t: e.activation(
                    RT8[:, 4 * c:4 * c + 4, t * 128:(t + 1) * 128],
                    bank[w][:, :].rearrange("p (k s) -> p k s", k=4), ACT.Copy), p)
        jobs += tok_job(HTH, HTL, ht, copy_to(lambda t: VV[:, t, 512:1024], pm), (2, 3))

        lm, lt = small(6), TMP[:, 0, 0:64]
        m = tmpf[0]
        for i in range(2):
            m = ve(lambda e, i=i: e.tensor_tensor(lt, br[:, 128 * i:128 * i + 64], br[:, 128 * i + 64:128 * i + 128],
                                                  ALU.mult), m, ld["br"])
            m = ve(lambda e, i=i: e.reduce_sum(lm[:, i:i + 1], lt, AX), m)
        tmpf[0] = m
        m = sc(lambda e: e.activation(lm[:, 2:4], lm[:, 0:2], ACT.Exp), m)
        m = ve(lambda e: e.tensor_tensor(lm[:, 4:5], lm[:, 3:4], lm[:, 2:3], ALU.subtract), m)
        nlam = ve(lambda e: e.tensor_scalar(lm[:, 5:6], lm[:, 4:5], -0.2, None, ALU.add), m)

        dT = CV
        mixp = [None]

        def pool_group(g):
            w = work((2, 3))
            pg = VV[:, :, 512 + g * 128:512 + (g + 1) * 128]
            pe(lambda e: e.matmul(bank[w][:, 0:256], pg[:, 0, :], pool_a[:, g * 384:g * 384 + 256], start=True,
                                  stop=False), pm[0], pm[1], ld["pa"], read[w], sig=False)
            p = pe(lambda e: e.matmul(bank[w][:, 128:256], pg[:, 1, :], pool_a[:, g * 384 + 256:g * 384 + 384],
                                      start=False, stop=True))
            m = read[w] = sc(lambda e: e.activation(dT[:, g, :], bank[w][:, 0:256], ACT.Copy), p, hold["junk"])
            w2 = work((2, 3))
            p = pe(lambda e: e.matmul(bank[w2][:, 0:256], pool_w[:, g, :], dT[:, g, :], start=True, stop=True), m,
                   ld["pw"], read[w2])
            hold["poolp"] = p
            j = turn[1] % 2
            turn[1] += 1
            tv = TMP[:, j, 0:256]
            m0 = read[w2] = ve(lambda e: e.tensor_scalar(tv, bank[w2][:, 0:256], ptcol("pool_scale", g), None,
                                                         ALU.mult), p, tmpf[j])
            m = sc(lambda e: e.activation(MXH[:, g, :], tv, ACT.Copy), m0)
            mixp[0] = tmpf[j] = ve(lambda e: e.tensor_tensor(MXL[:, g, :], tv, MXH[:, g, :].bitcast(F32),
                                                             ALU.subtract), m)

        NSC = 64 ** -0.5
        Sx, AT = big(2048 + 768, 1536), big(2048 + 2304, 768)
        mx, nm, sums, rr = small(4), small(4), small(4), small(4)
        sx_free, at_free = [None] * 2, [None] * 2
        half_c = ((0, 128), (128, 384))
        sxs = {}

        def scores(h):
            for n in range(2):
                w = 4 + 2 * (h % 2) + n
                q, k = RT8[64 * n:64 * n + 64, h, :], RT8[64 * n:64 * n + 64, 4 + h, :]
                pe(lambda e, w=w, q=q, k=k: e.matmul(bank[w][:, 0:128], q[:, 0:128], k[:, 0:128], start=True,
                                                     stop=True), rt, read[w], sig=False)
                p = pe(lambda e, w=w, q=q, k=k: e.matmul(bank[w][:, 128:384], q[:, 128:256], k[:, 0:256],
                                                         start=True, stop=True))
                sxs[(h, n)] = (w, p)

        avm = [None]

        def head(h):
            em = []
            for n in range(2):
                w, p = sxs[(h, n)]
                sx = Sx[:, ((h % 2) * 2 + n) * 384:((h % 2) * 2 + n + 1) * 384]
                m = read[w] = ve(lambda e, w=w, sx=sx: e.tensor_tensor(sx, bank[w][:, 0:384], const("chm", 384),
                                                                       ALU.add), p, sx_free[h % 2])
                ve(lambda e, sx=sx, n=n: e.reduce_max(mx[:, 2 * n:2 * n + 1], sx[:, 0:128], AX), m)
                m = ve(lambda e, sx=sx, n=n: e.reduce_max(mx[:, 2 * n + 1:2 * n + 2], sx[:, 128:384], AX))
                m = ve(lambda e, n=n: e.tensor_scalar(nm[:, 2 * n:2 * n + 2], mx[:, 2 * n:2 * n + 2], -NSC, None,
                                                      ALU.mult), m, hold.get("exp"))
                for i, (c0, c1) in enumerate(half_c):
                    em.append(sc(lambda e, sx=sx, n=n, i=i, c0=c0, c1=c1: e.activation(
                        sx[:, c0:c1], sx[:, c0:c1], ACT.Exp, bias=nm[:, 2 * n + i:2 * n + i + 1], scale=NSC,
                        accum_out=sums[:, 2 * n + i:2 * n + i + 1]), m, hold.get("sums")))
            hold["exp"] = em[-1]
            m = ve(lambda e: e.reciprocal(rr[:, 0:4], sums[:, 0:4]), em[-1])
            hold["sums"] = m
            m = ve(lambda e: e.tensor_scalar(rr[:, 2:4], rr[:, 2:4], lm[:, 5:6], None, ALU.mult), m, nlam)
            s0 = Sx[:, (h % 2) * 768:(h % 2) * 768 + 384]
            s1 = Sx[:, (h % 2) * 768 + 384:(h % 2) * 768 + 768]
            mas = []
            for i, (c0, c1) in enumerate(half_c):
                mas.append(ve(lambda e, i=i, c0=c0, c1=c1: e.tensor_scalar(s0[:, c0:c1], s0[:, c0:c1],
                                                                           rr[:, i:i + 1], None, ALU.mult), m))
            for i, (c0, c1) in enumerate(half_c):
                ma = ve(lambda e, i=i, c0=c0, c1=c1: e.scalar_tensor_tensor(
                    out=s0[:, c0:c1], in0=s1[:, c0:c1], scalar=rr[:, 2 + i:3 + i], in1=s0[:, c0:c1],
                    op0=ALU.mult, op1=ALU.add), mas[i])
            w = sxs[(h, 0)][0]
            for j in range(3):
                p = pe(lambda e, w=w, j=j: e.transpose(bank[w][:, j * 128:(j + 1) * 128],
                                                       s0[:, j * 128:(j + 1) * 128], ident), ma, read[w],
                       sig=(j == 2))
            sx_free[h % 2] = p
            at = AT[:, (h % 2) * 384:(h % 2) * 384 + 384]
            am = read[w] = sc(lambda e, w=w: e.activation(at, bank[w][:, 0:384], ACT.Copy), p, at_free[h % 2])
            vh = VV[:, :, h * 128:(h + 1) * 128]
            oc = slice(h * 128, (h + 1) * 128)

            def av():
                pe(lambda e: e.matmul(bank[0][:, oc], at[:, 0:128], vh[:, 0, :], start=True, stop=True), am, vm[0],
                   vm[1], read[0], read[1], sig=False)
                pe(lambda e: e.matmul(bank[1][:, oc], at[:, 128:256], vh[:, 0, :], start=True, stop=False),
                   sig=False)
                avm[0] = at_free[h % 2] = pe(lambda e: e.matmul(bank[1][:, oc], at[:, 256:384], vh[:, 1, :],
                                                                start=False, stop=True))
            return av

        scores(0)
        scores(1)
        jobs.pop(0)()
        av0 = head(0)
        scores(2)
        jobs.pop(0)()
        av1 = head(1)
        av0()
        scores(3)
        pool_group(0)
        pool_group(1)
        av2 = head(2)
        av1()
        pool_group(2)
        pool_group(3)
        av3 = head(3)
        av2()
        av3()
        hold["junk"] = hold["poolp"]
        os_, orr = small(8), small(8)
        om = []
        sqv = big(2048 + 768, 512)
        for i in range(T):
            o = bank[i][:, :]
            m = sc(lambda e, o=o: e.activation(sqv, o, ACT.Square), avm[0], hold.get("sq"))
            m = ve(lambda e, i=i: e.reduce_sum(os_[:, 4 * i:4 * i + 4], sqv.rearrange("p (h c) -> p h c", h=4),
                                               AX), m)
            hold["sq"] = m
            m = rstd(orr[:, 4 * i:4 * i + 4], os_[:, 4 * i:4 * i + 4], 128, m)
            m = ve(lambda e, i=i: e.tensor_scalar(orr[:, 4 * i:4 * i + 4], orr[:, 4 * i:4 * i + 4], 0.8, None,
                                                  ALU.mult), m)
            m = ve(lambda e, i=i, o=o: e.tensor_tensor(
                H[:, i, 0:512].rearrange("p (h c) -> p h c", h=4), o.rearrange("p (h c) -> p h c", h=4),
                bc(orr[:, 4 * i:4 * i + 4].unsqueeze(2), P, 4, 128), ALU.mult), m, hold.get("H"))
            read[i] = m
            om.append(m)
        for t in range(T):
            w = work()
            p = transpose4(w, H[:, t, 0:512], om[t])
            i = bank[w][:, :].rearrange("p (k c) -> p k c", k=4)
            g = bc(ptcol("attn_norm_g", 0, 4).unsqueeze(2), P, 4, 128)
            ts = slice(t * 128, (t + 1) * 128)
            read[w], mixa = split_cols(lambda e, tv, i=i, g=g: e.tensor_tensor(tv, i, g, ALU.mult),
                                       MXH[:, 4:8, ts], MXL[:, 4:8, ts], p)
        hold["H"] = p
        for kh in range(2):
            for c in range(2):
                ps = tok_half(MXH, MXL, mixp[0] if kh == 0 else mixa, (c, 2 + c), kh)
        mx_free = ps[1]

        def add_to_x(p, *marks):
            for b in range(4):
                xv = X[:, b // 2, (b % 2) * 512:(b % 2 + 1) * 512]
                read[b] = ve(lambda e, b=b, xv=xv: e.tensor_tensor(xv, bank[b][:, :], xv, ALU.add), p, *marks)
            return read[3]

        xm = add_to_x(ps[1])

        gb = big(9216, D)
        load("gb", gb, a["norm_final_g"].partition_broadcast(P), hold["poolp"], eng=sy)
        ht = rmsnorm_T(xm, "norm_ffn_g", pe.mark())
        UB = [CV[:, 0:2, :], CV[:, 2:4, :]]
        act_free = [mx_free] * 2
        ub_free = [hold["junk"]] * 2
        actm = {}

        def feature_tiles(htm, banks_cols):
            i, wh, wl, wm = take()
            wh, wl = (v[:, :].rearrange("p (k n) -> p k n", k=8) for v in (wh, wl))
            ps = []
            for f, (w, c) in enumerate(banks_cols):
                for k in range(8):
                    fs = slice(f * 128, (f + 1) * 128)
                    p = three(bank[w][:, c:c + 256], wh[:, k, fs], wl[:, k, fs], HTH[:, k, :], HTL[:, k, :], htm, wm,
                              *((read[w],) if c == 0 else ()), start=(k == 0), stop=(k == 7), sig=(k == 7))
                ps.append(p)
            done(i, p)
            return ps

        def up(g):
            ws = [work(), work()]
            feature_tiles(ht, [(w, 0) for w in ws])
            ps = feature_tiles(ht, [(w, 256) for w in ws])
            for f in range(2):
                j, w, p = 2 * g + f, ws[f], ps[f]
                ub = UB[j % 2]
                ms = []
                for half in range(2):
                    c = 22 * half + j
                    ms.append(sc(lambda e, w=w, half=half, ub=ub, c=c: e.activation(
                        ub[:, half, :], bank[w][:, half * 256:half * 256 + 256], ACT.Identity,
                        bias=ptcol("conv_b", c), scale=ptcol("conv_w", 88 + c)), p, ub_free[j % 2]))
                for tap, sh in ((1, 1), (0, 2)):
                    for half in range(2):
                        c = 22 * half + j
                        ms[half] = ve(lambda e, w=w, half=half, ub=ub, c=c, tap=tap, sh=sh: e.scalar_tensor_tensor(
                            out=ub[:, half, sh:256], in0=bank[w][:, half * 256:half * 256 + 256 - sh],
                            scalar=ptcol("conv_w", 44 * tap + c), in1=ub[:, half, sh:256], op0=ALU.mult,
                            op1=ALU.add), ms[1] if tap else None, ms[half])
                read[w] = ms[1]
                m = sc(lambda e, ub=ub: e.activation(ub[:, 0, :], ub[:, 0, :], ACT.Silu), ms[0])
                m = ve(lambda e, ub=ub: e.tensor_tensor(ub[:, 1, :], ub[:, 0, :], ub[:, 1, :], ALU.mult), m, ms[1])
                ah, al = (v[:, 2 * (g % 2) + f, :] for v in (MXH, MXL))
                m = sc(lambda e, ub=ub, ah=ah: e.activation(ah, ub[:, 1, :], ACT.Copy), m, act_free[g % 2])
                m = ve(lambda e, ub=ub, ah=ah, al=al: e.tensor_tensor(al, ub[:, 1, :], ah.bitcast(F32),
                                                                      ALU.subtract), m, act_free[g % 2])
                ub_free[j % 2] = m
                actm[j] = m

        def down(g):
            i, wh, wl, wm = take()
            wh, wl = (v[:, :].rearrange("p (k n) -> p k n", k=2) for v in (wh, wl))
            for f in range(2):
                j = 2 * g + f
                for t in range(T):
                    for hf in range(2):
                        ts, hs = slice(t * 128, (t + 1) * 128), slice(hf * 512, (hf + 1) * 512)
                        s = 2 * (g % 2) + f
                        p = three(bank[2 * t + hf][:, :], MXH[:, s, ts], MXL[:, s, ts], wh[:, f, hs], wl[:, f, hs],
                                  wm, actm[j], *(read[0:4] if j == 0 else ()), start=(j == 0), stop=(j == FF - 1),
                                  sig=(t == 1 and hf == 1))
            act_free[g % 2] = p
            done(i, p)
            return p

        for g in range(NG):
            up(g)
            if g:
                down(g - 1)
        htf = pe.mark()
        p = down(NG - 1)
        hold["junk"] = ub_free[1]
        xm = add_to_x(p)

        def final_norm(xm, gbv, gm):
            r = rms_rows(xm)
            for t in range(T):
                m = ve(lambda e, t=t: e.scalar_tensor_tensor(out=X[:, t, :], in0=X[:, t, :],
                                                             scalar=rs[:, t:t + 1], in1=gbv,
                                                             op0=ALU.mult, op1=ALU.mult), r, gm)
            hold["ss"] = m
            return m

        xm = final_norm(xm, gb, ld["gb"])
        ws_raw = big(10240, 256)
        load("wsm", ws_raw, a["wsm"], hold["poolp"], eng=sy)

        ht = rmsnorm_T(xm, "norm1_w_2", htf)
        cvfree = [hold["junk"]] * 4

        def conv_piece(c, cw, cb, ntile, dst, j0, banks, tanh, *dfree):
            ws = [work(banks), work(banks)]
            ps = feature_tiles(ht, [(w, 0) for w in ws])
            last = None
            for f in range(2):
                j, w, p = c + f, ws[f], ps[f]
                ui = j % 2 * 2
                u, u2 = CV[:, ui, :], CV[:, ui + 1, :]
                m = sc(lambda e, w=w, u=u, j=j: e.activation(u, bank[w][:, 0:256], ACT.Identity,
                                                             bias=ptcol(cb, j), scale=ptcol(cw, 3 * ntile + j)),
                       p, cvfree[ui])
                for tap, sh in ((2, 1), (1, 2), (0, 3)):
                    m = ve(lambda e, w=w, u=u, j=j, tap=tap, sh=sh: e.scalar_tensor_tensor(
                        out=u[:, sh:256], in0=bank[w][:, 0:256 - sh], scalar=ptcol(cw, ntile * tap + j),
                        in1=u[:, sh:256], op0=ALU.mult, op1=ALU.add), m)
                read[w] = m
                o = dst[:, j0 + f, :]
                if tanh:
                    m = sc(lambda e, u=u, u2=u2: e.activation(u2, u, ACT.Tanh, scale=0.5), m, cvfree[ui])
                    last = ve(lambda e, u=u, u2=u2, o=o: e.scalar_tensor_tensor(
                        out=o, in0=u2, scalar=1.0, in1=u, op0=ALU.add, op1=ALU.mult), m, *dfree)
                else:
                    last = sc(lambda e, u=u, o=o: e.activation(o, u, ACT.Silu), m, *dfree)
                cvfree[ui] = last
            return last

        for c in range(6):
            xbc = conv_piece(2 * c, "ssd_conv_w_2", "ssd_conv_b_2", 12, XBCT, 2 * c, (4, 5, 6, 7), False)
        zm = []

        def silu_z(c):
            def evac(t, w, p):
                m = sc(lambda e: e.activation(ZZ[:, t, c * 512:(c + 1) * 512], bank[w][:, :], ACT.Silu), p)
                zm.append(m)
                return m
            return evac
        for c in range(2):
            for step in tok_job(HTH, HTL, ht, silu_z(c), (6, 7)):
                step()
        G = small(64).rearrange("p (t c) -> p t c", t=T)
        LE = small(64).rearrange("p (t c) -> p t c", t=T)
        gm = small_proj(32, ht, ws_raw, ld["wsm"], lambda t, w, p: ve(
            lambda e: e.tensor_tensor(G[:, t, :], bank[w][:, 0:32], brow("ssd_dt_bias_2", 32), ALU.add), p))
        m = ve(lambda e: e.scalar_tensor_tensor(out=LE, in0=G, scalar=-1.0, in1=G, op0=ALU.mult, op1=ALU.max), gm)
        m = sc(lambda e: e.activation(LE, LE, ACT.Exp, scale=-1.0), m)
        m = sc(lambda e: e.activation(LE, LE, ACT.Ln, bias=1.0), m)
        DTv, LF = (small(n).rearrange("p (t c) -> p t c", t=T) for n in (32, 16))
        IG = G[:, :, 16:24]
        dtm = ve(lambda e: e.scalar_tensor_tensor(out=DTv, in0=G[:, :, 0:16], scalar=0.0, in1=LE[:, :, 0:16],
                                                  op0=ALU.max, op1=ALU.add), m)
        lfm = ve(lambda e: e.scalar_tensor_tensor(out=LF, in0=G[:, :, 24:32], scalar=0.0, in1=LE[:, :, 24:32],
                                                  op0=ALU.min, op1=ALU.subtract))
        AV, ADT = small(16), small(32).rearrange("p (t c) -> p t c", t=T)
        m = sc(lambda e: e.activation(AV, brow("ssd_a_log_2", 16), ACT.Exp))
        m = ve(lambda e: e.tensor_scalar(AV, AV, -1.0, None, ALU.mult), m)
        adm = ve(lambda e: e.tensor_tensor(ADT, DTv, bc(AV.unsqueeze(1), P, T, 16), ALU.mult), m, dtm)

        CB = TMP[:, :, 0:384]
        cbm = None
        for g in range(2):
            w = work((4, 5))
            bt, ct = XBCT[:, 8 + g, :], XBCT[:, 10 + g, :]
            pe(lambda e, w=w, bt=bt, ct=ct: e.matmul(bank[w][:, 0:256], bt[:, 0:128], ct, start=True, stop=True),
               xbc, read[w], sig=False)
            p = pe(lambda e, w=w, bt=bt, ct=ct: e.matmul(bank[w][:, 256:384], bt[:, 128:256], ct[:, 128:256],
                                                         start=True, stop=True))
            cbm = read[w] = ve(lambda e, w=w, g=g: e.tensor_tensor(CB[:, g, :], bank[w][:, 0:384],
                                                                   const("ux", 384), ALU.mult), p, *tmpf)
        for t in range(T):
            for b in range(2):
                w = work((4, 5))
                for k in range(4):
                    p = pe(lambda e, w=w, k=k, b=b, t=t: e.transpose(
                        bank[w][:, k * 128:(k + 1) * 128], XBCT[:, 4 * b + k, t * 128:(t + 1) * 128], ident),
                        xbc, read[w], sig=(k == 3))
                xsm = read[w] = sc(lambda e, w=w, b=b, t=t: e.activation(XS[:, t, b * 512:(b + 1) * 512],
                                                                         bank[w][:, :], ACT.Copy), p)
        xbct_free = p
        XDT = H
        for t in range(T):
            xd = ve(lambda e, t=t: e.tensor_tensor(
                XDT[:, t, :].rearrange("p (h c) -> p h c", h=16), XS[:, t, :].rearrange("p (h c) -> p h c", h=16),
                bc(DTv[:, t, :].unsqueeze(2), P, 16, 64), ALU.mult), xsm, dtm, hold["H"])
        for t in range(T):
            xsd = po(lambda e, t=t: e.tensor_tensor(
                XS[:, t, :].rearrange("p (h c) -> p h c", h=16), XS[:, t, :].rearrange("p (h c) -> p h c", h=16),
                bc(brow("ssd_d_2", 16).unsqueeze(2), P, 16, 64), ALU.mult), xd, xsm)

        slt, ux = const("slt", 128), const("ux", 384)
        LA = [big(9216 + 384 * i, 384) for i in range(2)]
        EE = [big(9216 + 768 + 384 * i, 384) for i in range(3)]
        la_free, ww_free = [gm] * 2, [ld["gb"]] * 3
        OG = XBCT[:, 0:8, :].rearrange("p (t a) b -> p t (a b)", t=T)
        vmm, ogm = [], []

        def og_copy(c):
            def evac(t, w, p):
                m = sc(lambda e: e.activation(OG[:, t, c * 512:(c + 1) * 512], bank[w][:, :], ACT.Copy), p,
                       xbct_free)
                ogm.append(m)
                return m
            return evac

        jobs = []
        for c in range(2):
            jobs += tok_job(HTH, HTL, ht, copy_to(lambda t, c=c: VV[:, t, c * 512:(c + 1) * 512], vmm), (6, 7))
        for c in range(2):
            jobs += tok_job(HTH, HTL, ht, og_copy(c), (6, 7))

        def ssd_seg(h):
            i, la = h % 2, LA[h % 2]
            for t in range(T):
                ve(lambda e, t=t: e.tensor_scalar(la[:, t * 128:(t + 1) * 128], slt, ADT[:, t, h:h + 1], None,
                                                  ALU.mult), adm, la_free[i], xm)
            lam_ = ve(lambda e: e.tensor_scalar(la[:, 256:384], ux[:, 128:256], ADT[:, 1, h:h + 1], None, ALU.mult))
            w = work((4, 5))
            pe(lambda e: e.matmul(bank[w][:, 0:256], la[:, 0:128], ux[:, 0:256], start=True, stop=False), lam_,
               read[w], sig=False)
            pe(lambda e: e.matmul(bank[w][:, 128:256], la[:, 256:384], ux[:, 0:128], start=False, stop=True),
               sig=False)
            p = pe(lambda e: e.matmul(bank[w][:, 256:384], la[:, 128:256], ux[:, 0:128], start=True, stop=True))
            la_free[i] = p
            ee = EE[h % 3]
            m = read[w] = sc(lambda e: e.activation(ee, bank[w][:, 0:384], ACT.Exp), p, ww_free[h % 3])
            return ve(lambda e: e.tensor_tensor(ee, ee, CB[:, h // 8, :], ALU.mult), m, cbm)

        def ssd_y(h, wm_):
            hb, hc, ee = h // 8, (h % 8) * 64, EE[h % 3]
            xd0, xd1 = XDT[:, 0, h * 64:(h + 1) * 64], XDT[:, 1, h * 64:(h + 1) * 64]
            pe(lambda e: e.matmul(bank[hb][:, hc:hc + 64], ee[:, 0:128], xd0, start=True, stop=True), wm_, xd,
               *read[0:4], sig=False)
            pe(lambda e: e.matmul(bank[2 + hb][:, hc:hc + 64], ee[:, 128:256], xd0, start=True, stop=False),
               sig=False)
            ww_free[h % 3] = pe(lambda e: e.matmul(bank[2 + hb][:, hc:hc + 64], ee[:, 256:384], xd1, start=False,
                                                   stop=True))
            return ww_free[h % 3]

        wms = {}
        for h in range(17):
            if h < 16:
                wms[h] = ssd_seg(h)
            if h % 2 == 0 and jobs:
                jobs.pop(0)()
            if h:
                yp = ssd_y(h - 1, wms[h - 1])
        for j in jobs:
            j()
        tmpf = [yp, yp]
        gss, grs = small(4), small(4)
        gmk = []
        for b in range(4):
            t, g = b // 2, b % 2
            yv, zv = XS[:, t, g * 512:(g + 1) * 512], ZZ[:, t, g * 512:(g + 1) * 512]
            m = read[b] = ve(lambda e, b=b, yv=yv: e.tensor_tensor(yv, bank[b][:, :], yv, ALU.add), yp, xsd)
            m = ve(lambda e, yv=yv, zv=zv: e.tensor_tensor(yv, yv, zv, ALU.mult), m, zm[3])
            hold["junk"] = sc(lambda e, b=b, yv=yv: e.activation(cvf[:, 0:512], yv, ACT.Square,
                                                                 accum_out=gss[:, b:b + 1]), m, hold["junk"],
                              *cvfree)
        m = rstd(grs, gss, 512, hold["junk"])
        for b in range(4):
            t, g = b // 2, b % 2
            yv = XS[:, t, g * 512:(g + 1) * 512]
            gmk.append(ve(lambda e, b=b, yv=yv: e.tensor_scalar(yv, yv, grs[:, b:b + 1], None, ALU.mult), m))
        cvfree = [hold["junk"]] * 4

        def qk_pieces(c):
            s = 4 * (c % 2)
            conv_piece(2 * c, "ml_conv_w_2", "ml_conv_b_2", 16, QKT, s, (6, 7), True, qk_free[c % 2])
            return conv_piece(8 + 2 * c, "ml_conv_w_2", "ml_conv_b_2", 16, QKT, s + 2, (6, 7), True, qk_free[c % 2])

        qk_free = [yp, yp]
        qkm = {0: qk_pieces(0)}
        mix0 = to_columns(XS, [gmk[1], gmk[3]], "ssd_norm_w_2", MXH, MXL, act_free[0], act_free[1], banks=(4, 5))
        xs_free = pe.mark()
        ogt = sc(lambda e: e.activation(OG, OG, ACT.Tanh, scale=0.5), *ogm)
        ogt = ve(lambda e: e.tensor_scalar(OG, OG, 1.0, None, ALU.add), ogt)

        xh = [None, None]

        def x_add(c):
            def evac(t, w, p):
                xv = X[:, t, c * 512:(c + 1) * 512]
                xh[c] = ve(lambda e: e.tensor_tensor(xv, bank[w][:, :], xv, ALU.add), p)
                return xh[c]
            return evac

        RR = [big(2048 + 2048 + 384 * i, 384) for i in range(2)]
        DD = [big(384 * i, 384) for i in range(2)]
        ST = [big(768 + 384 * i, 384) for i in range(2)]
        mmx, nmx, den = (small(16).rearrange("p (t h) -> p t h", t=T) for _ in range(3))
        rr_free, dd_free, st_free = [xbct_free] * 2, [gmk[3]] * 2, [gmk[3]] * 2
        KS = 0.25 * 128 ** -0.5

        def ml_d(h):
            i, R, DDi = h % 2, RR[h % 2], DD[h % 2]
            for t in range(T):
                m = ve(lambda e, t=t: e.tensor_scalar(R[:, t * 128:(t + 1) * 128], slt, LF[:, t, h:h + 1], None,
                                                      ALU.mult), lfm, rr_free[i])
                ve(lambda e, t=t: e.scalar_tensor_tensor(
                    out=R[:, t * 128:(t + 1) * 128], in0=ident, scalar=IG[:, t, h:h + 1],
                    in1=R[:, t * 128:(t + 1) * 128], op0=ALU.mult, op1=ALU.add), m)
            rm = ve(lambda e: e.tensor_scalar(R[:, 256:384], ux[:, 128:256], LF[:, 1, h:h + 1], None, ALU.mult))
            w = work((4, 5))
            pe(lambda e: e.matmul(bank[w][:, 0:128], ux[:, 0:128], R[:, 0:128], start=True, stop=True), rm,
               read[w], sig=False)
            pe(lambda e: e.matmul(bank[w][:, 128:256], ux[:, 128:256], R[:, 0:128], start=True, stop=False),
               sig=False)
            pe(lambda e: e.matmul(bank[w][:, 128:256], ux[:, 0:128], R[:, 256:384], start=False, stop=True),
               sig=False)
            p = pe(lambda e: e.matmul(bank[w][:, 256:384], ux[:, 0:128], R[:, 128:256], start=True, stop=True))
            rr_free[i] = p
            m = read[w] = ve(lambda e: e.tensor_tensor(DDi, bank[w][:, 0:384], const("neg", 384), ALU.add), p,
                             dd_free[i])
            ve(lambda e: e.reduce_max(mmx[:, 0, h:h + 1], DDi[:, 0:128], AX), m)
            m = ve(lambda e: e.reduce_max(mmx[:, 1, h:h + 1], DDi[:, 128:384], AX))
            m = ve(lambda e: e.tensor_scalar(nmx[:, :, h:h + 1], mmx[:, :, h:h + 1], -1.0, None, ALU.mult), m)
            for t, (c0, c1) in enumerate(half_c):
                em_ = sc(lambda e, t=t, c0=c0, c1=c1: e.activation(
                    DDi[:, c0:c1], DDi[:, c0:c1], ACT.Exp, bias=nmx[:, t, h:h + 1]), m)
            return em_

        def ml_s(h, em_, qk):
            i, DDi, STi = h % 2, DD[h % 2], ST[h % 2]
            s = 4 * ((h // 2) % 2) + h % 2
            w = work((4, 5))
            q, k = QKT[:, s, :], QKT[:, s + 2, :]
            pe(lambda e: e.matmul(bank[w][:, 0:128], q[:, 0:128], k[:, 0:128], start=True, stop=True), qk, read[w],
               sig=False)
            p = pe(lambda e: e.matmul(bank[w][:, 128:384], q[:, 128:256], k, start=True, stop=True))
            if h % 2:
                qk_free[(h // 2) % 2] = p
            for t, (c0, c1) in enumerate(half_c):
                m = ve(lambda e, t=t, c0=c0, c1=c1: e.tensor_tensor_reduce(
                    DDi[:, c0:c1], bank[w][:, c0:c1], DDi[:, c0:c1], KS, 0.0, ALU.mult, ALU.add,
                    den[:, t, h:h + 1]), p, em_)
            read[w] = m
            return m

        def ml_y(h, sm_):
            i, DDi, STi = h % 2, DD[h % 2], ST[h % 2]
            w = work((4, 5))
            for j in range(3):
                p = pe(lambda e, w=w, j=j: e.transpose(bank[w][:, j * 128:(j + 1) * 128],
                                                       DDi[:, j * 128:(j + 1) * 128], ident), sm_, read[w],
                       sig=(j == 2))
            dd_free[i] = p
            return read_set(w, sc(lambda e: e.activation(STi, bank[w][:, 0:384], ACT.Copy), p, st_free[i]))

        def read_set(w, m):
            read[w] = m
            return m

        def ml_v(h, am):
            STi = ST[h % 2]
            hb, hc = h // 4, (h % 4) * 128
            v0, v1 = VV[:, 0, h * 128:(h + 1) * 128], VV[:, 1, h * 128:(h + 1) * 128]
            pe(lambda e: e.matmul(bank[hb][:, hc:hc + 128], STi[:, 0:128], v0, start=True, stop=True), am, *vmm,
               *read[0:4], sig=False)
            pe(lambda e: e.matmul(bank[2 + hb][:, hc:hc + 128], STi[:, 128:256], v0, start=True, stop=False),
               sig=False)
            st_free[h % 2] = pe(lambda e: e.matmul(bank[2 + hb][:, hc:hc + 128], STi[:, 256:384], v1, start=False,
                                                   stop=True))
            return st_free[h % 2]

        wjobs = [tok_job(MXH, MXL, mix0, x_add(c), (6, 7)) for c in range(2)]
        emd = {0: ml_d(0)}
        for h in range(8):
            c = h // 2
            if h + 1 < 8:
                emd[h + 1] = ml_d(h + 1)
            s_ = ml_s(h, emd[h], qkm[c])
            if h % 2 == 0 and c < 3:
                conv_piece(2 * c + 2, "ml_conv_w_2", "ml_conv_b_2", 16, QKT, 4 * ((c + 1) % 2), (6, 7), True,
                           qk_free[(c + 1) % 2])
            elif h % 2 == 1 and c < 3:
                qkm[c + 1] = conv_piece(10 + 2 * c, "ml_conv_w_2", "ml_conv_b_2", 16, QKT, 4 * ((c + 1) % 2) + 2,
                                        (6, 7), True, qk_free[(c + 1) % 2])
            am = ml_y(h, s_)
            yp = ml_v(h, am)
            for at_h, job, step in FILL:
                if at_h == h:
                    wjobs[job][step]()
        em_ = sc(lambda e: e.activation(nmx, nmx, ACT.Exp))
        m = ve(lambda e: e.scalar_tensor_tensor(out=den, in0=den, scalar=-1.0, in1=den, op0=ALU.mult, op1=ALU.max),
               s_)
        m = ve(lambda e: e.tensor_tensor(den, den, nmx, ALU.max), m, em_)
        m = ve(lambda e: e.reciprocal(den, den), m)
        mu, va = (small(16).rearrange("p (b h) -> p b h", b=4) for _ in range(2))
        YM = XS
        ymk = []
        for b in range(4):
            t, g = b // 2, b % 2
            jb = cvf[:, (b % 2) * 512:(b % 2 + 1) * 512]
            jv = jb.rearrange("p (h c) -> p h c", h=4)
            yv = YM[:, t, g * 512:(g + 1) * 512].rearrange("p (h c) -> p h c", h=4)
            ov = OG[:, t, g * 512:(g + 1) * 512].rearrange("p (h c) -> p h c", h=4)
            bv = bank[b][:, :].rearrange("p (h c) -> p h c", h=4)
            m2 = read[b] = ve(lambda e, yv=yv, bv=bv, t=t, g=g: e.tensor_tensor(
                yv, bv, bc(den[:, t, 4 * g:4 * g + 4].unsqueeze(2), P, 4, 128), ALU.mult), m, yp, xs_free)
            m2 = ve(lambda e, yv=yv, b=b: e.reduce_sum(mu[:, b, :], yv, AX), m2)
            m2 = ve(lambda e, b=b: e.tensor_scalar(mu[:, b, :], mu[:, b, :], 1.0 / 128, None, ALU.mult), m2)
            m2 = ve(lambda e, yv=yv, b=b: e.tensor_tensor(yv, yv, bc(mu[:, b, :].unsqueeze(2), P, 4, 128),
                                                          ALU.subtract), m2)
            m3 = sc(lambda e, yv=yv, jv=jv: e.activation(jv, yv, ACT.Square), m2, hold["junk"], *cvfree,
                    hold.get(("jv", b % 2)))
            m3 = ve(lambda e, b=b, jv=jv: e.reduce_sum(va[:, b, :], jv, AX), m3)
            hold[("jv", b % 2)] = m3
            m3 = rstd(va[:, b, :], va[:, b, :], 128, m3)
            ov2 = ve(lambda e, yv=yv, ov=ov: e.tensor_tensor(yv, yv, ov, ALU.mult), m2, ogt, m3)
            ymk.append(ve(lambda e, yv=yv, b=b: e.scalar_tensor_tensor(
                out=yv, in0=yv, scalar=0.5, in1=bc(va[:, b, :].unsqueeze(2), P, 4, 128), op0=ALU.mult,
                op1=ALU.mult), m3, ov2))
        hold["junk"] = hold[("jv", 1)]
        mix1 = to_columns(YM, [ymk[1], ymk[3]], "ml_norm_w_2", MXH, MXL, pe.mark())
        mix_pe = pe.mark()
        ld_free = [yp, ymk[3], mix_pe]
        gbf = big(8192, D)
        iota = big(10240, 512)
        wr_raw = cvf[:, 0:288]
        load("gbf", gbf, a["norm_f_w_2"].partition_broadcast(P), *ld_free, eng=sy)
        load("iota", iota, a["iota512"].partition_broadcast(P), *ld_free, eng=sy)
        for c in range(2):
            for step in tok_job(MXH, MXL, mix1, x_add(c), (6 - 2 * c, 7 - 2 * c)):
                step()

        hold["H"] = yp
        ht = rmsnorm_T(xh[1], "norm2_w_2", pe.mark())
        h2m = hold["ss"]
        load("wrt", wr_raw, a["wrt"], hold["junk"], eng=sy)
        RB = big(9216, 1024)
        rb_at = [0]

        def rb(*shape):
            n = int(np.prod(shape))
            v = RB[:, rb_at[0]:rb_at[0] + n]
            rb_at[0] += n
            assert rb_at[0] <= 1024
            return v.rearrange("p (a b) -> p a b", a=shape[0]) if len(shape) == 2 else v

        L = rb(T, 36)
        lmk = small_proj(36, ht, wr_raw, ld["wrt"], lambda t, w, p: ve(
            lambda e: e.tensor_tensor(L[:, t, :], bank[w][:, 0:36], brow("router_g_b_2", 36), ALU.add), p,
            *ld_free))
        H2H, H2L = (v[:, :, :].rearrange("p (t a) b -> p t (a b)", t=T) for v in (MXH, MXL))
        m = sc(lambda e: e.activation(H2H, H[:, :, :], ACT.Copy), h2m, pe.mark())
        h2s = ve(lambda e: e.tensor_tensor(H2L, H[:, :, :], H2H.bitcast(F32), ALU.subtract), m)

        def bt(v, n):
            return bc(v.unsqueeze(2), P, T, n)

        def top1(vals, n, iot, mval, onehot, *marks):
            eq, idx = rb(T, n), rb(T, 1)
            m = ve(lambda e: e.reduce_max(mval, vals, AX), *marks)
            m = ve(lambda e: e.tensor_tensor(eq, vals, bt(mval, n), ALU.is_ge), m)
            m = ve(lambda e: e.scalar_tensor_tensor(out=eq, in0=eq, scalar=-100.0,
                                                    in1=bc(iot.unsqueeze(1), P, T, n),
                                                    op0=ALU.mult, op1=ALU.add), m)
            m = ve(lambda e: e.tensor_reduce(idx[:, :, 0], eq, AX, ALU.min), m)
            rb_at[0] -= T * (n + 1)
            return ve(lambda e: e.tensor_tensor(onehot, eq, bt(idx[:, :, 0], n), ALU.is_equal), m)

        goh, ge2 = rb(T, 4), rb(T, 4)
        oh1, oh2, el = rb(T, 32), rb(T, 32), rb(T, 32)
        gmx, gsum, m1_, m2_, dm, g1, g2, pos = (rb(2) for _ in range(8))
        pos2 = rb(2)
        m = top1(L[:, :, 0:4], 4, const("iota", 4), gmx, goh, lmk)
        gm1 = ve(lambda e: e.tensor_tensor(ge2, L[:, :, 0:4], bt(gmx, 4), ALU.subtract), m)
        gm1 = sc(lambda e: e.activation(ge2, ge2, ACT.Exp), gm1)
        m = ve(lambda e: e.tensor_scalar(goh, goh, 1.0, 1e30, ALU.subtract, ALU.mult), m)
        for t in range(T):
            m = ve(lambda e, t=t: e.tensor_tensor(el[:, t, :].rearrange("p (g c) -> p g c", g=4),
                                                  L[:, t, 4:36].rearrange("p (g c) -> p g c", g=4),
                                                  bc(goh[:, t, :].unsqueeze(2), P, 4, 8), ALU.add), m)
        m = top1(el, 32, const("iota", 32, 4), m1_, oh1, m)
        m = ve(lambda e: e.scalar_tensor_tensor(out=el, in0=oh1, scalar=-2e30, in1=el, op0=ALU.mult,
                                                op1=ALU.add), m)
        m = top1(el, 32, const("iota", 32, 4), m2_, oh2, m)
        MM = el
        mmm = ve(lambda e: e.tensor_tensor(MM, oh1, oh2, ALU.add), m)
        w = work()
        tri, ones = ux[:, 0:128], ux[:, 128:256]
        bw = bank[w]
        pe(lambda e: e.matmul(bw[:, 0:32], ones, MM[:, 0, :], start=True, stop=False), mmm, read[w], sig=False)
        pe(lambda e: e.matmul(bw[:, 0:32], ones, MM[:, 1, :], start=False, stop=True), sig=False)
        pe(lambda e: e.matmul(bw[:, 32:64], tri, MM[:, 0, :], start=True, stop=True), sig=False)
        pe(lambda e: e.matmul(bw[:, 64:96], ones, MM[:, 0, :], start=True, stop=False), sig=False)
        p = pe(lambda e: e.matmul(bw[:, 64:96], tri, MM[:, 1, :], start=False, stop=True))
        CR = rb(3, 32)
        m = read[w] = ve(lambda e: e.tensor_copy(CR, bw[:, 0:96].rearrange("p (a b) -> p a b", a=3)), p)
        cnt, rank = CR[:, 0, :], CR[:, 1:3, :]
        inc, off = rb(32), rb(32)
        m = ve(lambda e: e.tensor_tensor_scan(inc, ones[:, 0:32], cnt, 0.0, ALU.mult, ALU.add), m)
        offm = ve(lambda e: e.tensor_tensor(off, inc, cnt, ALU.subtract), m)
        m = ve(lambda e: e.tensor_tensor(rank, rank, bc(off.unsqueeze(1), P, T, 32), ALU.add), offm)
        pt_ = rb(T, 32)
        for ohx, px in ((oh1, pos), (oh2, pos2)):
            m = ve(lambda e, ohx=ohx: e.tensor_tensor(pt_, ohx, rank, ALU.mult), m)
            m = ve(lambda e, px=px: e.reduce_sum(px, pt_, AX), m)
            posm = m = ve(lambda e, px=px: e.tensor_scalar(px, px, -1.0, None, ALU.add), m)
        SEL = HTH[:, 0:4, :].rearrange("p (t a) b -> p t (a b)", t=T)
        SELT = HTL[:, 0:4, :]
        for t in range(T):
            m = ve(lambda e, t=t: e.tensor_scalar(cvf[:, t * 512:(t + 1) * 512], iota, pos[:, t:t + 1], None,
                                                  ALU.is_equal), posm, ld["iota"], lmk)
            selm = ve(lambda e, t=t: e.scalar_tensor_tensor(
                out=SEL[:, t, :], in0=iota, scalar=pos2[:, t:t + 1], in1=cvf[:, t * 512:(t + 1) * 512],
                op0=ALU.is_equal, op1=ALU.add), m)
        FL, US, EQ = rb(32, 4), rb(128), rb(128)
        o4, i4, c4 = (bc(v.unsqueeze(2), P, 32, 4) for v in (off, inc, cnt))
        lo, hi = (bc(const(n, 4).unsqueeze(1), P, 32, 4) for n in ("lo", "hi"))
        FLf = FL.rearrange("p a b -> p (a b)")
        EQ4 = EQ.rearrange("p (a b) -> p a b", a=32)
        m = ve(lambda e: e.tensor_tensor(FL, o4, hi, ALU.is_lt), offm)
        m = ve(lambda e: e.tensor_tensor(EQ4, i4, lo, ALU.is_gt), m)
        m = ve(lambda e: e.tensor_tensor(FL, FL, EQ4, ALU.mult), m)
        m = ve(lambda e: e.tensor_scalar(EQ4, c4, 0.0, None, ALU.is_gt), m)
        m = ve(lambda e: e.tensor_tensor(FL, FL, EQ4, ALU.mult), m)
        m = ve(lambda e: e.tensor_tensor_scan(US, bc(ones[:, 0:1], P, 128), FLf, 0.0, ALU.mult, ALU.add), m)
        m = ve(lambda e: e.scalar_tensor_tensor(out=EQ, in0=US, scalar=const("up1", 1), in1=FLf,
                                                op0=ALU.is_equal, op1=ALU.mult), m)
        TB = rb(4)
        TBI = small(4).bitcast(I32)
        for i, code in enumerate(("ecode", "tcode")):
            m = ve(lambda e, code=code: e.tensor_tensor(FLf, EQ, const(code, 128), ALU.mult), m)
            m = ve(lambda e, i=i: e.reduce_sum(TB[:, i:i + 1], FLf, AX), m)
        m = ve(lambda e: e.scalar_tensor_tensor(out=TB[:, 2:3], in0=TB[:, 1:2], scalar=32.0, in1=TB[:, 0:1],
                                                op0=ALU.mult, op1=ALU.add), m)
        m = ve(lambda e: e.tensor_copy(TB[:, 3:4], US[:, 127:128]), m)
        tbm = ve(lambda e: e.tensor_copy(TBI, TB), m)
        m = ve(lambda e: e.tensor_tensor(dm, m2_, m1_, ALU.subtract), tbm)
        m = sc(lambda e: e.activation(dm, dm, ACT.Exp), m)
        mg = ve(lambda e: e.reduce_sum(gsum, ge2, AX), gm1)
        m = ve(lambda e: e.tensor_scalar(g1, dm, 1.0, None, ALU.add), m)
        m = ve(lambda e: e.tensor_tensor(g1, g1, gsum, ALU.mult), m, mg)
        m = ve(lambda e: e.reciprocal(g1, g1), m)
        m = ve(lambda e: e.tensor_tensor(g2, g1, dm, ALU.mult), m)
        ma = ve(lambda e: e.tensor_tensor(oh1, oh1, bt(g1, 32), ALU.mult), m)
        mb = ve(lambda e: e.tensor_tensor(oh2, oh2, bt(g2, 32), ALU.mult), m)
        gtm = ve(lambda e: e.tensor_tensor(oh1, oh1, oh2, ALU.add), ma, mb)
        w = work()
        bg = bank[w][:, 0:128].rearrange("p (a b) -> p a b", a=4)
        for j in range(4):
            for t in range(T):
                p = pe(lambda e, j=j, t=t: e.matmul(bg[:, j, :], SEL[:, t, j * 128:(j + 1) * 128].bitcast(F32),
                                                    oh1[:, t, :], start=(t == 0), stop=(t == 1)), selm, gtm,
                       read[w], sig=(j == 3 and t == 1))
        GM = US.rearrange("p (a b) -> p a b", a=4)
        EQg = EQ.rearrange("p (a b) -> p a b", a=4)
        og, ig = (bc(v.unsqueeze(1), P, 4, 32) for v in (off, inc))
        sl = bc(const("slot", 4).unsqueeze(2), P, 4, 32)
        m = ve(lambda e: e.tensor_tensor(EQg, og, sl, ALU.is_le), tbm)
        m = read[w] = ve(lambda e: e.tensor_tensor(GM, bg, EQg, ALU.mult), m, p)
        m = ve(lambda e: e.tensor_tensor(EQg, ig, sl, ALU.is_gt), m)
        gmm = ve(lambda e: e.tensor_tensor(GM, GM, EQg, ALU.mult), m)
        GMf = GM.rearrange("p a b -> p (a b)")
        XST = [big(0, 4, 512), big(2048, 4, 512)]
        YACC = big(4096, 4, D)
        yz = ve(lambda e: e.memset(YACC, 0.0), mix_pe, yp, ymk[3])
        xstm = []
        for k in range(8):
            w = work()
            for t in range(T):
                for i, part in enumerate((H2H, H2L)):
                    p = pe(lambda e, w=w, k=k, t=t, part=part: e.matmul(
                        bank[w][:, :], part[:, t, k * 128:(k + 1) * 128], SEL[:, t, :],
                        start=(t == 0 and part is H2H), stop=(t == 1 and part is H2L)), selm, h2s, read[w],
                        sig=(t == 1 and i == 1))
            dst = XST[k // 4][:, k % 4, :]
            if k % 2:
                m = ve(lambda e, w=w, k=k, dst=dst: e.tensor_scalar(dst, bank[w][:, :], ptcol("norm2_w_2", k), None,
                                                                    ALU.mult), p, mix_pe, yp, ymk[3])
            else:
                m = sc(lambda e, w=w, k=k, dst=dst: e.activation(dst, bank[w][:, :], ACT.Copy,
                                                                 scale=ptcol("norm2_w_2", k)), p, mix_pe, yp,
                       ymk[3])
            read[w] = m
            xstm.append(m)
        x_free = pe.mark()
        for j in range(2):
            w = work()
            for i in range(4):
                tau, t = 2 * j + i // 2, i % 2
                p = pe(lambda e, w=w, i=i, tau=tau, t=t: e.transpose(
                    bank[w][:, i * 128:(i + 1) * 128], SEL[:, t, tau * 128:(tau + 1) * 128].bitcast(F32), ident),
                    selm, read[w], sig=(i == 3))
            stm = read[w] = sc(lambda e, w=w, j=j: e.activation(
                SELT[:, 2 * j:2 * j + 2, :].rearrange("p a b -> p (a b)"), bank[w][:, :], ACT.Copy), p, ht, x_free)

        XCH, XCL = ([v[:, 4 * i:4 * i + 4, :].rearrange("p a (b c) -> p (a b) c", c=128) for i in range(2)]
                    for v in (MXH, MXL))
        HIH, HIL = ([v[:, 4 + 2 * i:6 + 2 * i, :].rearrange("p a (b c) -> p (a b) c", c=128) for i in range(2)]
                    for v in (HTH, HTL))
        SG = [cvf[:, i * 512:(i + 1) * 512] for i in range(2)]
        gs = [small(1) for _ in range(2)]
        GU = [(0, 1), (2, 3)]
        TBK, YB = 4, (6, 7)
        regs = {}
        stacks = {}

        def load_value(eng, name, u, col, top):
            eng.wait(tbm)
            eng.do(lambda e: regs.__setitem__((id(eng), name, u),
                                              e.value_load(TBI[u:u + 1, col:col + 1], min_val=0, max_val=top)))

        def val(eng, name, u):
            return regs[(id(eng), name, u)]

        engines = (sy, sc, ve, pe)
        for eng in engines:
            load_value(eng, "n", 0, 3, UNITS)

        def dyn(w, u, k0, nk, c0, n):
            return lambda: w[bass.ds(val(sy, "e", u), 1), k0 * 128:(k0 + nk) * 128, c0:c0 + n].rearrange(
                "a (k p) n -> p (a k) n", p=P)

        u_ = {"gm": {}, "hid": {}, "hl": {}, "gu": {}, "d": {}, "y": {}, "xc": {}, "t": {}}

        def begin(u):
            load_value(sy, "e", u, 0, NE - 1)
            load_value(sc, "t", u, 1, 3)
            load_value(ve, "t", u, 1, 3)
            load_value(ve, "te", u, 2, 127)
            for w in (a["exp_w_gate_2"], a["exp_w_up_2"]):
                for kh in range(2):
                    add(dyn(w, u, 4 * kh, 4, 0, 512))
            if u:
                for kh in range(2):
                    add(dyn(a["exp_w_down_2"], u - 1, 2 * kh, 2, 0, D))
            pump()
            free = u_["gu"].get(u - 2)
            ms = []
            for i in range(2):
                xs4 = XST[i].rearrange("p k (t c) -> p k t c", t=4)
                dh, dl = XCH[u % 2][:, 4 * i:4 * i + 4, :], XCL[u % 2][:, 4 * i:4 * i + 4, :]

                def src(eng, xs4=xs4):
                    return xs4[:, :, bass.ds(val(eng, "t", u), 1), :]
                m = sc(lambda e, dh=dh, src=src: e.activation(dh.unsqueeze(2), src(sc), ACT.Copy), *xstm, free,
                       x_free)
                ms.append((dh, dl, src, m))
            for dh, dl, src, m in ms:
                m = ve(lambda e, dh=dh, dl=dl, src=src: e.tensor_tensor(
                    dl.unsqueeze(2), src(ve), dh.bitcast(F32).unsqueeze(2), ALU.subtract), m, *xstm, free, x_free)
            u_["xc"][u] = m
            u_["gm"][u] = ve(lambda e: e.tensor_copy(gs[u % 2], GMf[:, bass.ds(val(ve, "te", u), 1)]), gmm,
                             u_["hid"].get(u - 2))
            split_to(st["cur"] + 1)

        def gate_up(u):
            G_, U_ = GU[u % 2]
            for b in (G_, U_):
                for kh in range(2):
                    i, wh, wl, wm = take()
                    wh, wl = (v[:, :].rearrange("p (k n) -> p k n", k=4) for v in (wh, wl))
                    for k in range(4):
                        kk_ = 4 * kh + k
                        p = three(bank[b][:, :], XCH[u % 2][:, kk_, :], XCL[u % 2][:, kk_, :], wh[:, k, :],
                                  wl[:, k, :], wm, u_["xc"][u], read[b] if kh == 0 else None,
                                  start=(kh == 0 and k == 0), stop=(kh == 1 and k == 3), sig=(k == 3))
                    done(i, p)
                if b == G_:
                    sg = read[b] = sc(lambda e: e.activation(SG[u % 2], bank[G_][:, :], ACT.Silu), p,
                                      u_["t"].get(u - 2), selm)
            u_["gu"][u] = p
            u_["hid"][u] = read[U_] = ve(lambda e: e.scalar_tensor_tensor(
                out=SG[u % 2], in0=bank[U_][:, :], scalar=gs[u % 2], in1=SG[u % 2], op0=ALU.mult, op1=ALU.mult),
                p, sg, u_["gm"][u])

        def turn_hidden(u):
            p = transpose4(TBK, SG[u % 2], u_["hid"][u])
            u_["t"][u] = p
            hv = bank[TBK][:, :].rearrange("p (k c) -> p k c", k=4)
            m = sc(lambda e: e.activation(HIH[u % 2], hv, ACT.Copy), p, u_["d"].get(u - 2), stm, x_free)
            m = ve(lambda e: e.tensor_tensor(HIL[u % 2], hv, HIH[u % 2].bitcast(F32), ALU.subtract), m,
                   u_["d"].get(u - 2), stm)
            read[TBK] = u_["hl"][u] = m

        def down_u(u):
            for kh in range(2):
                i, wh, wl, wm = take()
                wh, wl = (v[:, :].rearrange("p (k n) -> p k n", k=2) for v in (wh, wl))
                for k in range(2):
                    for hf in range(2):
                        hs = slice(hf * 512, (hf + 1) * 512)
                        p = three(bank[YB[hf]][:, :], HIH[u % 2][:, 2 * kh + k, :], HIL[u % 2][:, 2 * kh + k, :],
                                  wh[:, k, hs], wl[:, k, hs], wm, u_["hl"][u],
                                  read[YB[hf]] if kh == 0 and k == 0 else None,
                                  start=(kh == 0 and k == 0), stop=(kh == 1 and k == 1),
                                  sig=(hf == 1 and k == 1))
                done(i, p)
            u_["d"][u] = p

        def gather_y(u):
            for hf in range(2):
                def yv(hf=hf):
                    return YACC[:, bass.ds(val(ve, "t", u), 1), hf * 512:(hf + 1) * 512]
                read[YB[hf]] = ve(lambda e, yv=yv, hf=hf: e.tensor_tensor(
                    yv(), bank[YB[hf]][:, :].unsqueeze(1), yv(), ALU.add), u_["d"][u], yz,
                    u_["y"].get(u - 1))
            u_["y"][u] = read[YB[1]]

        def unit(u):
            begin(u)
            if u:
                turn_hidden(u - 1)
            if u > 1:
                gather_y(u - 2)
            gate_up(u)
            if u:
                down_u(u - 1)

        def last_unit(u):
            for kh in range(2):
                add(dyn(a["exp_w_down_2"], u, 2 * kh, 2, 0, D))
            split_to(st["cur"] + 1)
            turn_hidden(u)
            if u:
                gather_y(u - 1)
            down_u(u)
            gather_y(u)

        def keep():
            return ({k: (v.copy() if isinstance(v, (dict, list)) else v) for k, v in st.items()},
                    [(e.n, dict(e.seen)) for e in engines], list(read), [s[1] for s in rsem], list(turn),
                    {k: dict(v) for k, v in u_.items()})

        def back(k):
            st.update(k[0])
            for e, (n, seen) in zip(engines, k[1]):
                e.n, e.seen = n, dict(seen)
            read[:] = k[2]
            for s, v in zip(rsem, k[3]):
                s[1] = v
            turn[:] = k[4]
            u_.update(k[5])

        def enter(u):
            for eng in engines:
                def op(e, eng=eng):
                    g = e.If(val(eng, "n", 0) > u)
                    g.__enter__()
                    stacks.setdefault(id(eng), []).append(g)
                eng.do(op)

        def leave():
            for eng in engines:
                eng.do(lambda e, eng=eng: stacks[id(eng)].pop().__exit__(None, None, None))

        def enter_else():
            for eng in engines:
                def op(e, eng=eng):
                    g = e.Else()
                    g.__enter__()
                    stacks.setdefault(id(eng), []).append(g)
                eng.do(op)

        unit(0)
        kept = []
        for u in range(1, UNITS):
            kept.append(keep())
            enter(u)
            unit(u)
        last_unit(UNITS - 1)
        for u in range(UNITS - 2, -1, -1):
            leave()
            back(kept[u])
            enter_else()
            last_unit(u)
            leave()

        s_join = sem("s_join")
        for eng in (ve, sc, pe):
            eng.do(lambda e: e.drain().then_inc(s_join, 1))
        for eng, name in zip((pe, ve, sc), ("s_pe2", "s_ve2", "s_sc2")):
            eng.sem, eng.n = sem(name), 0
        for eng in (pe, ve, sc):
            eng.wait((s_join, 3))
        read[:] = [None] * 8
        hold["junk"] = hold["ss"] = None
        YH = [WH[i][:, :].rearrange("p (a b) -> p a b", a=2) for i in range(2)]
        YL = [WL[i][:, :].rearrange("p (a b) -> p a b", a=2) for i in range(2)]
        ym = []
        for j in range(4):
            h, l = YH[j // 2][:, j % 2, :], YL[j // 2][:, j % 2, :]
            m = sc(lambda e, j=j, h=h: e.activation(h, YACC[:, j, :], ACT.Copy))
            ym.append(ve(lambda e, j=j, h=h, l=l: e.tensor_tensor(l, YACC[:, j, :], h.bitcast(F32), ALU.subtract),
                         m))
        for j in range(4):
            for b in range(4):
                t, hf = b // 2, b % 2
                hs = slice(hf * 512, (hf + 1) * 512)
                lhs = SELT[:, j, t * 128:(t + 1) * 128]
                pe(lambda e, j=j, b=b, hs=hs, lhs=lhs: e.matmul(bank[b][:, :], lhs, YH[j // 2][:, j % 2, hs],
                                                                start=(j == 0), stop=False), ym[j], sig=False)
                p = pe(lambda e, j=j, b=b, hs=hs, lhs=lhs: e.matmul(bank[b][:, :], lhs, YL[j // 2][:, j % 2, hs],
                                                                    start=False, stop=(j == 3)))
        xm = add_to_x(p)
        m = final_norm(xm, gbf, ld["gbf"])
        osem = dsem("s_out")
        om = sy.dma(osem, lambda e: e.dma_start(out.rearrange("(t p) d -> p t d", p=P), X[:, :, :]), m)
        sy.wait(om)

        block = ctx.enter_context(nc.Block())

        @block.sync
        def _(e):
            sy.run(e)

        @block.scalar
        def _(e):
            sc.run(e)

        @block.vector
        def _(e):
            ve.run(e)

        @block.gpsimd
        def _(e):
            po.run(e)

        @block.tensor
        def _(e):
            pe.run(e)


def kernel(**inputs):
    from concourse import bacc
    from concourse.bass_utils import run_bass_kernel_spmd

    f = {n: np.asarray(v) for n, v in inputs.items()}
    cn, pool_a = constants()
    w2 = f["w_in_2"][0]

    def kcols(w):
        return np.ascontiguousarray(w.reshape(8, P, w.shape[1]).transpose(1, 0, 2)).reshape(P, -1)

    arrays = {
        "x": f["x"][0], "positions": np.ascontiguousarray(f["positions"][0].reshape(T, P).T), "cn": cn, "pool_a": pool_a,
        "pt": np.ascontiguousarray(np.concatenate([f[n].reshape(k, P) for n, k in PT_ROWS]).T),
        "br": np.concatenate([f[n].reshape(k) for n, k in BR_ROWS]),
        "wsm": kcols(np.concatenate([w2[:, 2560:2576], w2[:, 6672:6688]], 1)),
        "wrt": kcols(np.concatenate([f["router_g_w_2"][0], f["router_e_w_2"][0]], 1)),
        "iota512": np.arange(512, dtype=np.float32),
        "norm_final_g": f["norm_final_g"], "norm_f_w_2": f["norm_f_w_2"],
    }
    for n in ("w_in", "pool_w", "w_o", "w_up", "w_down", "w_in_2", "w_out_2", "exp_w_gate_2", "exp_w_up_2",
              "exp_w_down_2"):
        arrays[n] = f[n][0]
    nc = bacc.Bacc("TRN2", target_bir_lowering=False, num_devices=1)
    a, fed = {}, {}
    for n, v in arrays.items():
        fed[f"in_{n}"] = v
        a[n] = nc.dram_tensor(f"in_{n}", v.shape, mybir.dt.from_np(v.dtype), kind="ExternalInput").ap()
    out = nc.dram_tensor("out", (S, D), F32, kind="ExternalOutput").ap()
    build(nc, a, out)
    r = run_bass_kernel_spmd(nc, [fed], core_ids=[0])
    return np.asarray(r.results[0]["out"]).reshape(1, S, D)
```

```python
from contextlib import ExitStack

import numpy as np

import concourse.bass as bass
from concourse import mybir

P = 128
T = 2
S = 256
D = 1024
ALU = mybir.AluOpType
ACT = mybir.ActivationFunctionType
F32 = mybir.dt.float32
F32R = mybir.dt.float32r
I32 = mybir.dt.int32
AX = mybir.AxisListType.X
EPS = 1e-6
NEG = -1e30
FF = 22
NE = 32
RAW = 5
HL = 3
PC = 2048
FILL = ((4, 0, 0), (4, 0, 1), (6, 1, 0), (7, 1, 1))
NT = 5
NS = 128 * NT
WARM = {"start": 30, "ffn": (18, 14), "mixers": (36, 14), "router": 14}
UNITS = 36

PT_ROWS = [("norm_mix_g", 8), ("pool_scale", 4), ("attn_norm_g", 4), ("norm_ffn_g", 8), ("conv_w", 132),
           ("conv_b", 44), ("norm1_w_2", 8), ("ssd_conv_w_2", 48), ("ssd_conv_b_2", 12), ("ssd_norm_w_2", 8),
           ("ml_conv_w_2", 64), ("ml_conv_b_2", 16), ("ml_norm_w_2", 8), ("norm2_w_2", 8)]
PT = {}
_at = 0
for _n, _k in PT_ROWS:
    PT[_n] = _at
    _at += _k
NPT = _at
BR_ROWS = [("lambda_q1", 64), ("lambda_k1", 64), ("lambda_q2", 64), ("lambda_k2", 64), ("ssd_dt_bias_2", 16),
           ("ml_i_bias_2", 8), ("ml_f_bias_2", 8), ("ssd_a_log_2", 16), ("ssd_d_2", 16), ("router_g_b_2", 4),
           ("router_e_b_2", 32)]
BR = {}
_at = 0
for _n, _k in BR_ROWS:
    BR[_n] = _at
    _at += _k
NBR = _at
CN_COLS = [("ident", 128), ("mh", 8), ("invf", 32), ("iota", 36), ("chm", 384), ("ux", 384), ("slt", 128), ("neg", 384), ("lo", NT), ("hi", NT),
           ("up1", 1), ("slot", NT), ("ecode", 32 * NT), ("tcode", 32 * NT)]
CN = {}
_at = 0
for _n, _k in CN_COLS:
    CN[_n] = _at
    _at += _k
NCN = _at


def inv_freq():
    exact = 10000.0 ** (-np.arange(0, 64, 2, dtype=np.float64) / 64)
    return exact.astype(np.float32)


def constants():
    c = np.zeros((P, NCN), np.float32)
    i = np.arange(P)
    tri = (i[:, None] <= i[None, :]).astype(np.float32)
    c[:, CN["ident"]:CN["ident"] + 128] = np.eye(P)
    c[:, CN["ux"]:CN["ux"] + 384] = np.concatenate([tri, np.ones((P, P)), tri], 1)
    c[:, CN["slt"]:CN["slt"] + 128] = i[:, None] > i[None, :]
    neg = np.where(i[None, :] > i[:, None], NEG, 0.0)
    c[:, CN["neg"]:CN["neg"] + 384] = np.concatenate([neg, 0 * neg, neg], 1)
    chm = np.where(i[None, :] // 64 > i[:, None] // 64, NEG, 0.0)
    c[:, CN["chm"]:CN["chm"] + 384] = np.concatenate([chm, 0 * chm, chm], 1)
    c[:, CN["invf"]:CN["invf"] + 32] = inv_freq()[None]
    c[:, CN["iota"]:CN["iota"] + 4] = 100 + np.arange(4)
    c[:, CN["iota"] + 4:CN["iota"] + 36] = 100 + np.arange(32)
    c[:, CN["mh"]:CN["mh"] + 8] = -0.5
    c[:, CN["lo"]:CN["lo"] + NT] = 128 * np.arange(NT)
    c[:, CN["hi"]:CN["hi"] + NT] = 128 * np.arange(NT) + 128
    c[:, CN["up1"]] = i + 1
    c[:, CN["slot"]:CN["slot"] + NT] = 128 * np.arange(NT)[None] + i[:, None]
    k = np.arange(32 * NT)
    c[:, CN["ecode"]:CN["ecode"] + 32 * NT] = k[None] // NT
    c[:, CN["tcode"]:CN["tcode"] + 32 * NT] = k[None] % NT
    pool = np.zeros((P, 4, 384), np.float32)
    t = np.arange(S)
    for g, w in enumerate((2, 4, 8, 16)):
        count = np.minimum(t + 1, w).astype(np.float32)
        a = ((t[:, None] <= t[None, :]) & (t[:, None] > t[None, :] - w)) / count[None, :] - np.eye(S)
        pool[:, g, 0:256] = a[0:128]
        pool[:, g, 256:384] = a[128:256, 128:256]
    return c, pool.reshape(P, 1536)


class Engine:

    def __init__(self, sem):
        self.sem, self.n, self.ops, self.seen = sem, 0, [], {}

    def wait(self, *marks):
        for m in marks:
            if m is None:
                continue
            s, v = m
            if self.seen.get(id(s), 0) < v:
                self.seen[id(s)] = v
                self.ops.append(lambda e, s=s, v=v: e.wait_ge(s, v))

    def __call__(self, fn, *marks, sig=True):
        self.wait(*marks)
        if not sig:
            self.ops.append(fn)
            return None
        self.n += 1
        s = self.sem
        self.ops.append(lambda e: fn(e).then_inc(s, 1))
        return s, self.n

    def dma(self, sem, fn, *marks):
        self.wait(*marks)
        sem[1] += 16
        s = sem[0]
        self.ops.append(lambda e: fn(e).then_inc(s, 16))
        return s, sem[1]

    def mark(self):
        return self.sem, self.n

    def do(self, fn):
        self.ops.append(fn)

    def run(self, e):
        for op in self.ops:
            op(e)


def bc(ap, *shape):
    return ap.broadcast_to(list(shape))


def build(nc, a, out):
    ctx = ExitStack()
    with ctx:
        def sb(name, *shape, dt=F32):
            return ctx.enter_context(nc.sbuf_tensor(name, [P, *shape], dt))

        def sem(name):
            return ctx.enter_context(nc.semaphore(name))

        def dsem(name):
            return [sem(name), 0]

        raw = [sb(f"raw{i}", PC) for i in range(RAW)]
        WH = [sb(f"WH{i}", PC, dt=F32R) for i in range(HL)]
        WL = [sb(f"WL{i}", PC, dt=F32R) for i in range(HL)]
        HTH, HTL = sb("HTH", 8, S, dt=F32R), sb("HTL", 8, S, dt=F32R)
        MXH, MXL = sb("MXH", 8, S, dt=F32R), sb("MXL", 8, S, dt=F32R)
        wsh, wsl = sb("wsh", 288, dt=F32R), sb("wsl", 288, dt=F32R)
        cn = sb("cn", NCN)
        pt = sb("pt", NPT)
        br = sb("br", NBR)
        X = sb("X", T, D)
        H = sb("H", T, D)
        TMP = sb("TMP", 2, 512)
        CV = sb("CV", 4, S)
        sm = sb("sm", 400)
        BIG = sb("BIG", 11264)
        bank = [ctx.enter_context(nc.psum_tensor(f"bank{i}", [P, 512], F32)) for i in range(8)]

        def big(at, *shape):
            n = int(np.prod(shape))
            v = BIG[:, at:at + n]
            if len(shape) == 2:
                v = v.rearrange("p (a b) -> p a b", a=shape[0])
            return v

        ZZ, XBCT, XS, VV = big(0, T, D), big(2048, 12, S), big(5120, T, D), big(7168, T, D)
        QKT = big(9216, 8, S)
        cvf = CV[:, :, :].rearrange("p a b -> p (a b)")

        def const(name, n, at=0):
            return cn[:, CN[name] + at:CN[name] + at + n]

        ident = const("ident", 128)
        pe, ve, sc, po, sy = (Engine(sem(n)) for n in ("s_pe", "s_ve", "s_sc", "s_po", "s_sy"))
        rsem = [dsem(f"s_raw{i}") for i in range(RAW)]

        st = {"stream": [], "whole": {}, "loaded": {}, "rawfree": {}, "split": {}, "hlfree": {}, "nxt": 0, "cur": 0}

        def pump(most=10 ** 6):
            while st["nxt"] < min(most, len(st["stream"])):
                i = st["nxt"]
                if i >= RAW and i - RAW not in st["rawfree"]:
                    return
                src = st["stream"][i]
                dst = raw[i % RAW][:, :]
                st["loaded"][i] = sy.dma(rsem[i % RAW], lambda e, dst=dst, src=src: e.dma_start(
                    dst.rearrange("p (k n) -> p k n", k=src().shape[1]), src()), st["rawfree"].get(i - RAW))
                st["nxt"] += 1

        def add(src, whole=False):
            if whole:
                st["whole"][len(st["stream"])] = True
            st["stream"].append(src if callable(src) else lambda: src)

        def split_to(i):
            while len(st["split"]) <= min(i, len(st["stream"]) - 1):
                j = len(st["split"])
                pump()
                if j in st["whole"]:
                    st["split"][j] = st["loaded"][j]
                    st["hlfree"][j] = st["hlfree"].get(j - HL)
                    continue
                r, h, l = raw[j % RAW][:, :], WH[j % HL], WL[j % HL]
                m = sc(lambda e, r=r, h=h: e.activation(h[:, :], r, ACT.Copy), st["loaded"][j],
                       st["hlfree"].get(j - HL))
                m = ve(lambda e, r=r, h=h, l=l: e.tensor_tensor(l[:, :], r, h[:, :].bitcast(F32), ALU.subtract), m,
                       st["loaded"][j], st["hlfree"].get(j - HL))
                st["split"][j] = m
                st["rawfree"][j] = m
                pump()

        def take():
            i = st["cur"]
            st["cur"] += 1
            split_to(i)
            return i, WH[i % HL], WL[i % HL], st["split"][i]

        def take_whole():
            i = st["cur"]
            st["cur"] += 1
            split_to(i)
            return i, raw[i % RAW], st["loaded"][i]

        def done(i, mark, split=True):
            if i in st["whole"]:
                st["rawfree"][i] = mark
                pump()
            else:
                st["hlfree"][i] = mark
            if split:
                split_to(i + 2)

        def split_next():
            split_to(st["cur"] + 1)

        def kpiece(w, k0, nk, c0, n):
            return w[k0 * 128:(k0 + nk) * 128, c0:c0 + n].rearrange("(k p) n -> p k n", p=P)

        for c in (1, 2, 3, 0):
            for kh in range(2):
                add(kpiece(a["w_in"], 4 * kh, 4, c * 512, 512))
        for kh in range(2):
            for c in range(2):
                add(kpiece(a["w_o"], 4 * kh, 4, c * 512, 512))
        NG = FF // 2
        for g in range(NG):
            add(kpiece(a["w_up"], 0, 8, g * 256, 256))
            add(kpiece(a["w_up"], 0, 8, 2816 + g * 256, 256))
            if g:
                add(kpiece(a["w_down"], 2 * g - 2, 2, 0, D))
        add(kpiece(a["w_down"], 2 * NG - 2, 2, 0, D))
        W2 = a["w_in_2"]
        for c in range(6):
            add(kpiece(W2, 0, 8, 1024 + 256 * c, 256))
        for c in range(2):
            for kh in range(2):
                add(kpiece(W2, 4 * kh, 4, 512 * c, 512))
        for c0 in (4624, 5136, 5648, 6160):
            for kh in range(2):
                add(kpiece(W2, 4 * kh, 4, c0, 512))
        for h in range(-2, 8):
            if h < 6:
                add(kpiece(W2, 0, 8, (2576 if h % 2 == 0 else 3600) + 256 * (h // 2 + 1), 256))
            for at_h, job, step in FILL:
                if at_h == h:
                    add(kpiece(a["w_out_2"], 4 * step, 4, job * 512, 512))
        for kh in range(2):
            for c in range(2):
                add(kpiece(a["w_out_2"], 8 + 4 * kh, 4, c * 512, 512))

        read = [None] * 8
        turn = [0, 0]

        def work(pool=(4, 5, 6, 7), which=0):
            b = pool[turn[which] % len(pool)]
            turn[which] += 1
            return b

        ld = {}

        def load(name, dst, src, *marks, eng=None):
            ld[name] = (eng or sc).dma(dsem(f"s_ld_{name}"), lambda e: e.dma_start(dst, src), *marks)

        for t in range(T):
            load(f"x{t}", X[:, t, :], a["x"][t * P:(t + 1) * P, :], eng=sy)
        n0 = CN["chm"]
        load("cn", cn[:, 0:n0], a["cn"][:, 0:n0], eng=sy)
        load("pt", pt[:, :], a["pt"], eng=sy)
        load("pos", sm[:, 0:2].bitcast(I32), a["positions"], eng=sy)
        pump(2)
        load("cn2", cn[:, n0:NCN], a["cn"][:, n0:NCN], eng=sy)
        pump()
        pool_a = BIG[:, 9216:10752]
        pool_w = BIG[:, 10752:11264].rearrange("p (g c) -> p g c", g=4)
        load("br", br[:, :], a["br"].partition_broadcast(P))
        load("pa", pool_a, a["pool_a"])
        load("pw", pool_w, a["pool_w"].rearrange("g c d -> c g d"))

        smat = [2]

        def small(n):
            v = sm[:, smat[0]:smat[0] + n]
            smat[0] += n
            assert smat[0] <= 400
            return v

        def ptcol(name, i=0, n=1):
            return pt[:, PT[name] + i:PT[name] + i + n]

        def brow(name, n):
            return br[:, BR[name]:BR[name] + n]

        ss, rs = small(2), small(2)
        hold = {}

        def rstd(dst, src, n, *marks):
            m = ve(lambda e: e.tensor_scalar(dst, src, 1.0 / n, EPS, ALU.mult, ALU.add), *marks)
            half = const("mh", dst.shape[1])
            return po(lambda e: e.tensor_tensor(dst, dst, half, ALU.pow), m, ld["cn"])

        def rms_rows(xm):
            ms = []
            for t in range(T):
                hold["junk"] = sc(lambda e, t=t: e.activation(cvf, X[:, t, :], ACT.Square,
                                                              accum_out=ss[:, t:t + 1]),
                                  xm[t], hold.get("junk"), hold.get("ss"))
                ms.append(rstd(rs[:, t:t + 1], ss[:, t:t + 1], D, hold["junk"]))
            hold["ss"] = ms[1]
            return ms

        tmpf = [None, None]

        def split_cols(v_fn, dh, dl, *marks):
            j = turn[1] % 2 if not hold.get("half") else 0
            turn[1] += 1
            tv = TMP[:, j, :]
            shape = dh.shape[1:]
            if len(shape) == 2:
                tv = tv.rearrange("p (a b) -> p a b", a=shape[0])
            m0 = ve(lambda e: v_fn(e, tv), *marks, tmpf[j])
            m = sc(lambda e: e.activation(dh, tv, ACT.Copy), m0)

            def rest():
                tmpf[j] = ve(lambda e: e.tensor_tensor(dl, tv, dh.bitcast(F32), ALU.subtract), m)
                return tmpf[j]
            return m0, rest

        def transpose4(w, src, *marks):
            for k in range(4):
                p = pe(lambda e, k=k: e.transpose(bank[w][:, k * 128:(k + 1) * 128],
                                                  src[:, k * 128:(k + 1) * 128], ident), *marks, read[w],
                       ld["cn"], sig=(k == 3))
            return p

        def to_columns(src, m, gname, dh, dl, *free, banks=(4, 5, 6, 7), halves=(0, 1)):
            rest = None
            for t in range(T):
                for b in halves:
                    w = work(banks)
                    p = transpose4(w, src[:, t, b * 512:(b + 1) * 512], m[t])
                    if rest and hold.get("half"):
                        rest()
                        rest = None
                    i = bank[w][:, :].rearrange("p (k c) -> p k c", k=4)
                    g = bc(ptcol(gname, 4 * b, 4).unsqueeze(2), P, 4, 128)
                    o = [d[:, 4 * b:4 * b + 4, t * 128:(t + 1) * 128] for d in (dh, dl)]
                    read[w], then = split_cols(lambda e, tv, i=i, g=g: e.tensor_tensor(tv, i, g, ALU.mult),
                                               o[0], o[1], p, ld["pt"], *free)
                    if rest:
                        rest()
                    rest = then
            return rest()

        def warm(n, w=0):
            for i in range(n):
                pe(lambda e: e.matmul(bank[w][:, 0:128], ident, ident, start=True, stop=True), read[w], ld["cn"],
                   sig=(i == n - 1))

        def rmsnorm_T(xm, gname, ht_free, before=0, w=7):
            warm(before, w)
            r = rms_rows(xm)
            m = [ve(lambda e: e.tensor_scalar(H[:, 0, :], X[:, 0, :], rs[:, 0:1], None, ALU.mult), r[0],
                    hold.get("H")),
                 sc(lambda e: e.activation(H[:, 1, :], X[:, 1, :], ACT.Copy, scale=rs[:, 1:2]), r[1],
                    hold.get("H"))]
            hold["ss"] = m[1]
            hold["hm"] = m
            last = to_columns(H, m, gname, HTH, HTL, ht_free)
            hold["H"] = pe.mark()
            return last

        def three(out_, ah, al, bh, bl, *marks, start, stop, sig=False):
            pe(lambda e: e.matmul(out_, ah, bh, start=start, stop=False), *marks, sig=False)
            pe(lambda e: e.matmul(out_, ah, bl, start=False, stop=False), sig=False)
            return pe(lambda e: e.matmul(out_, al, bh, start=False, stop=stop), sig=sig)

        def tok_half(lh, ll, lm, banks, kh, *marks, split=True):
            i, wh, wl, wm = take()
            wh, wl = (v[:, :].rearrange("p (k n) -> p k n", k=4) for v in (wh, wl))
            ps = []
            for t in range(T):
                w = banks[t]
                for k in range(4):
                    ts = slice(t * 128, (t + 1) * 128)
                    p = three(bank[w][:, :], lh[:, 4 * kh + k, ts], ll[:, 4 * kh + k, ts], wh[:, k, :], wl[:, k, :],
                              lm, wm, *marks, *((read[w],) if kh == 0 else ()), start=(kh == 0 and k == 0),
                              stop=(kh == 1 and k == 3), sig=(k == 3))
                ps.append(p)
            done(i, p, split)
            return ps

        def tok_job(lh, ll, lm, evac, banks):
            def first():
                tok_half(lh, ll, lm, banks, 0)

            def second():
                ps = tok_half(lh, ll, lm, banks, 1)
                for t in range(T):
                    read[banks[t]] = evac(t, banks[t], ps[t])
            return [first, second]

        def small_split(n, raw_w, raw_m):
            m = sc(lambda e: e.activation(wsh[:, 0:8 * n], raw_w, ACT.Copy), raw_m, hold.get("ws"))
            return ve(lambda e: e.tensor_tensor(wsl[:, 0:8 * n], raw_w, wsh[:, 0:8 * n].bitcast(F32), ALU.subtract),
                      m)

        def small_proj(n, lm, m, evac, also=lambda: None):
            also()
            h, l = (v[:, 0:8 * n].rearrange("p (k n) -> p k n", k=8) for v in (wsh, wsl))
            w = work()
            for k in range(8):
                p = three(bank[w][0:n, 0:256], h[:, k, :], l[:, k, :], HTH[:, k, :], HTL[:, k, :], lm, m, read[w],
                          start=(k == 0), stop=(k == 7), sig=(k == 7))
            hold["ws"] = p
            j = turn[1] % 2
            turn[1] += 1
            tv = TMP[0:n, j, 0:256]
            m = read[w] = sc(lambda e: e.activation(tv, bank[w][0:n, 0:256], ACT.Copy), p, tmpf[j])
            w2 = work()
            for t in range(T):
                p = pe(lambda e, t=t: e.transpose(bank[w2][:, t * 64:t * 64 + n], tv[:, t * 128:(t + 1) * 128],
                                                  ident[0:n, 0:n]), m, read[w2])
            tmpf[j] = p
            for t in range(T):
                read[w2] = last = evac(t, bank[w2][:, t * 64:t * 64 + n], p)
            return last

        ht = rmsnorm_T([ld["x0"], ld["x1"]], "norm_mix_g", None)
        warm(WARM["start"], 0)
        split_to(1)

        posf = small(2)
        m = ve(lambda e: e.tensor_copy(posf, sm[:, 0:2].bitcast(I32)), ld["pos"])
        ang, kk, kc = (XBCT[:, 0, 64 * i:64 * i + 64].rearrange("p (t f) -> p t f", t=T) for i in range(3))
        sin, cos = (XBCT[:, 1, 64 * i:64 * i + 64].rearrange("p (t f) -> p t f", t=T) for i in range(2))
        for t in range(T):
            am = ve(lambda e, t=t: e.tensor_scalar(ang[:, t, :], const("invf", 32), posf[:, t:t + 1], None,
                                                   ALU.mult), m, ld["cn"])
        MAGIC = 12582912.0
        C1, C2 = 6.28125, 0.0019350051879882812
        C3 = 6.283185307179586 - C1 - C2
        rot = []
        for dst, kb, off in ((sin, kk, 0.0), (cos, kc, 0.25)):
            m = ve(lambda e, kb=kb, off=off: e.tensor_scalar(kb, ang, 1.0 / 6.283185307179586, off, ALU.mult,
                                                             ALU.add), am)
            m = ve(lambda e, kb=kb: e.tensor_scalar(kb, kb, MAGIC, None, ALU.add), m)
            m = ve(lambda e, kb=kb: e.tensor_scalar(kb, kb, MAGIC, None, ALU.subtract), m)
            prev = ang
            for c in (C1, C2, C3):
                m = ve(lambda e, kb=kb, dst=dst, c=c, prev=prev: e.scalar_tensor_tensor(
                    out=dst, in0=kb, scalar=-c, in1=prev, op0=ALU.mult, op1=ALU.add), m)
                prev = dst
            if off:
                m = ve(lambda e, dst=dst: e.tensor_scalar(dst, dst, 1.5707963267948966, None, ALU.add), m)
            m = ve(lambda e, dst=dst: e.tensor_scalar(dst, dst, 3.1415925, -3.1415925, ALU.min, ALU.max), m)
            rot.append(sc(lambda e, dst=dst: e.activation(dst, dst, ACT.Sin), m))

        QKR = ZZ
        qkr = [[None] * T for _ in range(2)]
        t3 = [None]

        def rope(c):
            def evac(t, w, p):
                src = bank[w][:, :].rearrange("p (g f) -> p g f", f=32)
                A, B = (cvf[:, j * 512:(j + 1) * 512].rearrange("p (g f) -> p g f", f=32) for j in range(2))
                cb, sbb = (bc(v[:, t, :].unsqueeze(1), P, 16, 32) for v in (cos, sin))
                m1 = ve(lambda e: e.tensor_tensor(A, src, cb, ALU.mult), p, rot[1], t3[0], hold["junk"])
                m2 = ve(lambda e: e.tensor_tensor(B, src, sbb, ALU.mult), rot[0])
                o = QKR[:, t, c * 512:(c + 1) * 512].rearrange("p (g h f) -> p g h f", h=2, f=32)
                Av, Bv = (v.rearrange("p (g h) f -> p g h f", h=2) for v in (A, B))
                ve(lambda e: e.tensor_tensor(o[:, :, 0, :], Av[:, :, 0, :], Bv[:, :, 1, :], ALU.subtract), m1, m2)
                t3[0] = ve(lambda e: e.tensor_tensor(o[:, :, 1, :], Bv[:, :, 0, :], Av[:, :, 1, :], ALU.add))
                qkr[c][t] = t3[0]
                return m2
            return evac

        vm, pm = [], []

        def copy_to(dst_fn, marks):
            def evac(t, w, p):
                m = sc(lambda e: e.activation(dst_fn(t), bank[w][:, :], ACT.Copy), p)
                marks.append(m)
                return m
            return evac

        jobs = []
        for c in range(2):
            for step in tok_job(HTH, HTL, ht, rope(c), (4 + 2 * c, 5 + 2 * c)):
                step()
        for step in tok_job(HTH, HTL, ht, copy_to(lambda t: VV[:, t, 0:512], vm), (4, 5)):
            step()
        hold["junk"] = t3[0]
        RT8 = XS.rearrange("p t (i s) -> p (t i) s", s=S)
        rt = None
        for t in range(T):
            for c in range(2):
                w = work((6, 7))
                p = transpose4(w, QKR[:, t, c * 512:(c + 1) * 512], qkr[c][t])
                rt = read[w] = sc(lambda e, w=w, c=c, t=t: e.activation(
                    RT8[:, 4 * c:4 * c + 4, t * 128:(t + 1) * 128],
                    bank[w][:, :].rearrange("p (k s) -> p k s", k=4), ACT.Copy), p)
        jobs += tok_job(HTH, HTL, ht, copy_to(lambda t: VV[:, t, 512:1024], pm), (2, 3))

        lm, lt = small(6), TMP[:, 0, 0:64]
        m = tmpf[0]
        for i in range(2):
            m = ve(lambda e, i=i: e.tensor_tensor(lt, br[:, 128 * i:128 * i + 64], br[:, 128 * i + 64:128 * i + 128],
                                                  ALU.mult), m, ld["br"])
            m = ve(lambda e, i=i: e.reduce_sum(lm[:, i:i + 1], lt, AX), m)
        tmpf[0] = m
        m = sc(lambda e: e.activation(lm[:, 2:4], lm[:, 0:2], ACT.Exp), m)
        m = ve(lambda e: e.tensor_tensor(lm[:, 4:5], lm[:, 3:4], lm[:, 2:3], ALU.subtract), m)
        nlam = ve(lambda e: e.tensor_scalar(lm[:, 5:6], lm[:, 4:5], -0.2, None, ALU.add), m)

        dT = CV
        mixp = [None]

        dtm_ = {}

        def pool_mean(g):
            w = work((2, 3))
            pg = VV[:, :, 512 + g * 128:512 + (g + 1) * 128]
            pe(lambda e: e.matmul(bank[w][:, 0:256], pg[:, 0, :], pool_a[:, g * 384:g * 384 + 256], start=True,
                                  stop=False), pm[0], pm[1], ld["pa"], read[w], sig=False)
            p = pe(lambda e: e.matmul(bank[w][:, 128:256], pg[:, 1, :], pool_a[:, g * 384 + 256:g * 384 + 384],
                                      start=False, stop=True))
            dtm_[g] = read[w] = sc(lambda e: e.activation(dT[:, g, :], bank[w][:, 0:256], ACT.Copy), p,
                                   hold["junk"])

        def pool_mix(g):
            w2 = work((2, 3))
            p = pe(lambda e: e.matmul(bank[w2][:, 0:256], pool_w[:, g, :], dT[:, g, :], start=True, stop=True), dtm_[g],
                   ld["pw"], read[w2])
            hold["poolp"] = p
            j = turn[1] % 2
            turn[1] += 1
            tv = TMP[:, j, 0:256]
            m0 = read[w2] = ve(lambda e: e.tensor_scalar(tv, bank[w2][:, 0:256], ptcol("pool_scale", g), None,
                                                         ALU.mult), p, tmpf[j])
            m = sc(lambda e: e.activation(MXH[:, g, :], tv, ACT.Copy), m0)
            mixp[0] = tmpf[j] = ve(lambda e: e.tensor_tensor(MXL[:, g, :], tv, MXH[:, g, :].bitcast(F32),
                                                             ALU.subtract), m)

        NSC = 64 ** -0.5
        Sx, AT = big(2048 + 768, 1536), big(2048 + 2304, 768)
        mx, nm, sums, rr = small(4), small(4), small(4), small(4)
        sx_free, at_free = [None] * 2, [None] * 2
        half_c = ((0, 128), (128, 384))
        sxs = {}

        def scores(h):
            for n in range(2):
                w = 4 + 2 * (h % 2) + n
                q, k = RT8[64 * n:64 * n + 64, h, :], RT8[64 * n:64 * n + 64, 4 + h, :]
                pe(lambda e, w=w, q=q, k=k: e.matmul(bank[w][:, 0:128], q[:, 0:128], k[:, 0:128], start=True,
                                                     stop=True), rt, read[w], sig=False)
                p = pe(lambda e, w=w, q=q, k=k: e.matmul(bank[w][:, 128:384], q[:, 128:256], k[:, 0:256],
                                                         start=True, stop=True))
                sxs[(h, n)] = (w, p)

        avm = [None]

        softm = {}

        def soft(h):
            em = []
            for n in range(2):
                w, p = sxs[(h, n)]
                sx = Sx[:, ((h % 2) * 2 + n) * 384:((h % 2) * 2 + n + 1) * 384]
                m = read[w] = ve(lambda e, w=w, sx=sx: e.tensor_tensor(sx, bank[w][:, 0:384], const("chm", 384),
                                                                       ALU.add), p, sx_free[h % 2], ld["cn2"])
                ve(lambda e, sx=sx, n=n: e.reduce_max(mx[:, 2 * n:2 * n + 1], sx[:, 0:128], AX), m)
                m = ve(lambda e, sx=sx, n=n: e.reduce_max(mx[:, 2 * n + 1:2 * n + 2], sx[:, 128:384], AX))
                m = ve(lambda e, n=n: e.tensor_scalar(nm[:, 2 * n:2 * n + 2], mx[:, 2 * n:2 * n + 2], -NSC, None,
                                                      ALU.mult), m, hold.get("exp"))
                for i, (c0, c1) in enumerate(half_c):
                    em.append(sc(lambda e, sx=sx, n=n, i=i, c0=c0, c1=c1: e.activation(
                        sx[:, c0:c1], sx[:, c0:c1], ACT.Exp, bias=nm[:, 2 * n + i:2 * n + i + 1], scale=NSC,
                        accum_out=sums[:, 2 * n + i:2 * n + i + 1]), m, hold.get("sums")))
            hold["exp"] = em[-1]
            m = ve(lambda e: e.reciprocal(rr[:, 0:4], sums[:, 0:4]), em[-1])
            hold["sums"] = m
            m = ve(lambda e: e.tensor_scalar(rr[:, 2:4], rr[:, 2:4], lm[:, 5:6], None, ALU.mult), m, nlam)
            s0 = Sx[:, (h % 2) * 768:(h % 2) * 768 + 384]
            s1 = Sx[:, (h % 2) * 768 + 384:(h % 2) * 768 + 768]
            mas = []
            for i, (c0, c1) in enumerate(half_c):
                mas.append(ve(lambda e, i=i, c0=c0, c1=c1: e.tensor_scalar(s0[:, c0:c1], s0[:, c0:c1],
                                                                           rr[:, i:i + 1], None, ALU.mult), m))
            for i, (c0, c1) in enumerate(half_c):
                ma = ve(lambda e, i=i, c0=c0, c1=c1: e.scalar_tensor_tensor(
                    out=s0[:, c0:c1], in0=s1[:, c0:c1], scalar=rr[:, 2 + i:3 + i], in1=s0[:, c0:c1],
                    op0=ALU.mult, op1=ALU.add), mas[i])
            softm[h] = ma

        def turn_probs(h):
            s0 = Sx[:, (h % 2) * 768:(h % 2) * 768 + 384]
            ma = softm[h]
            w = sxs[(h, 0)][0]
            for j in range(3):
                p = pe(lambda e, w=w, j=j: e.transpose(bank[w][:, j * 128:(j + 1) * 128],
                                                       s0[:, j * 128:(j + 1) * 128], ident), ma, read[w],
                       sig=(j == 2))
            sx_free[h % 2] = p
            at = AT[:, (h % 2) * 384:(h % 2) * 384 + 384]
            am = read[w] = sc(lambda e, w=w: e.activation(at, bank[w][:, 0:384], ACT.Copy), p, at_free[h % 2])
            vh = VV[:, :, h * 128:(h + 1) * 128]
            oc = slice(h * 128, (h + 1) * 128)

            def av():
                pe(lambda e: e.matmul(bank[0][:, oc], at[:, 0:128], vh[:, 0, :], start=True, stop=True), am, vm[0],
                   vm[1], read[0], read[1], sig=False)
                pe(lambda e: e.matmul(bank[1][:, oc], at[:, 128:256], vh[:, 0, :], start=True, stop=False),
                   sig=False)
                avm[0] = at_free[h % 2] = pe(lambda e: e.matmul(bank[1][:, oc], at[:, 256:384], vh[:, 1, :],
                                                                start=False, stop=True))
            return av

        scores(0)
        scores(1)
        soft(0)
        jobs.pop(0)()
        soft(1)
        av0 = turn_probs(0)
        scores(2)
        jobs.pop(0)()
        av1 = turn_probs(1)
        av0()
        scores(3)
        soft(2)
        for g in range(4):
            pool_mean(g)
        soft(3)
        av2 = turn_probs(2)
        av1()
        pool_mix(0)
        pool_mix(1)
        av3 = turn_probs(3)
        av2()
        pool_mix(2)
        pool_mix(3)
        av3()
        for c in range(2):
            tok_half(MXH, MXL, mixp[0], (4 + 2 * c, 5 + 2 * c), 0)
        hold["junk"] = hold["poolp"]
        os_, orr = small(8), small(8)
        om = []
        sqv = big(2048 + 768, 512)
        for i in range(T):
            o = bank[i][:, :]
            m = sc(lambda e, o=o: e.activation(sqv, o, ACT.Square), avm[0], hold.get("sq"))
            m = ve(lambda e, i=i: e.reduce_sum(os_[:, 4 * i:4 * i + 4], sqv.rearrange("p (h c) -> p h c", h=4),
                                               AX), m)
            hold["sq"] = m
            m = rstd(orr[:, 4 * i:4 * i + 4], os_[:, 4 * i:4 * i + 4], 128, m)
            m = ve(lambda e, i=i: e.tensor_scalar(orr[:, 4 * i:4 * i + 4], orr[:, 4 * i:4 * i + 4], 0.8, None,
                                                  ALU.mult), m)
            m = ve(lambda e, i=i, o=o: e.tensor_tensor(
                H[:, i, 0:512].rearrange("p (h c) -> p h c", h=4), o.rearrange("p (h c) -> p h c", h=4),
                bc(orr[:, 4 * i:4 * i + 4].unsqueeze(2), P, 4, 128), ALU.mult), m, hold.get("H"))
            read[i] = m
            om.append(m)
        mixa = []
        for t in range(T):
            w = work((2, 3))
            p = transpose4(w, H[:, t, 0:512], om[t])
            i = bank[w][:, :].rearrange("p (k c) -> p k c", k=4)
            g = bc(ptcol("attn_norm_g", 0, 4).unsqueeze(2), P, 4, 128)
            ts = slice(t * 128, (t + 1) * 128)
            read[w], then = split_cols(lambda e, tv, i=i, g=g: e.tensor_tensor(tv, i, g, ALU.mult),
                                       MXH[:, 4:8, ts], MXL[:, 4:8, ts], p)
            mixa.append(then)
        mixa = [f() for f in mixa][-1]
        hold["H"] = p
        for c in range(2):
            ps = tok_half(MXH, MXL, mixa, (4 + 2 * c, 5 + 2 * c), 1, split=(c == 0))
        mx_free = ps[1]

        def add_to_x(p, banks=(0, 1, 2, 3)):
            for i, b in enumerate(banks):
                xv = X[:, i // 2, (i % 2) * 512:(i % 2 + 1) * 512]
                read[b] = ve(lambda e, b=b, xv=xv: e.tensor_tensor(xv, bank[b][:, :], xv, ALU.add), p)
            return [read[banks[1]], read[banks[3]]]

        xm = add_to_x(ps[1], (4, 6, 5, 7))

        gb = big(9216, D)
        load("gb", gb, a["norm_final_g"].partition_broadcast(P), hold["poolp"], eng=sy)
        ht = rmsnorm_T(xm, "norm_ffn_g", pe.mark(), WARM["ffn"][0], 0)
        warm(WARM["ffn"][1], 0)
        split_next()
        UB = [CV[:, 0:2, :], CV[:, 2:4, :]]
        act_free = [mx_free] * 2
        ub_free = [hold["junk"]] * 2
        actm = {}

        def feature_tiles(htm, banks_cols, split=True, mid=None):
            i, wh, wl, wm = take()
            wh, wl = (v[:, :].rearrange("p (k n) -> p k n", k=8) for v in (wh, wl))
            ps = []
            for f, (w, c) in enumerate(banks_cols):
                for k in range(8):
                    fs = slice(f * 128, (f + 1) * 128)
                    p = three(bank[w][:, c:c + 256], wh[:, k, fs], wl[:, k, fs], HTH[:, k, :], HTL[:, k, :], htm, wm,
                              *((read[w],) if c == 0 else ()), start=(k == 0), stop=(k == 7), sig=(k == 7))
                ps.append(p)
                if mid and f == 0:
                    mid()
            done(i, p, split)
            return ps

        def up(g):
            ws = [work(), work()]
            feature_tiles(ht, [(w, 0) for w in ws])
            ps = feature_tiles(ht, [(w, 256) for w in ws])
            for f in range(2):
                j, w, p = 2 * g + f, ws[f], ps[f]
                ub = UB[j % 2]
                ms = []
                for half in range(2):
                    c = 22 * half + j
                    ms.append(sc(lambda e, w=w, half=half, ub=ub, c=c: e.activation(
                        ub[:, half, :], bank[w][:, half * 256:half * 256 + 256], ACT.Identity,
                        bias=ptcol("conv_b", c), scale=ptcol("conv_w", 88 + c)), p, ub_free[j % 2]))
                for tap, sh in ((1, 1), (0, 2)):
                    for half in range(2):
                        c = 22 * half + j
                        ms[half] = ve(lambda e, w=w, half=half, ub=ub, c=c, tap=tap, sh=sh: e.scalar_tensor_tensor(
                            out=ub[:, half, sh:256], in0=bank[w][:, half * 256:half * 256 + 256 - sh],
                            scalar=ptcol("conv_w", 44 * tap + c), in1=ub[:, half, sh:256], op0=ALU.mult,
                            op1=ALU.add), ms[1] if tap else None, ms[half])
                read[w] = ms[1]
                m = sc(lambda e, ub=ub: e.activation(ub[:, 0, :], ub[:, 0, :], ACT.Silu), ms[0])
                m = ve(lambda e, ub=ub: e.tensor_tensor(ub[:, 1, :], ub[:, 0, :], ub[:, 1, :], ALU.mult), m, ms[1])
                ah, al = (v[:, 2 * (g % 2) + f, :] for v in (MXH, MXL))
                m = sc(lambda e, ub=ub, ah=ah: e.activation(ah, ub[:, 1, :], ACT.Copy), m, act_free[g % 2])
                m = ve(lambda e, ub=ub, ah=ah, al=al: e.tensor_tensor(al, ub[:, 1, :], ah.bitcast(F32),
                                                                      ALU.subtract), m, act_free[g % 2])
                ub_free[j % 2] = m
                actm[j] = m

        def down(g, split=True):
            i, wh, wl, wm = take()
            wh, wl = (v[:, :].rearrange("p (k n) -> p k n", k=2) for v in (wh, wl))
            for f in range(2):
                j = 2 * g + f
                for t in range(T):
                    for hf in range(2):
                        ts, hs = slice(t * 128, (t + 1) * 128), slice(hf * 512, (hf + 1) * 512)
                        s = 2 * (g % 2) + f
                        p = three(bank[2 * t + hf][:, :], MXH[:, s, ts], MXL[:, s, ts], wh[:, f, hs], wl[:, f, hs],
                                  wm, actm[j], *(read[0:4] if j == 0 else ()), start=(j == 0), stop=(j == FF - 1),
                                  sig=(t == 1 and hf == 1))
            act_free[g % 2] = p
            done(i, p, split)
            return p

        for g in range(NG):
            up(g)
            if g:
                down(g - 1)
        htf = pe.mark()
        p = down(NG - 1, split=False)
        hold["junk"] = ub_free[1]
        xm = add_to_x(p)

        def final_norm(xm, gbv, gm):
            r = rms_rows(xm)
            m = [ve(lambda e, t=t: e.scalar_tensor_tensor(out=X[:, t, :], in0=X[:, t, :], scalar=rs[:, t:t + 1],
                                                          in1=gbv, op0=ALU.mult, op1=ALU.mult), r[t], gm)
                 for t in range(T)]
            hold["ss"] = m[1]
            return m

        xm = final_norm(xm, gb, ld["gb"])
        ws_raw = big(10240, 256)
        load("wsm", ws_raw, a["wsm"], hold["poolp"], eng=sy)

        ht = rmsnorm_T(xm, "norm1_w_2", htf, WARM["mixers"][0])
        warm(WARM["mixers"][1], 0)
        split_next()
        cvfree = [hold["junk"]] * 4

        def conv_piece(c, cw, cb, ntile, dst, j0, banks, tanh, *dfree, mid=None, after=None):
            ws = [work(banks), work(banks)]
            ps = feature_tiles(ht, [(w, 0) for w in ws], split=False, mid=mid)
            if after:
                after()
            last = None
            for f in range(2):
                j, w, p = c + f, ws[f], ps[f]
                ui = j % 2 * 2
                u, u2 = CV[:, ui, :], CV[:, ui + 1, :]
                m = sc(lambda e, w=w, u=u, j=j: e.activation(u, bank[w][:, 0:256], ACT.Identity,
                                                             bias=ptcol(cb, j), scale=ptcol(cw, 3 * ntile + j)),
                       p, cvfree[ui])
                for tap, sh in ((2, 1), (1, 2), (0, 3)):
                    m = ve(lambda e, w=w, u=u, j=j, tap=tap, sh=sh: e.scalar_tensor_tensor(
                        out=u[:, sh:256], in0=bank[w][:, 0:256 - sh], scalar=ptcol(cw, ntile * tap + j),
                        in1=u[:, sh:256], op0=ALU.mult, op1=ALU.add), m)
                read[w] = m
                o = dst[:, j0 + f, :]
                if f:
                    split_next()
                if tanh:
                    m = sc(lambda e, u=u, u2=u2: e.activation(u2, u, ACT.Tanh, scale=0.5), m, cvfree[ui])
                    last = ve(lambda e, u=u, u2=u2, o=o: e.scalar_tensor_tensor(
                        out=o, in0=u2, scalar=1.0, in1=u, op0=ALU.add, op1=ALU.mult), m, *dfree)
                else:
                    last = sc(lambda e, u=u, o=o: e.activation(o, u, ACT.Silu), m, *dfree)
                cvfree[ui] = last
            return last

        for c in range(6):
            if c == 3:
                wsm_ = small_split(32, ws_raw, ld["wsm"])
            xbc = conv_piece(2 * c, "ssd_conv_w_2", "ssd_conv_b_2", 12, XBCT, 2 * c, (4, 5, 6, 7), False)
        zm = []

        def silu_z(c):
            def evac(t, w, p):
                m = sc(lambda e: e.activation(ZZ[:, t, c * 512:(c + 1) * 512], bank[w][:, :], ACT.Silu), p)
                zm.append(m)
                return m
            return evac
        G = small(64).rearrange("p (t c) -> p t c", t=T)
        LE = small(64).rearrange("p (t c) -> p t c", t=T)
        gm = small_proj(32, ht, wsm_, lambda t, v, p: ve(
            lambda e: e.tensor_tensor(G[:, t, :], v, brow("ssd_dt_bias_2", 32), ALU.add), p))
        m = ve(lambda e: e.scalar_tensor_tensor(out=LE, in0=G, scalar=-1.0, in1=G, op0=ALU.mult, op1=ALU.max), gm)
        m = sc(lambda e: e.activation(LE, LE, ACT.Exp, scale=-1.0), m)
        m = sc(lambda e: e.activation(LE, LE, ACT.Ln, bias=1.0), m)
        DTv, LF = (small(n).rearrange("p (t c) -> p t c", t=T) for n in (32, 16))
        IG = G[:, :, 16:24]
        dtm = ve(lambda e: e.scalar_tensor_tensor(out=DTv, in0=G[:, :, 0:16], scalar=0.0, in1=LE[:, :, 0:16],
                                                  op0=ALU.max, op1=ALU.add), m)
        lfm = ve(lambda e: e.scalar_tensor_tensor(out=LF, in0=G[:, :, 24:32], scalar=0.0, in1=LE[:, :, 24:32],
                                                  op0=ALU.min, op1=ALU.subtract))
        AV, ADT = small(16), small(32).rearrange("p (t c) -> p t c", t=T)
        m = sc(lambda e: e.activation(AV, brow("ssd_a_log_2", 16), ACT.Exp))
        m = ve(lambda e: e.tensor_scalar(AV, AV, -1.0, None, ALU.mult), m)
        adm = ve(lambda e: e.tensor_tensor(ADT, DTv, bc(AV.unsqueeze(1), P, T, 16), ALU.mult), m, dtm)

        zjobs = [tok_job(HTH, HTL, ht, silu_z(c), (6, 7)) for c in range(2)]
        for step in zjobs[0]:
            step()
        CB = TMP[:, :, 0:384]
        cbm = None
        for g in range(2):
            w = work((4, 5))
            bt, ct = XBCT[:, 8 + g, :], XBCT[:, 10 + g, :]
            pe(lambda e, w=w, bt=bt, ct=ct: e.matmul(bank[w][:, 0:256], bt[:, 0:128], ct, start=True, stop=True),
               xbc, read[w], sig=False)
            p = pe(lambda e, w=w, bt=bt, ct=ct: e.matmul(bank[w][:, 256:384], bt[:, 128:256], ct[:, 128:256],
                                                         start=True, stop=True))
            cbm = read[w] = ve(lambda e, w=w, g=g: e.tensor_tensor(CB[:, g, :], bank[w][:, 0:384],
                                                                   const("ux", 384), ALU.mult), p, *tmpf)
        for t in range(T):
            for b in range(2):
                w = work((4, 5))
                for k in range(4):
                    p = pe(lambda e, w=w, k=k, b=b, t=t: e.transpose(
                        bank[w][:, k * 128:(k + 1) * 128], XBCT[:, 4 * b + k, t * 128:(t + 1) * 128], ident),
                        xbc, read[w], sig=(k == 3))
                xsm = read[w] = sc(lambda e, w=w, b=b, t=t: e.activation(XS[:, t, b * 512:(b + 1) * 512],
                                                                         bank[w][:, :], ACT.Copy), p)
        xbct_free = p
        XDT = H
        for t in range(T):
            xd = ve(lambda e, t=t: e.tensor_tensor(
                XDT[:, t, :].rearrange("p (h c) -> p h c", h=16), XS[:, t, :].rearrange("p (h c) -> p h c", h=16),
                bc(DTv[:, t, :].unsqueeze(2), P, 16, 64), ALU.mult), xsm, dtm, hold["H"])
        for step in zjobs[1]:
            step()

        slt, ux = const("slt", 128), const("ux", 384)
        LA = [big(9216 + 384 * i, 384) for i in range(2)]
        EE = [big(9216 + 768 + 384 * i, 384) for i in range(3)]
        la_free, ww_free = [gm] * 2, [ld["gb"]] * 3
        OG = XBCT[:, 0:8, :].rearrange("p (t a) b -> p t (a b)", t=T)
        vmm, ogm = [], []

        def og_copy(c):
            def evac(t, w, p):
                m = sc(lambda e: e.activation(OG[:, t, c * 512:(c + 1) * 512], bank[w][:, :], ACT.Copy), p,
                       xbct_free)
                ogm.append(m)
                return m
            return evac

        jobs = []
        for c in range(2):
            jobs += tok_job(HTH, HTL, ht, copy_to(lambda t, c=c: VV[:, t, c * 512:(c + 1) * 512], vmm), (6, 7))
        for c in range(2):
            jobs += tok_job(HTH, HTL, ht, og_copy(c), (6, 7))

        def ssd_seg(h):
            i, la = h % 2, LA[h % 2]
            for t in range(T):
                po(lambda e, t=t: e.tensor_scalar(la[:, t * 128:(t + 1) * 128], slt, ADT[:, t, h:h + 1], None,
                                                  ALU.mult), adm, la_free[i], *xm)
            lam_ = po(lambda e: e.tensor_scalar(la[:, 256:384], ux[:, 128:256], ADT[:, 1, h:h + 1], None, ALU.mult))
            w = work((4, 5))
            pe(lambda e: e.matmul(bank[w][:, 0:256], la[:, 0:128], ux[:, 0:256], start=True, stop=False), lam_,
               read[w], sig=False)
            pe(lambda e: e.matmul(bank[w][:, 128:256], la[:, 256:384], ux[:, 0:128], start=False, stop=True),
               sig=False)
            p = pe(lambda e: e.matmul(bank[w][:, 256:384], la[:, 128:256], ux[:, 0:128], start=True, stop=True))
            la_free[i] = p
            ee = EE[h % 3]
            m = read[w] = sc(lambda e: e.activation(ee, bank[w][:, 0:384], ACT.Exp), p, ww_free[h % 3])
            return ve(lambda e: e.tensor_tensor(ee, ee, CB[:, h // 8, :], ALU.mult), m, cbm)

        def ssd_y(h, wm_):
            hb, hc, ee = h // 8, (h % 8) * 64, EE[h % 3]
            xd0, xd1 = XDT[:, 0, h * 64:(h + 1) * 64], XDT[:, 1, h * 64:(h + 1) * 64]
            pe(lambda e: e.matmul(bank[hb][:, hc:hc + 64], ee[:, 0:128], xd0, start=True, stop=True), wm_, xd,
               *read[0:4], sig=False)
            pe(lambda e: e.matmul(bank[2 + hb][:, hc:hc + 64], ee[:, 128:256], xd0, start=True, stop=False),
               sig=False)
            ww_free[h % 3] = pe(lambda e: e.matmul(bank[2 + hb][:, hc:hc + 64], ee[:, 256:384], xd1, start=False,
                                                   stop=True))
            return ww_free[h % 3]

        gss, grs = small(4), small(4)
        gmk, sqm, gsm = [None] * 4, {}, {}
        sq_free = [hold["junk"], *cvfree]

        def gated(g):
            for t in range(T):
                b = 2 * t + g
                yv, zv = XS[:, t, g * 512:(g + 1) * 512], ZZ[:, t, g * 512:(g + 1) * 512]
                m = read[b] = ve(lambda e, b=b, yv=yv: e.tensor_tensor(yv, bank[b][:, :], yv, ALU.add), yp, xsd)
                m = ve(lambda e, yv=yv, zv=zv: e.tensor_tensor(yv, yv, zv, ALU.mult), m, zm[3])
                sqm[b] = sc(lambda e, yv=yv, b=b, t=t, g=g: e.activation(
                    cvf[:, t * 512:(t + 1) * 512], yv, ACT.Square, accum_out=gss[:, 2 * g + t:2 * g + t + 1]), m,
                    *sq_free, *sqm.values())

        def group_norm(g):
            m = rstd(grs[:, 2 * g:2 * g + 2], gss[:, 2 * g:2 * g + 2], 512, sqm[g], sqm[2 + g])
            for t in range(T):
                yv = XS[:, t, g * 512:(g + 1) * 512]
                gmk[2 * t + g] = ve(lambda e, yv=yv, t=t: e.tensor_scalar(
                    yv, yv, grs[:, 2 * g + t:2 * g + t + 1], None, ALU.mult), m)

        def ssd_columns(g):
            return to_columns(XS, [gmk[g], gmk[2 + g]], "ssd_norm_w_2", MXH, MXL, act_free[0], act_free[1],
                              banks=(4, 5), halves=(g,))

        wms = {}
        for h in range(17):
            if h < 16:
                wms[h] = ssd_seg(h)
            if h % 2 == 0 and jobs:
                jobs.pop(0)()
            if h:
                yp = ssd_y(h - 1, wms[h - 1])
            if h == 1:
                for t in range(T):
                    xsd = po(lambda e, t=t: e.tensor_tensor(
                        XS[:, t, :].rearrange("p (h c) -> p h c", h=16), XS[:, t, :].rearrange("p (h c) -> p h c", h=16),
                        bc(brow("ssd_d_2", 16).unsqueeze(2), P, 16, 64), ALU.mult), xd, xsm)
            if h == 9:
                gated(0)
            elif h == 11:
                group_norm(0)
            elif h == 13:
                hold["half"], tmpf[0] = True, wms[8]
                ssd_columns(0)
                hold["half"] = False
        for j in jobs:
            j()
        tmpf[1] = wms[15]
        gated(1)
        group_norm(1)
        hold["junk"] = sqm[3]
        cvfree = [hold["junk"]] * 4

        RR = [big(2048 + 2048 + 384 * i, 384) for i in range(2)]
        DD = [big(384 * i, 384) for i in range(2)]
        ST = [big(768 + 384 * i, 384) for i in range(2)]
        DG, dg = big(4864, 256), [xbct_free] * 2
        mmx, nmx, den = (small(16).rearrange("p (t h) -> p t h", t=T) for _ in range(3))
        rr_free, dd_free, st_free = [xbct_free] * 2, [gmk[3]] * 2, [gmk[3]] * 2
        KS = 0.25 * 128 ** -0.5

        rms_ = {}

        def ml_r(h):
            i, R = h % 2, RR[h % 2]
            for t in range(T):
                r, d = R[:, t * 128:(t + 1) * 128], DG[:, t * 128:(t + 1) * 128]
                m = po(lambda e, t=t, r=r: e.tensor_scalar(r, slt, LF[:, t, h:h + 1], None, ALU.mult), lfm, rr_free[i])
                m2 = po(lambda e, t=t, d=d: e.tensor_scalar(d, ident, IG[:, t, h:h + 1], None, ALU.mult), gm, dg[t])
                dg[t] = po(lambda e, r=r, d=d: e.tensor_tensor(r, r, d, ALU.add), m, m2)
            rms_[h] = po(lambda e: e.tensor_scalar(R[:, 256:384], ux[:, 128:256], LF[:, 1, h:h + 1], None, ALU.mult))

        def ml_d(h):
            i, R, DDi = h % 2, RR[h % 2], DD[h % 2]
            rm = rms_[h]
            w = work((4, 5))
            pe(lambda e: e.matmul(bank[w][:, 0:128], ux[:, 0:128], R[:, 0:128], start=True, stop=True), rm,
               read[w], sig=False)
            pe(lambda e: e.matmul(bank[w][:, 128:256], ux[:, 128:256], R[:, 0:128], start=True, stop=False),
               sig=False)
            pe(lambda e: e.matmul(bank[w][:, 128:256], ux[:, 0:128], R[:, 256:384], start=False, stop=True),
               sig=False)
            p = pe(lambda e: e.matmul(bank[w][:, 256:384], ux[:, 0:128], R[:, 128:256], start=True, stop=True))
            rr_free[i] = p
            if h + 2 < 8:
                ml_r(h + 2)
            m = read[w] = ve(lambda e: e.tensor_tensor(DDi, bank[w][:, 0:384], const("neg", 384), ALU.add), p,
                             dd_free[i])
            ve(lambda e: e.reduce_max(mmx[:, 0, h:h + 1], DDi[:, 0:128], AX), m)
            m = ve(lambda e: e.reduce_max(mmx[:, 1, h:h + 1], DDi[:, 128:384], AX))
            m = ve(lambda e: e.tensor_scalar(nmx[:, :, h:h + 1], mmx[:, :, h:h + 1], -1.0, None, ALU.mult), m)
            for t, (c0, c1) in enumerate(half_c):
                em_ = sc(lambda e, t=t, c0=c0, c1=c1: e.activation(
                    DDi[:, c0:c1], DDi[:, c0:c1], ACT.Exp, bias=nmx[:, t, h:h + 1]), m)
            return em_

        def qk_pieces(c):
            s = 4 * (c % 2)
            conv_piece(2 * c, "ml_conv_w_2", "ml_conv_b_2", 16, QKT, s, (6, 7), True, qk_free[c % 2])
            return conv_piece(8 + 2 * c, "ml_conv_w_2", "ml_conv_b_2", 16, QKT, s + 2, (6, 7), True, qk_free[c % 2])

        qk_free = [yp, yp]
        qkm = {0: qk_pieces(0)}
        ml_r(0)
        ml_r(1)
        emd = {0: ml_d(0)}
        mix0 = ssd_columns(1)
        xs_free = pe.mark()
        xh = [None, None]

        def x_add(c):
            def evac(t, w, p):
                xv = X[:, t, c * 512:(c + 1) * 512]
                xh[c] = ve(lambda e: e.tensor_tensor(xv, bank[w][:, :], xv, ALU.add), p)
                return xh[c]
            return evac

        def ml_s(h, em_, qk):
            i, DDi, STi = h % 2, DD[h % 2], ST[h % 2]
            s = 4 * ((h // 2) % 2) + h % 2
            w = work((4, 5))
            q, k = QKT[:, s, :], QKT[:, s + 2, :]
            pe(lambda e: e.matmul(bank[w][:, 0:128], q[:, 0:128], k[:, 0:128], start=True, stop=True), qk, read[w],
               sig=False)
            p = pe(lambda e: e.matmul(bank[w][:, 128:384], q[:, 128:256], k, start=True, stop=True))
            if h % 2:
                qk_free[(h // 2) % 2] = p
            for t, (c0, c1) in enumerate(half_c):
                m = ve(lambda e, t=t, c0=c0, c1=c1: e.tensor_tensor_reduce(
                    DDi[:, c0:c1], bank[w][:, c0:c1], DDi[:, c0:c1], KS, 0.0, ALU.mult, ALU.add,
                    den[:, t, h:h + 1]), p, em_)
            read[w] = m
            return m

        def ml_y(h, sm_):
            i, DDi, STi = h % 2, DD[h % 2], ST[h % 2]
            w = work((4, 5))
            for j in range(3):
                p = pe(lambda e, w=w, j=j: e.transpose(bank[w][:, j * 128:(j + 1) * 128],
                                                       DDi[:, j * 128:(j + 1) * 128], ident), sm_, read[w],
                       sig=(j == 2))
            dd_free[i] = p
            return read_set(w, sc(lambda e: e.activation(STi, bank[w][:, 0:384], ACT.Copy), p, st_free[i]))

        def read_set(w, m):
            read[w] = m
            return m

        def ml_v(h, am):
            STi = ST[h % 2]
            hb, hc = h // 4, (h % 4) * 128
            v0, v1 = VV[:, 0, h * 128:(h + 1) * 128], VV[:, 1, h * 128:(h + 1) * 128]
            pe(lambda e: e.matmul(bank[hb][:, hc:hc + 128], STi[:, 0:128], v0, start=True, stop=True), am, *vmm,
               *read[0:4], sig=False)
            pe(lambda e: e.matmul(bank[2 + hb][:, hc:hc + 128], STi[:, 128:256], v0, start=True, stop=False),
               sig=False)
            st_free[h % 2] = pe(lambda e: e.matmul(bank[2 + hb][:, hc:hc + 128], STi[:, 256:384], v1, start=False,
                                                   stop=True))
            return st_free[h % 2]

        wjobs = [tok_job(MXH, MXL, mix0, x_add(c), (6, 7)) for c in range(2)]
        mu, va = (small(16).rearrange("p (b h) -> p b h", b=4) for _ in range(2))
        YM = XS
        ymk, ym2, ym3 = [None] * 4, {}, {}

        def heads4(v, t, g):
            return v[:, t, g * 512:(g + 1) * 512].rearrange("p (h c) -> p h c", h=4)

        def divide(g, s_):
            d4, n4 = den[:, :, 4 * g:4 * g + 4], nmx[:, :, 4 * g:4 * g + 4]
            em_ = sc(lambda e: e.activation(n4, n4, ACT.Exp))
            m = ve(lambda e: e.scalar_tensor_tensor(out=d4, in0=d4, scalar=-1.0, in1=d4, op0=ALU.mult, op1=ALU.max),
                   s_)
            m = ve(lambda e: e.tensor_tensor(d4, d4, n4, ALU.max), m, em_)
            m = ve(lambda e: e.reciprocal(d4, d4), m)
            for t in range(T):
                b = 2 * t + g
                yv, bv = heads4(YM, t, g), bank[b][:, :].rearrange("p (h c) -> p h c", h=4)
                ym2[b] = read[b] = ve(lambda e, yv=yv, bv=bv, t=t: e.tensor_tensor(
                    yv, bv, bc(d4[:, t, :].unsqueeze(2), P, 4, 128), ALU.mult), m, yp, xs_free)
            for t in range(T):
                b = 2 * t + g
                yv = heads4(YM, t, g)
                ym3[b] = ve(lambda e, yv=yv, b=b: e.reduce_sum(mu[:, b, :], yv, AX), ym2[b])
            for t in range(T):
                b = 2 * t + g
                ym3[b] = ve(lambda e, b=b: e.tensor_scalar(mu[:, b, :], mu[:, b, :], 1.0 / 128, None, ALU.mult),
                            ym3[b])

        def centre(g):
            for t in range(T):
                b = 2 * t + g
                yv = heads4(YM, t, g)
                ym2[b] = ve(lambda e, yv=yv, b=b: e.tensor_tensor(
                    yv, yv, bc(mu[:, b, :].unsqueeze(2), P, 4, 128), ALU.subtract), ym3[b])
                jv = TMP[:, t, :].rearrange("p (h c) -> p h c", h=4)
                ym3[b] = sc(lambda e, yv=yv, jv=jv: e.activation(jv, yv, ACT.Square), ym2[b], tmpf[t])
            for t in range(T):
                b = 2 * t + g
                jv = TMP[:, t, :].rearrange("p (h c) -> p h c", h=4)
                tmpf[t] = m = ve(lambda e, b=b, jv=jv: e.reduce_sum(va[:, b, :], jv, AX), ym3[b])
                ym3[b] = rstd(va[:, b, :], va[:, b, :], 128, m)

        def gate_heads(g):
            for t in range(T):
                b = 2 * t + g
                yv, ov = heads4(YM, t, g), heads4(OG, t, g)
                ym2[b] = ve(lambda e, yv=yv, ov=ov: e.tensor_tensor(yv, yv, ov, ALU.mult), ym2[b], ogt, ym3[b])
            for t in range(T):
                b = 2 * t + g
                yv = heads4(YM, t, g)
                ymk[b] = ve(lambda e, yv=yv, b=b: e.scalar_tensor_tensor(
                    out=yv, in0=yv, scalar=0.5, in1=bc(va[:, b, :].unsqueeze(2), P, 4, 128), op0=ALU.mult,
                    op1=ALU.mult), ym3[b], ym2[b])

        def ml_columns(g):
            return to_columns(YM, [ymk[g], ymk[2 + g]], "ml_norm_w_2", HTH, HTL, ht_free, banks=(0, 2), halves=(g,))

        for h in range(8):
            c = h // 2
            if h + 1 < 8:
                emd[h + 1] = ml_d(h + 1)
            s_ = ml_s(h, emd[h], qkm[c])
            ymark = {}

            def mid(h=h, s_=s_):
                ymark["t"] = ml_y(h, s_)

            def after(h=h):
                ymark[h] = ml_v(h, ymark["t"])

            if h % 2 == 0 and c < 3:
                conv_piece(2 * c + 2, "ml_conv_w_2", "ml_conv_b_2", 16, QKT, 4 * ((c + 1) % 2), (6, 7), True,
                           qk_free[(c + 1) % 2], mid=mid, after=after)
            elif h % 2 == 1 and c < 3:
                qkm[c + 1] = conv_piece(10 + 2 * c, "ml_conv_w_2", "ml_conv_b_2", 16, QKT, 4 * ((c + 1) % 2) + 2,
                                        (6, 7), True, qk_free[(c + 1) % 2], mid=mid, after=after)
                ht_free = pe.mark()
            for at_h, job, step in FILL:
                if at_h == h:
                    wjobs[job][step]()
            if h >= 6:
                mid()
                after()
            yp = ymark[h]
            if h == 7:
                divide(1, s_)
                centre(1)
                gate_heads(1)
            if h == 3:
                sm_ = s_
                ogt = sc(lambda e: e.activation(OG, OG, ACT.Tanh, scale=0.5), *ogm)
                ogt = ve(lambda e: e.tensor_scalar(OG, OG, 1.0, None, ALU.add), ogt)
            elif h == 4:
                divide(0, sm_)
            elif h == 5:
                centre(0)
            elif h == 6:
                gate_heads(0)
                mixg = ml_columns(0)
        tok_half(HTH, HTL, mixg, (6, 7), 0)
        tok_half(HTH, HTL, mixg, (4, 5), 0)
        hold["junk"] = ymk[3]
        mix1 = ml_columns(1)
        mix_pe = pe.mark()
        ld_free = [yp, ymk[3], mix_pe]
        gbf = H[:, 0, :]
        iota = big(10240, NS)
        wr_raw = cvf[:, 0:288]
        load("iota", iota, a["iota"].partition_broadcast(P), *ld_free, eng=sy)
        xw = [None, None]
        for c in range(2):
            bs = (6 - 2 * c, 7 - 2 * c)
            ps = tok_half(HTH, HTL, mix1, bs, 1)
            for t in range(T):
                read[bs[t]] = xw[t] = x_add(c)(t, bs[t], ps[t])

        hold["H"] = yp
        mixw = pe.mark()
        ht = rmsnorm_T(xw, "norm2_w_2", mixw)
        warm(WARM["router"], 0)
        h2m, h_free = hold["hm"], hold["H"]
        load("wrt", wr_raw, a["wrt"], hold["junk"], eng=sy)
        RB = H[:, 1, :]
        rb_at = [0]

        def rb(*shape):
            n = int(np.prod(shape))
            v = RB[:, rb_at[0]:rb_at[0] + n]
            rb_at[0] += n
            assert rb_at[0] <= 1024
            return v.rearrange("p (a b) -> p a b", a=shape[0]) if len(shape) == 2 else v

        L = rb(T, 36)
        H2H, H2L = (v[:, :, :].rearrange("p (t a) b -> p t (a b)", t=T) for v in (MXH, MXL))

        def split_h2():
            m = sc(lambda e: e.activation(H2H, H[:, :, :], ACT.Copy), *h2m, mixw)
            hold["h2s"] = ve(lambda e: e.tensor_tensor(H2L, H[:, :, :], H2H.bitcast(F32), ALU.subtract), m, mixw)

        lmk = small_proj(36, ht, small_split(36, wr_raw, ld["wrt"]), lambda t, v, p: ve(
            lambda e: e.tensor_tensor(L[:, t, :], v, brow("router_g_b_2", 36), ALU.add), p,
            hold["h2s"], h_free), split_h2)
        h2s = hold["h2s"]
        load("gbf", gbf, a["norm_f_w_2"].partition_broadcast(P), h2s, h_free, eng=sy)

        def bt(v, n):
            return bc(v.unsqueeze(2), P, T, n)

        def top1(vals, n, iot, mval, onehot, *marks):
            eq, idx = rb(T, n), rb(T, 1)
            m = ve(lambda e: e.reduce_max(mval, vals, AX), *marks)
            m = ve(lambda e: e.tensor_tensor(eq, vals, bt(mval, n), ALU.is_ge), m)
            m = ve(lambda e: e.scalar_tensor_tensor(out=eq, in0=eq, scalar=-100.0,
                                                    in1=bc(iot.unsqueeze(1), P, T, n),
                                                    op0=ALU.mult, op1=ALU.add), m)
            m = ve(lambda e: e.tensor_reduce(idx[:, :, 0], eq, AX, ALU.min), m)
            rb_at[0] -= T * (n + 1)
            return ve(lambda e: e.tensor_tensor(onehot, eq, bt(idx[:, :, 0], n), ALU.is_equal), m)

        goh, ge2 = rb(T, 4), rb(T, 4)
        oh1, oh2, el = rb(T, 32), rb(T, 32), rb(T, 32)
        gmx, gsum, m1_, m2_, dm, g1, g2, pos = (rb(2) for _ in range(8))
        pos2 = rb(2)
        m = top1(L[:, :, 0:4], 4, const("iota", 4), gmx, goh, lmk)
        gm1 = ve(lambda e: e.tensor_tensor(ge2, L[:, :, 0:4], bt(gmx, 4), ALU.subtract), m)
        gm1 = sc(lambda e: e.activation(ge2, ge2, ACT.Exp), gm1)
        m = ve(lambda e: e.tensor_scalar(goh, goh, 1.0, 1e30, ALU.subtract, ALU.mult), m)
        for t in range(T):
            m = ve(lambda e, t=t: e.tensor_tensor(el[:, t, :].rearrange("p (g c) -> p g c", g=4),
                                                  L[:, t, 4:36].rearrange("p (g c) -> p g c", g=4),
                                                  bc(goh[:, t, :].unsqueeze(2), P, 4, 8), ALU.add), m)
        m = top1(el, 32, const("iota", 32, 4), m1_, oh1, m)
        m = ve(lambda e: e.scalar_tensor_tensor(out=el, in0=oh1, scalar=-2e30, in1=el, op0=ALU.mult,
                                                op1=ALU.add), m)
        m = top1(el, 32, const("iota", 32, 4), m2_, oh2, m)
        MM = el
        mmm = ve(lambda e: e.tensor_tensor(MM, oh1, oh2, ALU.add), m)
        w = work()
        tri, ones = ux[:, 0:128], ux[:, 128:256]
        bw = bank[w]
        pe(lambda e: e.matmul(bw[:, 0:32], ones, MM[:, 0, :], start=True, stop=False), mmm, read[w], sig=False)
        pe(lambda e: e.matmul(bw[:, 0:32], ones, MM[:, 1, :], start=False, stop=True), sig=False)
        pe(lambda e: e.matmul(bw[:, 32:64], tri, MM[:, 0, :], start=True, stop=True), sig=False)
        pe(lambda e: e.matmul(bw[:, 64:96], ones, MM[:, 0, :], start=True, stop=False), sig=False)
        p = pe(lambda e: e.matmul(bw[:, 64:96], tri, MM[:, 1, :], start=False, stop=True))
        CR = rb(3, 32)
        m = read[w] = ve(lambda e: e.tensor_copy(CR, bw[:, 0:96].rearrange("p (a b) -> p a b", a=3)), p)
        cnt, rank = CR[:, 0, :], CR[:, 1:3, :]
        OI = rb(2, 32)
        off, inc = OI[:, 0, :], OI[:, 1, :]
        m = ve(lambda e: e.tensor_tensor_scan(inc, ones[:, 0:32], cnt, 0.0, ALU.mult, ALU.add), m)
        m = ve(lambda e: e.tensor_tensor(off, inc, cnt, ALU.subtract), m)
        fits, t1, pad = rb(32), rb(32), rb(4)
        m = ve(lambda e: e.tensor_scalar(fits, cnt, 128.0, None, ALU.is_le), m)
        m = ve(lambda e: e.memset(pad, 0.0), m)
        for b in range(1, NT):
            edge = 128.0 * b
            m = ve(lambda e, edge=edge: e.scalar_tensor_tensor(out=t1, in0=off, scalar=edge, in1=fits, op0=ALU.is_lt,
                                                               op1=ALU.mult), m)
            m = ve(lambda e, edge=edge: e.scalar_tensor_tensor(out=t1, in0=inc, scalar=edge, in1=t1, op0=ALU.is_gt,
                                                               op1=ALU.mult), m)
            m = ve(lambda e, edge=edge: e.scalar_tensor_tensor(out=t1, in0=off, scalar=edge, in1=t1,
                                                               op0=ALU.subtract, op1=ALU.mult), m)
            m = ve(lambda e: e.reduce_sum(pad[:, 0:1], t1, AX), m)
            m = ve(lambda e: e.tensor_scalar(pad[:, 1:2], pad[:, 0:1], pad[:, 2:3], -128.0, ALU.add, ALU.is_ge), m)
            m = ve(lambda e: e.tensor_tensor(pad[:, 0:1], pad[:, 0:1], pad[:, 1:2], ALU.mult), m)
            m = ve(lambda e: e.tensor_tensor(pad[:, 2:3], pad[:, 2:3], pad[:, 0:1], ALU.add), m)
            m = ve(lambda e, edge=edge: e.tensor_scalar(t1, inc, edge, pad[:, 0:1], ALU.is_gt, ALU.mult), m)
            m = ve(lambda e: e.tensor_tensor(OI, OI, bc(t1.unsqueeze(1), P, 2, 32), ALU.subtract), m)
        offm = m
        FL, US, EQ = rb(32, NT), rb(32 * NT), rb(32 * NT)
        o4, i4, c4 = (bc(v.unsqueeze(2), P, 32, NT) for v in (off, inc, cnt))
        lo, hi = (bc(const(n, NT).unsqueeze(1), P, 32, NT) for n in ("lo", "hi"))
        FLf = FL.rearrange("p a b -> p (a b)")
        EQ4 = EQ.rearrange("p (a b) -> p a b", a=32)
        m = ve(lambda e: e.tensor_tensor(FL, o4, hi, ALU.is_lt), offm)
        m = ve(lambda e: e.tensor_tensor(EQ4, i4, lo, ALU.is_gt), m)
        m = ve(lambda e: e.tensor_tensor(FL, FL, EQ4, ALU.mult), m)
        m = ve(lambda e: e.tensor_scalar(EQ4, c4, 0.0, None, ALU.is_gt), m)
        m = ve(lambda e: e.tensor_tensor(FL, FL, EQ4, ALU.mult), m)
        m = ve(lambda e: e.tensor_tensor_scan(US, bc(ones[:, 0:1], P, 32 * NT), FLf, 0.0, ALU.mult, ALU.add), m)
        m = ve(lambda e: e.scalar_tensor_tensor(out=EQ, in0=US, scalar=const("up1", 1), in1=FLf,
                                                op0=ALU.is_equal, op1=ALU.mult), m)
        TB = rb(4)
        TBI = small(4).bitcast(I32)
        for i, code in enumerate(("ecode", "tcode")):
            m = ve(lambda e, code=code: e.tensor_tensor(FLf, EQ, const(code, 32 * NT), ALU.mult), m)
            m = ve(lambda e, i=i: e.reduce_sum(TB[:, i:i + 1], FLf, AX), m)
        m = ve(lambda e: e.scalar_tensor_tensor(out=TB[:, 2:3], in0=TB[:, 1:2], scalar=32.0, in1=TB[:, 0:1],
                                                op0=ALU.mult, op1=ALU.add), m)
        m = ve(lambda e: e.tensor_copy(TB[:, 3:4], US[:, 32 * NT - 1:32 * NT]), m)
        tbm = ve(lambda e: e.tensor_copy(TBI, TB), m)
        regs = {}
        stacks = {}

        def load_value(eng, name, u, col, top):
            eng.wait(tbm)
            eng.do(lambda e: regs.__setitem__((id(eng), name, u),
                                              e.value_load(TBI[u:u + 1, col:col + 1], min_val=0, max_val=top)))

        def val(eng, name, u):
            return regs[(id(eng), name, u)]

        engines = (sy, sc, ve, pe)
        for eng in engines:
            load_value(eng, "n", 0, 3, UNITS)

        def dyn(w, u, k0, nk, c0, n):
            return lambda: w[bass.ds(val(sy, "e", u), 1), k0 * 128:(k0 + nk) * 128, c0:c0 + n].rearrange(
                "a (k p) n -> p (a k) n", p=P)

        def begin_load(u):
            load_value(sy, "e", u, 0, NE - 1)
            load_value(sc, "t", u, 1, NT - 1)
            load_value(ve, "t", u, 1, NT - 1)
            load_value(ve, "te", u, 2, 32 * NT - 1)
            for w in (a["exp_w_gate_2"], a["exp_w_up_2"]):
                for kh in range(2):
                    add(dyn(w, u, 4 * kh, 4, 0, 512))
            if u:
                for kh in range(2):
                    add(dyn(a["exp_w_down_2"], u - 1, 2 * kh, 2, 0, D), kh == 1)
            pump()

        begin_load(0)
        m = ve(lambda e: e.tensor_tensor(rank, rank, bc(off.unsqueeze(1), P, T, 32), ALU.add), tbm)
        pt_ = MM
        for ohx, px in ((oh1, pos), (oh2, pos2)):
            m = ve(lambda e, ohx=ohx: e.tensor_tensor(pt_, ohx, rank, ALU.mult), m)
            m = ve(lambda e, px=px: e.reduce_sum(px, pt_, AX), m)
            posm = m = ve(lambda e, px=px: e.tensor_scalar(px, px, -1.0, None, ALU.add), m)
        SEL = HTH[:, 0:NT, :].rearrange("p a b -> p (a b)").rearrange("p (t s) -> p t s", t=T)
        SELT = HTL[:, 0:NT, :]
        for t in range(T):
            m = ve(lambda e, t=t: e.tensor_scalar(SEL[:, t, :], iota, pos[:, t:t + 1], None, ALU.is_equal), posm,
                   ld["iota"], lmk)
            selm = ve(lambda e, t=t: e.scalar_tensor_tensor(
                out=SEL[:, t, :], in0=iota, scalar=pos2[:, t:t + 1], in1=SEL[:, t, :].bitcast(F32),
                op0=ALU.is_equal, op1=ALU.add), m)
        m = ve(lambda e: e.tensor_tensor(dm, m2_, m1_, ALU.subtract), tbm)
        m = sc(lambda e: e.activation(dm, dm, ACT.Exp), m)
        mg = ve(lambda e: e.reduce_sum(gsum, ge2, AX), gm1)
        m = ve(lambda e: e.tensor_scalar(g1, dm, 1.0, None, ALU.add), m)
        m = ve(lambda e: e.tensor_tensor(g1, g1, gsum, ALU.mult), m, mg)
        m = ve(lambda e: e.reciprocal(g1, g1), m)
        m = ve(lambda e: e.tensor_tensor(g2, g1, dm, ALU.mult), m)
        ma = ve(lambda e: e.tensor_tensor(oh1, oh1, bt(g1, 32), ALU.mult), m)
        mb = ve(lambda e: e.tensor_tensor(oh2, oh2, bt(g2, 32), ALU.mult), m)
        gtm = ve(lambda e: e.tensor_tensor(oh1, oh1, oh2, ALU.add), ma, mb)
        split_to(st["cur"] + 1)
        XST = [big(4 * NS * i, 4, NS) for i in range(2)]
        YACC = [big(8 * NS + 512 * NT * i, NT, 512) for i in range(2)]
        for v in YACC:
            yz = po(lambda e, v=v: e.memset(v, 0.0), mix_pe, yp, ymk[3])
        xstm = []

        def rows_to_columns(out_, k, s0, s1, last):
            for t in range(T):
                for i, part in enumerate((H2H, H2L)):
                    p = pe(lambda e, t=t, part=part, i=i: e.matmul(
                        out_, part[:, t, k * 128:(k + 1) * 128], SEL[:, t, s0:s1],
                        start=(t == 0 and i == 0), stop=(t == 1 and i == 1)), selm, h2s, *last,
                        sig=(t == 1 and i == 1))
            return p

        hs_ = NS // 2
        for k in range(8):
            for half in range(2):
                w = work((4, 5, 6, 7, 0, 1, 2, 3))
                p = rows_to_columns(bank[w][:, 0:hs_], k, half * hs_, (half + 1) * hs_, [read[w]])
                dst = XST[k // 4][:, k % 4, half * hs_:(half + 1) * hs_]
                if half:
                    m = ve(lambda e, w=w, k=k, dst=dst: e.tensor_scalar(dst, bank[w][:, 0:hs_],
                                                                        ptcol("norm2_w_2", k), None, ALU.mult),
                           p, mix_pe, yp, ymk[3])
                else:
                    m = sc(lambda e, w=w, k=k, dst=dst: e.activation(dst, bank[w][:, 0:hs_], ACT.Copy,
                                                                     scale=ptcol("norm2_w_2", k)), p, mix_pe, yp,
                           ymk[3])
                read[w] = m
                xstm.append(m)
        x_free = pe.mark()
        for j in range(3):
            w = work()
            n = min(4, 2 * NT - 4 * j)
            for i in range(n):
                tau, t = 2 * j + i // 2, i % 2
                p = pe(lambda e, w=w, i=i, tau=tau, t=t: e.transpose(
                    bank[w][:, i * 128:(i + 1) * 128], SEL[:, t, tau * 128:(tau + 1) * 128].bitcast(F32), ident),
                    selm, read[w], sig=(i == n - 1))
            stm = read[w] = sc(lambda e, w=w, j=j, n=n: e.activation(
                SELT[:, 2 * j:2 * j + n // 2, :].rearrange("p a b -> p (a b)"), bank[w][:, 0:128 * n], ACT.Copy), p,
                ht, x_free)

        w = work()
        bg = bank[w][:, 0:32 * NT].rearrange("p (a b) -> p a b", a=NT)
        for j in range(NT):
            for t in range(T):
                p = pe(lambda e, j=j, t=t: e.matmul(bg[:, j, :], SEL[:, t, j * 128:(j + 1) * 128].bitcast(F32),
                                                    oh1[:, t, :], start=(t == 0), stop=(t == 1)), selm, gtm,
                       read[w], sig=(j == NT - 1 and t == 1))
        GM = US.rearrange("p (a b) -> p a b", a=NT)
        EQg = EQ.rearrange("p (a b) -> p a b", a=NT)
        og, ig = (bc(v.unsqueeze(1), P, NT, 32) for v in (off, inc))
        sl = bc(const("slot", NT).unsqueeze(2), P, NT, 32)
        m = ve(lambda e: e.tensor_tensor(EQg, og, sl, ALU.is_le), tbm)
        m = read[w] = ve(lambda e: e.tensor_tensor(GM, bg, EQg, ALU.mult), m, p)
        m = ve(lambda e: e.tensor_tensor(EQg, ig, sl, ALU.is_gt), m)
        gmm = ve(lambda e: e.tensor_tensor(GM, GM, EQg, ALU.mult), m)
        GMf = GM.rearrange("p a b -> p (a b)")
        XCH, XCL = ([v[:, 4 * i:4 * i + 4, :].rearrange("p a (b c) -> p (a b) c", c=128) for i in range(2)]
                    for v in (MXH, MXL))
        HIH, HIL = ([HTH[:, o + i:o + i + 1, :].rearrange("p a (b c) -> p (a b) c", c=128)
                     for i in range(2)] for o in (0, 2))
        tmp_free = list(tmpf)
        SG = [cvf[:, i * 512:(i + 1) * 512] for i in range(2)]
        gs = [small(1) for _ in range(2)]
        GU = [(0, 1), (2, 3)]
        TBK, YB = 4, (6, 7)
        u_ = {"gm": {}, "hid": {}, "hl": {}, "gu": {}, "d": {}, "y": {}, "xc": {}, "t": {}}

        def begin(u):
            if u > 1:
                begin_load(u)
            free = u_["gu"].get(u - 2)
            ms = []
            for i in range(2):
                xs4 = XST[i].rearrange("p k (t c) -> p k t c", t=NT)
                dh, dl = XCH[u % 2][:, 4 * i:4 * i + 4, :], XCL[u % 2][:, 4 * i:4 * i + 4, :]

                def src(eng, xs4=xs4):
                    return xs4[:, :, bass.ds(val(eng, "t", u), 1), :]
                m = sc(lambda e, dh=dh, src=src: e.activation(dh.unsqueeze(2), src(sc), ACT.Copy), *xstm, free,
                       x_free)
                ms.append((dh, dl, src, m))
            for dh, dl, src, m in ms:
                m = ve(lambda e, dh=dh, dl=dl, src=src: e.tensor_tensor(
                    dl.unsqueeze(2), src(ve), dh.bitcast(F32).unsqueeze(2), ALU.subtract), m, *xstm, free, x_free)
            u_["xc"][u] = m
            u_["gm"][u] = ve(lambda e: e.tensor_copy(gs[u % 2], GMf[:, bass.ds(val(ve, "te", u), 1)]), gmm,
                             u_["hid"].get(u - 2))
            split_to(st["cur"] + (1 if u else 2))

        def gate_up(u):
            G_, U_ = GU[u % 2]
            for b in (G_, U_):
                for kh in range(2):
                    i, wh, wl, wm = take()
                    wh, wl = (v[:, :].rearrange("p (k n) -> p k n", k=4) for v in (wh, wl))
                    for k in range(4):
                        kk_ = 4 * kh + k
                        p = three(bank[b][:, :], XCH[u % 2][:, kk_, :], XCL[u % 2][:, kk_, :], wh[:, k, :],
                                  wl[:, k, :], wm, u_["xc"][u], read[b] if kh == 0 else None,
                                  start=(kh == 0 and k == 0), stop=(kh == 1 and k == 3), sig=(k == 3))
                    done(i, p)
                if b == G_:
                    sg = read[b] = sc(lambda e: e.activation(SG[u % 2], bank[G_][:, :], ACT.Silu), p,
                                      u_["t"].get(u - 2), selm)
            u_["gu"][u] = p
            u_["hid"][u] = read[U_] = ve(lambda e: e.scalar_tensor_tensor(
                out=SG[u % 2], in0=bank[U_][:, :], scalar=gs[u % 2], in1=SG[u % 2], op0=ALU.mult, op1=ALU.mult),
                p, sg, u_["gm"][u])

        def turn_hidden(u):
            p = transpose4(TBK, SG[u % 2], u_["hid"][u])
            u_["t"][u] = p
            hv = bank[TBK][:, 0:256].rearrange("p (k c) -> p k c", k=2)
            m = sc(lambda e: e.activation(HIH[u % 2], hv, ACT.Copy), p, u_["d"].get(u - 2), stm, x_free)
            m = sc(lambda e: e.activation(TMP[:, u % 2, 0:256], bank[TBK][:, 256:512], ACT.Copy), *tmp_free)
            m = ve(lambda e: e.tensor_tensor(HIL[u % 2], hv, HIH[u % 2].bitcast(F32), ALU.subtract), m,
                   u_["d"].get(u - 2), stm)
            read[TBK] = u_["hl"][u] = m

        def down_u(u):
            i, wh, wl, wm = take()
            wh, wl = (v[:, :].rearrange("p (k n) -> p k n", k=2) for v in (wh, wl))
            for k in range(2):
                for hf in range(2):
                    hs = slice(hf * 512, (hf + 1) * 512)
                    p = three(bank[YB[hf]][:, :], HIH[u % 2][:, k, :], HIL[u % 2][:, k, :], wh[:, k, hs],
                              wl[:, k, hs], wm, u_["hl"][u], read[YB[hf]] if k == 0 else None, start=(k == 0),
                              stop=False, sig=(hf == 1 and k == 1))
            done(i, p)
            i, w, wm = take_whole()
            w = w[:, :].rearrange("p (k n) -> p k n", k=2)
            for k in range(2):
                for hf in range(2):
                    p = pe(lambda e, k=k, hf=hf: e.matmul(
                        bank[YB[hf]][:, :], TMP[:, u % 2, k * 128:(k + 1) * 128], w[:, k, hf * 512:(hf + 1) * 512],
                        start=False, stop=(k == 1)), wm, sig=(hf == 1 and k == 1))
            done(i, p)
            u_["d"][u] = p

        def gather_y(u):
            for hf in range(2):
                def yv(hf=hf):
                    return YACC[hf][:, bass.ds(val(ve, "t", u), 1), :]
                read[YB[hf]] = ve(lambda e, yv=yv, hf=hf: e.tensor_tensor(
                    yv(), bank[YB[hf]][:, :].unsqueeze(1), yv(), ALU.add), u_["d"][u], yz,
                    u_["y"].get(u - 1))
            u_["y"][u] = read[YB[1]]

        def unit(u):
            begin(u)
            if u == 0:
                begin_load(1)
            if u:
                turn_hidden(u - 1)
            if u > 1:
                gather_y(u - 2)
            gate_up(u)
            if u:
                down_u(u - 1)

        def last_unit(u):
            for kh in range(2):
                add(dyn(a["exp_w_down_2"], u, 2 * kh, 2, 0, D), kh == 1)
            split_to(st["cur"] + 1)
            turn_hidden(u)
            if u:
                gather_y(u - 1)
            down_u(u)
            gather_y(u)

        def keep():
            return ({k: (v.copy() if isinstance(v, (dict, list)) else v) for k, v in st.items()},
                    [(e.n, dict(e.seen)) for e in engines], list(read), [s[1] for s in rsem], list(turn),
                    {k: dict(v) for k, v in u_.items()})

        def back(k):
            st.update(k[0])
            for e, (n, seen) in zip(engines, k[1]):
                e.n, e.seen = n, dict(seen)
            read[:] = k[2]
            for s, v in zip(rsem, k[3]):
                s[1] = v
            turn[:] = k[4]
            u_.update(k[5])

        def enter(u):
            for eng in engines:
                def op(e, eng=eng):
                    g = e.If(val(eng, "n", 0) > u)
                    g.__enter__()
                    stacks.setdefault(id(eng), []).append(g)
                eng.do(op)

        def leave():
            for eng in engines:
                eng.do(lambda e, eng=eng: stacks[id(eng)].pop().__exit__(None, None, None))

        def enter_else():
            for eng in engines:
                def op(e, eng=eng):
                    g = e.Else()
                    g.__enter__()
                    stacks.setdefault(id(eng), []).append(g)
                eng.do(op)

        LEAST = 4
        for u in range(LEAST):
            unit(u)
        kept = []
        for u in range(LEAST, UNITS):
            kept.append(keep())
            enter(u)
            unit(u)
        last_unit(UNITS - 1)
        for u in range(UNITS - 2, LEAST - 2, -1):
            leave()
            back(kept[u + 1 - LEAST])
            enter_else()
            last_unit(u)
            leave()

        s_join = sem("s_join")
        for eng in (ve, sc, pe):
            eng.do(lambda e: e.drain().then_inc(s_join, 1))
        for eng, name in zip((pe, ve, sc), ("s_pe2", "s_ve2", "s_sc2")):
            eng.sem, eng.n = sem(name), 0
        for eng in (pe, ve, sc):
            eng.wait((s_join, 3))
        read[:] = [None] * 8
        hold["junk"] = hold["ss"] = None
        ym = {}
        for j in range(NT):
            for hf in range(2):
                i = 2 * j + hf
                h, l = (v[i // 4][:, (i % 4) * 512:(i % 4 + 1) * 512] for v in (WH, WL))
                src = YACC[hf][:, j, :]
                m = sc(lambda e, src=src, h=h: e.activation(h, src, ACT.Copy))
                m = ve(lambda e, src=src, h=h, l=l: e.tensor_tensor(l, src, h.bitcast(F32), ALU.subtract), m)
                ym[(j, hf)] = h, l, m
        for j in range(NT):
            for hf in range(2):
                h, l, m = ym[(j, hf)]
                for t in range(T):
                    b = 2 * t + hf
                    lhs = SELT[:, j, t * 128:(t + 1) * 128]
                    pe(lambda e, b=b, h=h, lhs=lhs, j=j: e.matmul(bank[b][:, :], lhs, h, start=(j == 0),
                                                                  stop=False), m, sig=False)
                    p = pe(lambda e, b=b, l=l, lhs=lhs, j=j: e.matmul(bank[b][:, :], lhs, l, start=False,
                                                                      stop=(j == NT - 1)))
        xm = add_to_x(p)
        m = final_norm(xm, gbf, ld["gbf"])
        osem = dsem("s_out")
        for t in range(T):
            om = sy.dma(osem, lambda e, t=t: e.dma_start(out[t * P:(t + 1) * P, :], X[:, t, :]), m[t])
        sy.wait(om)

        block = ctx.enter_context(nc.Block())

        @block.sync
        def _(e):
            sy.run(e)

        @block.scalar
        def _(e):
            sc.run(e)

        @block.vector
        def _(e):
            ve.run(e)

        @block.gpsimd
        def _(e):
            po.run(e)

        @block.tensor
        def _(e):
            pe.run(e)


def kernel(**inputs):
    from concourse import bacc
    from concourse.bass_utils import run_bass_kernel_spmd

    f = {n: np.asarray(v) for n, v in inputs.items()}
    cn, pool_a = constants()
    w2 = f["w_in_2"][0]

    def kcols(w):
        return np.ascontiguousarray(w.reshape(8, P, w.shape[1]).transpose(1, 0, 2)).reshape(P, -1)

    arrays = {
        "x": f["x"][0], "positions": np.ascontiguousarray(f["positions"][0].reshape(T, P).T), "cn": cn, "pool_a": pool_a,
        "pt": np.ascontiguousarray(np.concatenate([f[n].reshape(k, P) for n, k in PT_ROWS]).T),
        "br": np.concatenate([f[n].reshape(k) for n, k in BR_ROWS]),
        "wsm": kcols(np.concatenate([w2[:, 2560:2576], w2[:, 6672:6688]], 1)),
        "wrt": kcols(np.concatenate([f["router_g_w_2"][0], f["router_e_w_2"][0]], 1)),
        "iota": np.arange(NS, dtype=np.float32),
        "norm_final_g": f["norm_final_g"], "norm_f_w_2": f["norm_f_w_2"],
    }
    for n in ("w_in", "pool_w", "w_o", "w_up", "w_down", "w_in_2", "w_out_2", "exp_w_gate_2", "exp_w_up_2",
              "exp_w_down_2"):
        arrays[n] = f[n][0]
    nc = bacc.Bacc("TRN2", target_bir_lowering=False, num_devices=1)
    a, fed = {}, {}
    for n, v in arrays.items():
        fed[f"in_{n}"] = v
        a[n] = nc.dram_tensor(f"in_{n}", v.shape, mybir.dt.from_np(v.dtype), kind="ExternalInput").ap()
    out = nc.dram_tensor("out", (S, D), F32, kind="ExternalOutput").ap()
    build(nc, a, out)
    r = run_bass_kernel_spmd(nc, [fed], core_ids=[0])
    return np.asarray(r.results[0]["out"]).reshape(1, S, D)
```
